# Optimizing a Trainium2 kernel written in Bass

```python
import math
import jax, jax.numpy as jnp
from jax import lax
import numpy as np
import jax
import jax.numpy as jnp

D_MODEL = 1024
BATCH = 1
SEQ = 512
DEPTH = 1

ROPE_THETA = 500000.0
NORM_EPS = 1e-6
BLOCK_Q = 128
MLA_HEADS = 8
MLA_NOPE_DIM = 64
MLA_ROPE_DIM = 32
MLA_QK_DIM = MLA_NOPE_DIM + MLA_ROPE_DIM
MLA_V_DIM = 64
MLA_Q_RANK = 384
MLA_KV_RANK = 256
MLA_WIDTH = MLA_HEADS * MLA_V_DIM
DIFF_HEADS = 4
DIFF_HEAD_DIM = 64
DIFF_V_DIM = 2 * DIFF_HEAD_DIM
DIFF_ROT_DIM = DIFF_HEAD_DIM // 4
DIFF_QK_WIDTH = DIFF_HEADS * 2 * DIFF_HEAD_DIM
DIFF_WIDTH = DIFF_HEADS * DIFF_V_DIM
N_BRANCHES = 2
IN_SIZES = (MLA_Q_RANK, MLA_KV_RANK, MLA_ROPE_DIM, DIFF_QK_WIDTH, DIFF_QK_WIDTH, DIFF_WIDTH, N_BRANCHES * D_MODEL)
IN_WIDTH = MLA_Q_RANK + MLA_KV_RANK + MLA_ROPE_DIM + 2 * DIFF_QK_WIDTH + DIFF_WIDTH + N_BRANCHES * D_MODEL
FFN_HIDDEN = ((-(-8 * D_MODEL // 3) + 255) // 256) * 256


def rmsnorm(x, g):
    xf = x.astype(jnp.float32)
    y = xf * lax.rsqrt(jnp.mean(xf * xf, axis=-1, keepdims=True) + NORM_EPS)
    return (y * g.astype(jnp.float32)).astype(x.dtype)

def apply_rope(x, positions, rot_dim):
    half = rot_dim // 2
    inv_freq = jnp.exp(-math.log(ROPE_THETA) * jnp.arange(half, dtype=jnp.float32) * (2.0 / rot_dim))
    ang = positions.astype(jnp.float32)[..., None] * inv_freq
    ang = ang.reshape(ang.shape[:2] + (1,) * (x.ndim - 3) + (half,))
    cos, sin = jnp.cos(ang), jnp.sin(ang)
    xr = x[..., :rot_dim].astype(jnp.float32)
    x1, x2 = xr[..., :half], xr[..., half:]
    rot = jnp.concatenate([x1 * cos - x2 * sin, x2 * cos + x1 * sin], axis=-1).astype(x.dtype)
    return jnp.concatenate([rot, x[..., rot_dim:]], axis=-1)

def causal_attention(q, k, v):
    B, S, H, Dk = q.shape
    Dv = v.shape[-1]
    nb = S // BLOCK_Q
    scale = Dk ** -0.5
    qb = q.reshape(B, nb, BLOCK_Q, H, Dk).transpose(1, 0, 2, 3, 4)
    kpos = jnp.arange(S)

    def one_block(args):
        qi, i = args
        s = jnp.einsum('bqhd,bkhd->bhqk', qi, k).astype(jnp.float32) * scale
        qpos = i * BLOCK_Q + jnp.arange(BLOCK_Q)
        s = jnp.where(kpos[None, :] <= qpos[:, None], s, -jnp.inf)
        p = jax.nn.softmax(s, axis=-1).astype(v.dtype)
        return jnp.einsum('bhqk,bkhd->bqhd', p, v)

    out = lax.map(one_block, (qb, jnp.arange(nb)))
    return out.transpose(1, 0, 2, 3, 4).reshape(B, S, H, Dv)

def first_inputs(seed: int = 0) -> dict:
    key = jax.random.key(seed)
    ks = jax.random.split(key, 24)

    def dense(k, fan_in, fan_out):
        return jax.random.normal(k, (DEPTH, fan_in, fan_out), jnp.float32) * fan_in ** -0.5

    def gain(k, n):
        return 1.0 + 0.02 * jax.random.normal(k, (DEPTH, n), jnp.float32)

    def small(k, n, s):
        return s * jax.random.normal(k, (DEPTH, n), jnp.float32)

    x = jax.random.normal(ks[0], (BATCH, SEQ, D_MODEL), jnp.float32)
    positions = jnp.broadcast_to(jnp.arange(SEQ, dtype=jnp.int32)[None, :], (BATCH, SEQ))
    return {
        "x": x,
        "positions": positions,
        "norm_mix_g": gain(ks[1], D_MODEL),
        "w_in": dense(ks[2], D_MODEL, IN_WIDTH),
        "b_gate": small(ks[3], N_BRANCHES * D_MODEL, 0.1),
        "mla_q_norm_g": gain(ks[4], MLA_Q_RANK),
        "mla_w_uq": dense(ks[5], MLA_Q_RANK, MLA_HEADS * MLA_QK_DIM),
        "mla_kv_norm_g": gain(ks[6], MLA_KV_RANK),
        "mla_w_ukv": dense(ks[7], MLA_KV_RANK, MLA_HEADS * (MLA_NOPE_DIM + MLA_V_DIM)),
        "diff_lambda_q1": small(ks[8], DIFF_HEAD_DIM, 0.1),
        "diff_lambda_k1": small(ks[9], DIFF_HEAD_DIM, 0.1),
        "diff_lambda_q2": small(ks[10], DIFF_HEAD_DIM, 0.1),
        "diff_lambda_k2": small(ks[11], DIFF_HEAD_DIM, 0.1),
        "diff_subln_g": gain(ks[12], DIFF_V_DIM),
        "w_branch_mla": dense(ks[13], MLA_WIDTH, D_MODEL),
        "w_branch_diff": dense(ks[14], DIFF_WIDTH, D_MODEL),
        "w_out": dense(ks[15], D_MODEL, D_MODEL),
        "norm_ffn_g": gain(ks[16], D_MODEL),
        "w_ffn_gate": dense(ks[17], D_MODEL, FFN_HIDDEN),
        "w_ffn_up": dense(ks[18], D_MODEL, FFN_HIDDEN),
        "w_ffn_down": dense(ks[19], FFN_HIDDEN, D_MODEL),
        "norm_final_g": 1.0 + 0.02 * jax.random.normal(ks[20], (D_MODEL,), jnp.float32),
    }

def first_block(x, positions, norm_mix_g, w_in, b_gate, mla_q_norm_g, mla_w_uq, mla_kv_norm_g, mla_w_ukv,
              diff_lambda_q1, diff_lambda_k1, diff_lambda_q2, diff_lambda_k2, diff_subln_g,
              w_branch_mla, w_branch_diff, w_out, norm_ffn_g, w_ffn_gate, w_ffn_up, w_ffn_down, norm_final_g):
    B, S, _ = x.shape
    split_idx = [int(v) for v in np.cumsum(IN_SIZES)[:-1]]
    for l in range(DEPTH):
        xn = rmsnorm(x, norm_mix_g[l])
        proj = jnp.einsum('bsd,de->bse', xn, w_in[l])
        q_lat, kv_lat, k_rope, dq, dk, dv, gate_pre = jnp.split(proj, split_idx, axis=-1)

        q = jnp.einsum('bsr,re->bse', rmsnorm(q_lat, mla_q_norm_g[l]), mla_w_uq[l])
        q = q.reshape(B, S, MLA_HEADS, MLA_QK_DIM)
        q_nope, q_pe = q[..., :MLA_NOPE_DIM], apply_rope(q[..., MLA_NOPE_DIM:], positions, MLA_ROPE_DIM)
        kv = jnp.einsum('bsr,re->bse', rmsnorm(kv_lat, mla_kv_norm_g[l]), mla_w_ukv[l])
        kv = kv.reshape(B, S, MLA_HEADS, MLA_NOPE_DIM + MLA_V_DIM)
        k_nope, v_mla = kv[..., :MLA_NOPE_DIM], kv[..., MLA_NOPE_DIM:]
        k_pe = apply_rope(k_rope[:, :, None, :], positions, MLA_ROPE_DIM)
        q_mla = jnp.concatenate([q_nope, q_pe], axis=-1)
        k_mla = jnp.concatenate([k_nope, jnp.broadcast_to(k_pe, (B, S, MLA_HEADS, MLA_ROPE_DIM))], axis=-1)
        o_mla = causal_attention(q_mla, k_mla, v_mla).reshape(B, S, MLA_WIDTH)

        dq = apply_rope(dq.reshape(B, S, DIFF_HEADS, 2, DIFF_HEAD_DIM), positions, DIFF_ROT_DIM)
        dk = apply_rope(dk.reshape(B, S, DIFF_HEADS, 2, DIFF_HEAD_DIM), positions, DIFF_ROT_DIM)
        dv = dv.reshape(B, S, DIFF_HEADS, DIFF_V_DIM)
        o1 = causal_attention(dq[..., 0, :], dk[..., 0, :], dv)
        o2 = causal_attention(dq[..., 1, :], dk[..., 1, :], dv)
        lambda_init = 0.8 - 0.6 * math.exp(-0.3 * l)
        lam = (jnp.exp(jnp.sum(diff_lambda_q1[l].astype(jnp.float32) * diff_lambda_k1[l].astype(jnp.float32)))
               - jnp.exp(jnp.sum(diff_lambda_q2[l].astype(jnp.float32) * diff_lambda_k2[l].astype(jnp.float32)))
               + lambda_init).astype(o1.dtype)
        o_diff = rmsnorm(o1 - lam * o2, diff_subln_g[l]) * (1.0 - lambda_init)
        o_diff = o_diff.reshape(B, S, DIFF_WIDTH)

        gates = jax.nn.sigmoid(gate_pre + b_gate[l])
        g_mla, g_diff = gates[..., :D_MODEL], gates[..., D_MODEL:]
        merged = (g_mla * jnp.einsum('bse,ed->bsd', o_mla, w_branch_mla[l])
                  + g_diff * jnp.einsum('bse,ed->bsd', o_diff, w_branch_diff[l]))
        x = x + jnp.einsum('bsd,de->bse', merged, w_out[l])

        hn = rmsnorm(x, norm_ffn_g[l])
        hid = jax.nn.silu(jnp.einsum('bsd,df->bsf', hn, w_ffn_gate[l])) * jnp.einsum('bsd,df->bsf', hn, w_ffn_up[l])
        x = x + jnp.einsum('bsf,fd->bsd', hid, w_ffn_down[l])
    return rmsnorm(x, norm_final_g)


CHUNK = 64
Q_BLOCK = 128
HEAD_DIM = 64
FOX_HEADS = 8
DSA_HEADS = 8
IDX_HEADS = 8
IDX_DIM = 32
TOPK_MAX = 256
ROPE_FRACTION = 4
D_FF = 2816
N_SUBLAYERS = 3
FOX_WIDTH = FOX_HEADS * HEAD_DIM
DSA_WIDTH = DSA_HEADS * HEAD_DIM
IN_SIZES_2 = (FOX_WIDTH, FOX_WIDTH, FOX_WIDTH, FOX_HEADS, DSA_WIDTH, HEAD_DIM, HEAD_DIM, IDX_HEADS * IDX_DIM, IDX_DIM, IDX_HEADS, D_MODEL, D_MODEL)
D_IN = sum(IN_SIZES_2)


def rms_norm(x, g):
    xf = x.astype(jnp.float32)
    y = xf * lax.rsqrt(jnp.mean(xf * xf, axis=-1, keepdims=True) + NORM_EPS)
    return (y * g.astype(jnp.float32)).astype(x.dtype)

def modulate(x, g, shift, scale):
    return rms_norm(x, g) * (1 + scale[:, None, :]) + shift[:, None, :]

def swiglu(h, w1, w3, w2):
    return (jax.nn.silu(h @ w1) * (h @ w3)) @ w2

def rope_tables(positions, rot_dim):
    inv_freq = ROPE_THETA ** (-jnp.arange(0, rot_dim, 2, dtype=jnp.float32) / rot_dim)
    ang = positions.astype(jnp.float32)[..., None] * inv_freq
    return jnp.cos(ang), jnp.sin(ang)

def partial_rope(x, cos, sin):
    half = cos.shape[-1]
    x1 = x[..., :half].astype(jnp.float32)
    x2 = x[..., half:2 * half].astype(jnp.float32)
    r1 = (x1 * cos - x2 * sin).astype(x.dtype)
    r2 = (x2 * cos + x1 * sin).astype(x.dtype)
    return jnp.concatenate([r1, r2, x[..., 2 * half:]], axis=-1)

def fox_attention(q, k, v, log_f):
    B, S, H, dh = q.shape
    F = jnp.cumsum(log_f.astype(jnp.float32), axis=1).transpose(0, 2, 1)
    kpos = jnp.arange(S)
    scale = dh ** -0.5

    def block(i):
        qs = i * Q_BLOCK
        qb = lax.dynamic_slice_in_dim(q, qs, Q_BLOCK, axis=1)
        Fq = lax.dynamic_slice_in_dim(F, qs, Q_BLOCK, axis=2)
        s = jnp.einsum('bqhd,bkhd->bhqk', qb, k, preferred_element_type=jnp.float32) * scale
        s = s + Fq[..., None] - F[:, :, None, :]
        qpos = qs + jnp.arange(Q_BLOCK)
        mask = kpos[None, :] <= qpos[:, None]
        s = jnp.where(mask[None, None], s, -jnp.inf)
        p = jax.nn.softmax(s, axis=-1)
        return jnp.einsum('bhqk,bkhd->bqhd', p.astype(v.dtype), v)

    out = lax.map(block, jnp.arange(S // Q_BLOCK))
    return out.transpose(1, 0, 2, 3, 4).reshape(B, S, H, dh)

def dsa_attention(q, k, v, iq, ik, iw, top_k):
    B, S, H, dh = q.shape
    kchunk = jnp.arange(S) // CHUNK
    scale = dh ** -0.5
    idx_scale = IDX_DIM ** -0.5

    def block(i):
        qs = i * Q_BLOCK
        qb = lax.dynamic_slice_in_dim(q, qs, Q_BLOCK, axis=1)
        iqb = lax.dynamic_slice_in_dim(iq, qs, Q_BLOCK, axis=1)
        iwb = lax.dynamic_slice_in_dim(iw, qs, Q_BLOCK, axis=1)
        qchunk = (qs + jnp.arange(Q_BLOCK)) // CHUNK
        admissible = kchunk[None, :] <= qchunk[:, None]
        dots = jnp.einsum('bqhd,bkd->bqhk', iqb, ik, preferred_element_type=jnp.float32) * idx_scale
        score = jnp.einsum('bqh,bqhk->bqk', iwb.astype(jnp.float32), jax.nn.relu(dots))
        score = jnp.where(admissible[None], score, -jnp.inf)
        _, sel = lax.top_k(score, top_k)
        kg = jax.vmap(lambda kb, ib: kb[ib])(k, sel)
        vg = jax.vmap(lambda vb, ib: vb[ib])(v, sel)
        valid = (sel // CHUNK) <= qchunk[None, :, None]
        s = jnp.einsum('bqhd,bqkd->bhqk', qb, kg, preferred_element_type=jnp.float32) * scale
        s = jnp.where(valid[:, None], s, -jnp.inf)
        p = jax.nn.softmax(s, axis=-1)
        return jnp.einsum('bhqk,bqkd->bqhd', p.astype(vg.dtype), vg)

    out = lax.map(block, jnp.arange(S // Q_BLOCK))
    return out.transpose(1, 0, 2, 3, 4).reshape(B, S, H, dh)

def hybrid_mixer(h, w_in, fox_f_bias, fox_qk_g, dsa_qk_g, w_br_fox, w_br_dsa, w_out, rope_a, rope_i, top_k):
    B, S, _ = h.shape
    cos_a, sin_a = rope_a
    cos_i, sin_i = rope_i
    z = h @ w_in
    split_points = [int(p) for p in np.cumsum(IN_SIZES_2)[:-1]]
    (fq, fk, fv, ff, dq, dk, dv, iq, ik, iw, ga, gb) = jnp.split(z, split_points, axis=-1)
    fq = rms_norm(fq.reshape(B, S, FOX_HEADS, HEAD_DIM), fox_qk_g[0])
    fk = rms_norm(fk.reshape(B, S, FOX_HEADS, HEAD_DIM), fox_qk_g[1])
    fv = fv.reshape(B, S, FOX_HEADS, HEAD_DIM)
    log_f = jax.nn.log_sigmoid(ff.astype(jnp.float32) + fox_f_bias.astype(jnp.float32))
    ya = fox_attention(fq, fk, fv, log_f).reshape(B, S, FOX_WIDTH)
    dq = partial_rope(rms_norm(dq.reshape(B, S, DSA_HEADS, HEAD_DIM), dsa_qk_g[0]), cos_a[:, :, None, :], sin_a[:, :, None, :])
    dk = partial_rope(rms_norm(dk, dsa_qk_g[1]), cos_a, sin_a)
    iq = partial_rope(iq.reshape(B, S, IDX_HEADS, IDX_DIM), cos_i[:, :, None, :], sin_i[:, :, None, :])
    ik = partial_rope(ik, cos_i, sin_i)
    iw = iw * (IDX_HEADS ** -0.5)
    yb = dsa_attention(dq, dk, dv, iq, ik, iw, top_k).reshape(B, S, DSA_WIDTH)
    merged = jax.nn.sigmoid(ga) * (ya @ w_br_fox) + jax.nn.sigmoid(gb) * (yb @ w_br_dsa)
    return merged @ w_out

def second_inputs(seed: int = 0) -> dict:
    key = jax.random.key(seed)
    ks = jax.random.split(key, 24)
    L = DEPTH

    def nrm(k, shape, fan_in, gain=1.0):
        return jax.random.normal(k, shape, jnp.float32) * (gain * fan_in ** -0.5)

    x = jax.random.normal(ks[0], (BATCH, SEQ, D_MODEL), jnp.float32)
    c = jax.random.normal(ks[1], (BATCH, D_MODEL), jnp.float32)
    offsets = jax.random.randint(ks[2], (BATCH, 1), 0, 1024) * CHUNK
    positions = (offsets + jnp.arange(SEQ, dtype=jnp.int32)[None, :]).astype(jnp.int32)
    ada_w = nrm(ks[3], (L, D_MODEL, 3 * N_SUBLAYERS * D_MODEL), D_MODEL, 0.5)
    ada_b = 0.02 * jax.random.normal(ks[4], (L, 3 * N_SUBLAYERS * D_MODEL), jnp.float32)
    norm_g = 1.0 + 0.05 * jax.random.normal(ks[5], (L, N_SUBLAYERS, D_MODEL), jnp.float32)
    ffn1_w1 = nrm(ks[6], (L, D_MODEL, D_FF), D_MODEL)
    ffn1_w3 = nrm(ks[7], (L, D_MODEL, D_FF), D_MODEL)
    ffn1_w2 = nrm(ks[8], (L, D_FF, D_MODEL), D_FF)
    w_in = nrm(ks[9], (L, D_MODEL, D_IN), D_MODEL)
    fox_f_bias = 2.0 + 0.1 * jax.random.normal(ks[10], (L, FOX_HEADS), jnp.float32)
    fox_qk_g = 1.0 + 0.05 * jax.random.normal(ks[11], (L, 2, HEAD_DIM), jnp.float32)
    dsa_qk_g = 1.0 + 0.05 * jax.random.normal(ks[12], (L, 2, HEAD_DIM), jnp.float32)
    w_br_fox = nrm(ks[13], (L, FOX_WIDTH, D_MODEL), FOX_WIDTH)
    w_br_dsa = nrm(ks[14], (L, DSA_WIDTH, D_MODEL), DSA_WIDTH)
    w_out = nrm(ks[15], (L, D_MODEL, D_MODEL), D_MODEL)
    ffn2_w1 = nrm(ks[16], (L, D_MODEL, D_FF), D_MODEL)
    ffn2_w3 = nrm(ks[17], (L, D_MODEL, D_FF), D_MODEL)
    ffn2_w2 = nrm(ks[18], (L, D_FF, D_MODEL), D_FF)
    return {'x': x, 'c': c, 'positions': positions, 'ada_w': ada_w, 'ada_b': ada_b,
            'norm_g': norm_g, 'ffn1_w1': ffn1_w1, 'ffn1_w3': ffn1_w3, 'ffn1_w2': ffn1_w2,
            'w_in': w_in, 'fox_f_bias': fox_f_bias, 'fox_qk_g': fox_qk_g, 'dsa_qk_g': dsa_qk_g,
            'w_br_fox': w_br_fox, 'w_br_dsa': w_br_dsa, 'w_out': w_out,
            'ffn2_w1': ffn2_w1, 'ffn2_w3': ffn2_w3, 'ffn2_w2': ffn2_w2}

def second_block(x, c, positions, ada_w, ada_b, norm_g, ffn1_w1, ffn1_w3, ffn1_w2, w_in, fox_f_bias, fox_qk_g, dsa_qk_g, w_br_fox, w_br_dsa, w_out, ffn2_w1, ffn2_w3, ffn2_w2):
    B, S, _ = x.shape
    top_k = min(TOPK_MAX, S // 4)
    rope_a = rope_tables(positions, HEAD_DIM // ROPE_FRACTION)
    rope_i = rope_tables(positions, IDX_DIM // ROPE_FRACTION)
    cond = jax.nn.silu(c)
    for l in range(DEPTH):
        mod = (cond @ ada_w[l] + ada_b[l]).reshape(B, N_SUBLAYERS, 3, D_MODEL)
        h = modulate(x, norm_g[l, 0], mod[:, 0, 0], mod[:, 0, 1])
        x = x + 0.5 * mod[:, 0, 2][:, None, :] * swiglu(h, ffn1_w1[l], ffn1_w3[l], ffn1_w2[l])
        h = modulate(x, norm_g[l, 1], mod[:, 1, 0], mod[:, 1, 1])
        y = hybrid_mixer(h, w_in[l], fox_f_bias[l], fox_qk_g[l], dsa_qk_g[l], w_br_fox[l], w_br_dsa[l], w_out[l], rope_a, rope_i, top_k)
        x = x + mod[:, 1, 2][:, None, :] * y
        h = modulate(x, norm_g[l, 2], mod[:, 2, 0], mod[:, 2, 1])
        x = x + 0.5 * mod[:, 2, 2][:, None, :] * swiglu(h, ffn2_w1[l], ffn2_w3[l], ffn2_w2[l])
    return x


def setup_inputs(seed=0):
    out = dict(first_inputs(seed))
    for name, value in second_inputs(seed + 1).items():
        if name != "x":
            out[name + "_2"] = value
    return out


def reference(
    x, positions, norm_mix_g, w_in, b_gate, mla_q_norm_g, mla_w_uq, mla_kv_norm_g, mla_w_ukv,
    diff_lambda_q1, diff_lambda_k1, diff_lambda_q2, diff_lambda_k2, diff_subln_g, w_branch_mla,
    w_branch_diff, w_out, norm_ffn_g, w_ffn_gate, w_ffn_up, w_ffn_down, norm_final_g, c_2,
    positions_2, ada_w_2, ada_b_2, norm_g_2, ffn1_w1_2, ffn1_w3_2, ffn1_w2_2, w_in_2,
    fox_f_bias_2, fox_qk_g_2, dsa_qk_g_2, w_br_fox_2, w_br_dsa_2, w_out_2, ffn2_w1_2, ffn2_w3_2,
    ffn2_w2_2,
):
    x = first_block(
        x, positions, norm_mix_g, w_in, b_gate, mla_q_norm_g, mla_w_uq, mla_kv_norm_g,
        mla_w_ukv, diff_lambda_q1, diff_lambda_k1, diff_lambda_q2, diff_lambda_k2, diff_subln_g,
        w_branch_mla, w_branch_diff, w_out, norm_ffn_g, w_ffn_gate, w_ffn_up, w_ffn_down,
        norm_final_g,
    )
    return second_block(
        x, c_2, positions_2, ada_w_2, ada_b_2, norm_g_2, ffn1_w1_2, ffn1_w3_2, ffn1_w2_2,
        w_in_2, fox_f_bias_2, fox_qk_g_2, dsa_qk_g_2, w_br_fox_2, w_br_dsa_2, w_out_2,
        ffn2_w1_2, ffn2_w3_2, ffn2_w2_2,
    )


_drawn_inputs = setup_inputs


def setup_inputs(seed=0):
    import zlib

    import numpy as np

    out = dict(_drawn_inputs(seed))
    spreads = {}
    factors = {'norm_mix_g': 3.104,
     'b_gate': 3.25,
     'mla_q_norm_g': 8.0,
     'mla_kv_norm_g': 8.0,
     'diff_lambda_k1': 8.0,
     'diff_lambda_q2': 8.0,
     'diff_subln_g': 6.659,
     'norm_ffn_g': 4.01,
     'norm_final_g': 2.887,
     'ada_b_2': 3.695,
     'norm_g_2': 4.34,
     'fox_f_bias_2': 64.0,
     'fox_qk_g_2': 8.0,
     'dsa_qk_g_2': 8.0}
    for name, (base, spread) in spreads.items():
        noise = np.random.default_rng([zlib.crc32(name.encode()), seed]).standard_normal(out[name].shape)
        drawn = base * np.exp(spread * noise) if base else spread * noise
        out[name] = jnp.asarray(drawn.astype(out[name].dtype))
    for name, factor in factors.items():
        out[name] = (out[name] * factor).astype(out[name].dtype)
    return out
```

```python
from contextlib import ExitStack

import numpy as np

import concourse.bass as bass
from concourse import mybir

F32 = mybir.dt.float32
F32R = mybir.dt.float32r
I32 = mybir.dt.int32
ALU = mybir.AluOpType
ACT = mybir.ActivationFunctionType
AX = mybir.AxisListType.X

P = 128
S = 512
D = 1024
DT = D // P
FF = 2816
FT = FF // P
NB = S // P
EPS = 1e-6
NEG = -1.0e30
TAKEN = -3.0e38
THETA = 500000.0
H1, NOPE, ROPE, VDIM = 8, 64, 32, 64
QR, KVR = 384, 256
DH, DHD = 4, 64
TOPK = 128
CHUNK = 64

COLS = {}
_at = 0
for _name, _n in (("g_mix", DT), ("g_q", QR // P), ("g_kv", KVR // P), ("g_sub", 1), ("g_ffn", DT),
                  ("g_final", DT), ("b_gate", 2 * DT), ("g2", 3 * DT), ("ada_b", 9 * DT), ("cond", DT),
                  ("fox_g", 2), ("dsa_g", 2), ("f_bias", 1), ("freq_a", 1), ("freq_p", 1),
                  ("freq_i", 1)):
    COLS[_name] = (_at, _n)
    _at += _n
NCOLS = _at
SQUARES = ("ident", "ones", "halves", "rot_a", "rot_p", "rot_i", "rot_m", "causal", "chunked")
NSQ = len(SQUARES)

STREAM = (("in1", 14), ("dv1", 4), ("uq", 3), ("uk", 1), ("uv", 1), ("merge1", 24), ("out1", 8),
          ("up1", 2 * FT), ("down1", 3 * DT),
          ("up2", 2 * FT), ("down2", 3 * DT), ("in2", 15), ("fv2", 4), ("dvw2", 1), ("merge2", 24),
          ("out2", 8), ("up3", 2 * FT), ("down3", 3 * DT))
FIRST = {}
_at = 0
for _name, _n in STREAM:
    FIRST[_name] = _at
    _at += _n
NCH = _at
LAST_DOWN = [8, 8, 6]

KB = 1024


def build(nc, wst, ada, xT, cols_d, squares_d, pos1_d, pos2_d, lams_d, out):
    ctx = ExitStack()
    with ctx:
        used_sems = {}

        def sem(name):
            if name not in used_sems:
                used_sems[name] = ctx.enter_context(nc.semaphore(name))
            return used_sems[name]

        region = ctx.enter_context(nc.sbuf_tensor("region", [P, 207 * KB // 4], F32))
        base = 0
        if nc.sbuf_base - 207 * KB > 0:
            base = nc.sbuf_base - 207 * KB

        def at(name, kb, shape, dt=F32):
            return nc.alloc_sbuf_tensor_at(name, shape, dt, offset=base + int(kb * KB))

        PS = ctx.enter_context(nc.psum_tensor("PS", [P, 8, S], F32))

        X = at("X", 0, [P, DT, S])
        XH, XL = at("XH", 16, [P, DT, S], F32R), at("XL", 32, [P, DT, S], F32R)
        RAW = [at(f"RAW{j}", 48 + 4 * j, [P, 1024]) for j in range(3)]
        HI = [at(f"HI{j}", 60 + 4 * j, [P, 1024], F32R) for j in range(3)]
        LO = [at(f"LO{j}", 72 + 4 * j, [P, 1024], F32R) for j in range(3)]
        ADA = [at(f"ADA{j}", 84 + 4 * j, [P, 1024]) for j in range(2)]
        ACC = at("ACC", 92, [P, 1024])
        RB = at("RB", 96, [P, 2, S])
        SQ = at("SQ", 100, [P, 2, S])
        Y = at("Y", 104, [P, 2, S])
        T = at("T", 108, [P, 2, S])
        SQC = at("SQC", 112, [P, NSQ, P])
        CO = at("CO", 116.5, [P, NCOLS])
        MOD = at("MOD", 117.25, [P, 9 * DT])
        SM = at("SM", 117.625, [P, 96])
        A0 = 118
        HIDH = at("HIDH", A0, [P, FT, S], F32R)
        HIDL = at("HIDL", A0 + 44, [P, FT, S], F32R)
        LATQ = at("LATQ", A0, [P, 3, S])
        LATK = at("LATK", A0 + 6, [P, 2, S])
        KR = at("KR", A0 + 10, [P, S])
        DQ, DK = at("DQ", A0 + 12, [P, 4, S]), at("DK", A0 + 20, [P, 4, S])
        DV = at("DV", A0 + 28, [P, NB, S])
        TAB_A1 = at("TAB_A1", A0 + 36, [P, 2, S])
        TAB_P1 = at("TAB_P1", A0 + 40, [P, 2, S])
        P1, PT1 = at("P1", A0 + 44, [P, 2, S]), at("PT1", A0 + 48, [P, 2, S])
        OD = at("OD", A0 + 52, [P, NB, S])
        LQH, LQL = at("LQH", A0 + 60, [P, 3, S], F32R), at("LQL", A0 + 66, [P, 3, S], F32R)
        LKH, LKL = at("LKH", A0 + 72, [P, 2, S], F32R), at("LKL", A0 + 76, [P, 2, S], F32R)
        QM = at("QM", A0 + 12, [P, 8, S])
        VM = at("VM", A0 + 28, [P, NB, S])
        KM = [at("KM0", A0 + 80, [P, 4, S]), at("KM1", A0, [P, 4, S])]
        OM = at("OM", A0 + 36, [P, NB, S])
        OTH1, OTL1 = at("OTH1", A0 + 60, [P, 8, S], F32R), at("OTL1", A0 + 12, [P, 8, S], F32R)
        MH1, ML1 = at("MH1", A0 + 28, [P, 8, S], F32R), at("ML1", A0 + 44, [P, 8, S], F32R)
        QF, KF = at("QF", A0, [P, 8, S]), at("KF", A0 + 16, [P, 8, S])
        VF = at("VF", A0 + 32, [P, NB, S])
        DQ2 = at("DQ2", A0 + 40, [P, 4, S])
        IQ, IK, DK2 = at("IQ", A0 + 48, [P, 2, S]), at("IK", A0 + 52, [P, S]), at("DK2", A0 + 54, [P, S])
        DVW = at("DVW", A0 + 56, [P, NB, 72])
        IW = at("IW", A0 + 57.25, [P, NB, 8])
        TAB_A2, TAB_I2 = at("TAB_A2", A0 + 58, [P, 2, S]), at("TAB_I2", A0 + 62, [P, 2, S])
        P2, PT2 = at("P2", A0 + 66, [P, 2, S]), at("PT2", A0 + 70, [P, 2, S])
        FW = at("FW", A0 + 66, [P, 4, S])
        OF = at("OF", A0 + 74, [P, NB, S])
        R = at("R", A0 + 82, [P, 3, S])
        OS = at("OS", A0 + 58, [P, NB, S])
        BIAS = [at(f"BIAS{i}", A0 + 82 + 0.5 * (i * (i + 1) // 2), [P, P * (i + 1)]) for i in range(NB)]
        OTH2, OTL2 = at("OTH2", A0, [P, 8, S], F32R), at("OTL2", A0 + 16, [P, 8, S], F32R)
        MH2, ML2 = at("MH2", A0 + 32, [P, 8, S], F32R), at("ML2", A0 + 48, [P, 8, S], F32R)

        SQV = {n: SQC[:, k, :] for k, n in enumerate(SQUARES)}

        def col(name, k=0, n=1, rows=slice(0, P)):
            a = COLS[name][0] + k
            return CO[rows, a:a + n]

        NMX, NBI, RSU, RIN = (SM[:, 4 * k:4 * k + 4] for k in range(4))
        LAM = SM[:, 16:24]
        SSD = SM[:, 24:40]
        RSD = SM[:, 40:56]
        M8 = SM[:, 56:64]
        GM = SM[:, 64:72]
        HG = SM[:, 72:80]
        PIH = SM[:, 80:81]
        EPSC = SM[:, 81:82]
        CND = SM[:, 88:96]

        NORMS = [
            (DT, X, D, "g_mix", XH, XL), (3, LATQ, QR, "g_q", LQH, LQL), (2, LATK, KVR, "g_kv", LKH, LKL),
            (DT, X, D, "g_ffn", XH, XL), (DT, X, D, "g_final", None, None),
            (DT, X, D, 0, XH, XL), (DT, X, D, 1, XH, XL), (DT, X, D, 2, XH, XL)]
        NTB = np.cumsum([0] + [n[0] for n in NORMS]).tolist()
        SPLIT_TB = np.cumsum([0] + [n[0] if n[4] is not None else 0 for n in NORMS]).tolist()

        def repeat(eng, times, body):
            if times == 1:
                body(0)
                return
            with eng.Fori(0, times) as i:
                body(i)

        IN1 = [("copy", LATQ[:, t, :]) for t in range(3)] + [("copy", LATK[:, t, :]) for t in range(2)] \
            + [("rope", KR[:, :], TAB_P1, "rot_p")] \
            + [("rope", DQ[:, t, :], TAB_A1, "rot_a") for t in range(4)] \
            + [("rope", DK[:, t, :], TAB_A1, "rot_a") for t in range(4)]
        IN2 = [("foxq", t) for t in range(4)] + [("foxk", t) for t in range(4)] \
            + [("dsaq", DQ2[:, t, :], TAB_A2, "rot_a") for t in range(4)] \
            + [("rope", IQ[:, t, :], TAB_I2, "rot_i") for t in range(2)] + [("misc", R[:, 14 % 3, :])]

        def rot_tiles(tiles):
            return [k for k, t in enumerate(tiles) if t[0] in ("rope", "dsaq", "misc")]

        ROT1, ROT2 = rot_tiles(IN1), rot_tiles(IN2)
        NRM2 = [k for k, t in enumerate(IN2) if t[0] in ("foxq", "foxk", "dsaq", "misc")]
        ROT_BASE = {"in1": 0, "uq": len(ROT1), "in2": len(ROT1) + 2}
        rot_src = {}

        def q_diff(c, i):
            return DQ[64 * (c % 2):64 * (c % 2) + 64, c // 2, i * P:(i + 1) * P]

        def k_diff(c, n):
            return DK[64 * (c % 2):64 * (c % 2) + 64, c // 2, 0:n]

        ATT = [
            dict(q=q_diff, k=k_diff, v=lambda kb, c: DV[:, kb, (c // 2) * P:(c // 2 + 1) * P], dv=P,
                 scale=DHD ** -0.5, P=P1, PT=PT1),
            dict(q=lambda h, i: QM[0:96, h, i * P:(i + 1) * P], k=lambda h, n: KM[h // 4][0:96, h % 4, 0:n],
                 v=lambda kb, h: VM[:, kb, h * 64:h * 64 + 64], dv=64, scale=(NOPE + ROPE) ** -0.5,
                 P=P1, PT=PT1),
            dict(q=lambda h, i: QF[0:66, h, i * P:(i + 1) * P], k=lambda h, n: KF[0:66, h, 0:n],
                 v=lambda kb, h: VF[:, kb, h * 64:h * 64 + 64], dv=64, scale=0.125, P=P2, PT=PT2),
            dict(q=lambda h, i: DQ2[64 * (h % 2):64 * (h % 2) + 64, h // 2, i * P:(i + 1) * P],
                 k=lambda h, n: DK2[64 * (h % 2):64 * (h % 2) + 64, 0:n],
                 v=lambda kb, h: DVW[:, kb, 0:64], dv=64, scale=0.125, P=P2, PT=PT2)]
        NU = 8 * NB
        XA = {"out1": 0, "down1": DT, "down2": 2 * DT, "out2": 3 * DT, "down3": 4 * DT}
        OUT_T = [(OD, OTH1, OTL1, 4, 0), (OM, OTH1, OTL1, 0, 1), (OF, OTH2, OTL2, 0, 2), (OS, OTH2, OTL2, 4, 3)]

        block = ctx.enter_context(nc.Block())

        @block.sync
        def _(sp):
            sp.dma_start(CO[:], cols_d).then_inc(sem("consts_loaded"), 16)
            sp.dma_start(SQC[:], squares_d).then_inc(sem("consts_loaded"), 16)
            sp.dma_start(X[:, 0:4, :], xT[:, 0:4, :]).then_inc(sem("x_loaded"), 16)
            sp.dma_start(X[:, 4:8, :], xT[:, 4:8, :]).then_inc(sem("x_loaded"), 16)
            for j in range(3):
                sp.dma_start(RAW[j][:], wst[j]).then_inc(sem(f"raw{j}"), 16)

            def more(i):
                for j in range(3):
                    sp.wait_ge(sem("lo_ready"), 3 * i + j + 1)
                    sp.dma_start(RAW[j][:], wst[3 * i + (j + 3)]).then_inc(sem(f"raw{j}"), 16)

            repeat(sp, (NCH - 3) // 3, more)
            for n in range(3 + (NCH - 3) // 3 * 3, NCH):
                sp.wait_ge(sem("lo_ready"), n - 2)
                sp.dma_start(RAW[n % 3][:], wst[n]).then_inc(sem(f"raw{n % 3}"), 16)
            for t in range(DT):
                sp.wait_ge(sem("x_added"), XA["down3"] + t + 1)
                sp.dma_start(out[:, t, :], X[:, t, :]).then_inc(sem("stored"), 16)
            sp.wait_ge(sem("stored"), 16 * DT)

        @block.gpsimd
        def _(pool):
            pool.dma_start(T[:, 0, :].bitcast(I32), pos1_d.partition_broadcast(P)).then_inc(sem("pos_loaded"), 16)
            pool.dma_start(SQ[:, 0, 0:256], lams_d.partition_broadcast(P)).then_inc(sem("lams_loaded"), 16)
            for j in range(2):
                pool.dma_start(ADA[j][:], ada[j]).then_inc(sem(f"ada{j}"), 16)

            def ada_more(i):
                for j in range(2):
                    pool.wait_ge(sem("ada_added"), 2 * i + j + 1)
                    pool.dma_start(ADA[j][:], ada[2 * i + (j + 2)]).then_inc(sem(f"ada{j}"), 16)

            repeat(pool, 7, ada_more)
            pool.wait_ge(sem("rotated"), 1)
            pool.wait_ge(sem("split_lo"), SPLIT_TB[3])
            for h in range(8):
                pool.tensor_copy(KM[h // 4][64:96, h % 4, :], KR[0:32, :]).then_inc(sem("k_shared"), 1)
            repeat(pool, 28, lambda i: ada_more(i + 7))
            pool.wait_ge(sem("x_added"), 3 * DT)
            pool.dma_start(T[:, 1, :].bitcast(I32), pos2_d.partition_broadcast(P)).then_inc(sem("pos_loaded"), 16)
            pool.memset(QF[64:66, :, :], 1.0).then_inc(sem("f_ones"), 1)
            pool.memset(KF[64:66, :, :], 1.0).then_inc(sem("f_ones"), 1)
            pool.wait_ge(sem("f_ones"), 2)
            pool.wait_ge(sem("f_scaled"), 2)
            pool.dma_start(QF[65:66, :, :], FW[0:8, 2, :]).then_inc(sem("f_rows"), 16)
            pool.dma_start(KF[64:65, :, :], FW[0:8, 3, :]).then_inc(sem("f_rows"), 16)

        @block.tensor
        def _(pe):
            mm = nc.tensor.matmul
            released = dict.fromkeys(("in_copied", "v_copied", "proj_copied", "branch_scaled", "x_added", "hid"), 0)

            def all_released():
                for name, count in released.items():
                    if count:
                        pe.wait_ge(sem(name), count)

            def split_product(bank, w, blocks, tiles, moving, first=True, last=True):
                hi, lo = HI[w][:], LO[w][:]
                for b, t in zip(blocks, tiles):
                    a, z = hi[:, b * P:(b + 1) * P], lo[:, b * P:(b + 1) * P]
                    start, stop = first and b == blocks[0], last and b == blocks[-1]
                    mm(bank, a, moving[0][:, t, :], start=start, stop=False)
                    mm(bank, a, moving[1][:, t, :], start=False, stop=False)
                    ins = mm(bank, z, moving[0][:, t, :], start=False, stop=stop)
                return ins

            def chunk(n0, step, i):
                pe.wait_ge(sem("lo_ready"), step * i + (n0 + 1))
                return n0 % 3

            def used(ins):
                ins.then_inc(sem("chunk_used"), 1)

            def norm(k):
                nt = NORMS[k][0]
                if k:
                    pe.wait_ge(sem("stds"), k)
                for t in range(nt):
                    pe.wait_ge(sem("squared"), NTB[k] + t + 1)
                    mm(PS[:, 7, :], SQV["ones"], SQ[:, t % 2, :], start=t == 0, stop=t == nt - 1)\
                        .then_inc(sem("sq_summed"), 1)

            def rotate(q, src, perm, bank):
                mm(PS[:, bank, :], SQV[perm], src, start=True, stop=True).then_inc(sem("rot_mm"), 1)

            def token_major(n0, nchunks, tiles_per, width, moving):
                all_released()
                for j in range(nchunks):
                    w = chunk(n0 + j, 0, 0)
                    for b in range(NB):
                        for r in range(tiles_per):
                            t = j * tiles_per + r
                            lw = 1024 // tiles_per
                            wh, wl = HI[w][:, r * lw:r * lw + width], LO[w][:, r * lw:r * lw + width]
                            xh, xl = (m[:, t, b * P:(b + 1) * P] for m in moving)
                            end = j == nchunks - 1 and r == tiles_per - 1
                            mm(PS[:, b, 0:width], xh, wh, start=t == 0, stop=False)
                            mm(PS[:, b, 0:width], xh, wl, start=False, stop=False)
                            ins = mm(PS[:, b, 0:width], xl, wh, start=False, stop=end)
                    used(ins)
                released["v_copied"] += NB

            def ada_sum(g, bank):
                pe.wait_ge(sem("ada_added"), 8 * g + 8)
                if g:
                    pe.wait_ge(sem("mod"), g)
                for t in range(8):
                    ins = mm(PS[:, bank, t:t + 1], ACC[:, t * P:(t + 1) * P], SQV["ones"][:, 0:1],
                             start=True, stop=True)
                ins.then_inc(sem("ada_summed"), 1)

            def project_in(name, tiles, nrms, rots, moving):
                n0 = FIRST[name]
                all_released()
                e0 = released["in_copied"]
                nn = rr = 0
                for j in range(len(tiles) + 5):
                    if j - 2 >= 0 and j - 2 in nrms:
                        pe.wait_ge(sem("hsq"), nn + 1)
                        if nn >= 2:
                            pe.wait_ge(sem("hstd"), nn - 1)
                        mm(PS[:, 4 + nn % 2, :], SQV["halves"], SQ[:, nn % 2, :], start=True, stop=True)\
                            .then_inc(sem("hsum"), 1)
                        nn += 1
                    for k in rots:
                        if rot_at(tiles, k) == j:
                            q = ROT_BASE[name] + rr
                            if tiles[k][0] == "rope":
                                pe.wait_ge(sem("in_copied"), e0 + k + 1)
                            else:
                                pe.wait_ge(sem("hnormed"), nrms.index(k) + 1)
                            if rr >= 2:
                                pe.wait_ge(sem("rot_read"), q - 1)
                            rotate(q, tiles[k][1], "rot_m" if tiles[k][0] == "misc" else tiles[k][3], 6 + rr % 2 if name == "in2" else 4 + rr % 2)
                            rr += 1
                    if name == "in1" and j == 9:
                        ada_sum(0, 7)
                    if j < len(tiles):
                        w = chunk(n0 + j, 0, 0)
                        if j >= 4:
                            pe.wait_ge(sem("in_copied"), e0 + j - 3)
                        used(split_product(PS[:, j % 4, :], w, range(8), range(8), moving))
                released["in_copied"] += len(tiles)

            def attention(a):
                at_ = ATT[a]
                for u in range(NU + 2):
                    if u < NU:
                        h, i = divmod(u, NB)
                        n = P * (i + 1)
                        if u >= 2:
                            pe.wait_ge(sem("probs"), NU * a + u - 1)
                        mm(PS[:, u % 2, 0:n], at_["q"](h, i), at_["k"](h, n), start=True, stop=True)\
                            .then_inc(sem("scores"), 1)
                    if 1 <= u <= NU:
                        v = u - 1
                        i = v % NB
                        pe.wait_ge(sem("probs"), NU * a + v + 1)
                        if v >= 2:
                            pe.wait_ge(sem("pt_copied"), NU * a + v - 1)
                        for kb in range(i + 1):
                            ins = nc.tensor.transpose(PS[:, 2 + v % 2, kb * P:(kb + 1) * P],
                                                      at_["P"][:, v % 2, kb * P:(kb + 1) * P], SQV["ident"])
                        ins.then_inc(sem("pt"), 1)
                    if u >= 2:
                        v = u - 2
                        h, i = divmod(v, NB)
                        pe.wait_ge(sem("pt_copied"), NU * a + v + 1)
                        if v >= 2:
                            pe.wait_ge(sem("onorm"), NU * a + v - 1)
                        for kb in range(i + 1):
                            ins = mm(PS[:, 4 + v % 2, 0:at_["dv"]], at_["PT"][:, v % 2, kb * P:(kb + 1) * P],
                                     at_["v"](kb, h), start=kb == 0, stop=kb == i)
                        ins.then_inc(sem("pv"), 1)

            def turn(a):
                src, _, _, _, g = OUT_T[a]
                for f in range(4):
                    k = 4 * g + f
                    if k >= 2:
                        pe.wait_ge(sem("turned_lo"), k - 1)
                    for i in range(NB):
                        ins = nc.tensor.transpose(PS[:, 6 + k % 2, i * P:(i + 1) * P],
                                                  src[:, i, f * P:(f + 1) * P], SQV["ident"])
                    ins.then_inc(sem("turned"), 1)

            def merge(b, oh, ol):
                all_released()
                n0 = FIRST[f"merge{b + 1}"]

                def pair(i):
                    for j in range(2):
                        if not isinstance(i, int):
                            pe.wait_ge(sem("branch_scaled"), 2 * i + (DT * b + j - 1))
                        for g in range(2):
                            w = chunk(n0 + 3 * j + g, 6, i)
                            used(split_product(PS[:, 4 * j + g, :], w, range(8), range(8), (XH, XL)))
                        w = chunk(n0 + 3 * j + 2, 6, i)
                        split_product(PS[:, 4 * j + 2, :], w, range(4), range(4), (oh, ol))
                        used(split_product(PS[:, 4 * j + 3, :], w, range(4, 8), range(4, 8), (oh, ol)))

                pair(0)
                with pe.Fori(1, 4) as i:
                    pair(i)
                released["branch_scaled"] += DT

            def out_proj(b, mh, ml):
                all_released()
                n0 = FIRST[f"out{b + 1}"]
                for m in range(DT):
                    w = chunk(n0 + m, 0, 0)
                    if m >= 4:
                        pe.wait_ge(sem("x_added"), XA[f"out{b + 1}"] + m - 3)
                    used(split_product(PS[:, m % 4, :], w, range(8), range(8), (mh, ml)))
                released["x_added"] += DT

            def ffn(f):
                all_released()
                n0 = FIRST[f"up{f + 1}"]

                def three(i, tiles=3):
                    for j in range(tiles):
                        if not (isinstance(i, int) and i == 0):
                            pe.wait_ge(sem("hid"), 3 * i + (FT * f + j - 2))
                        for g in range(2):
                            w = chunk(n0 + 2 * j + g, 6, i)
                            if f == 0 and j == 2 and g == 1 and tiles == 3:
                                ada_sum_loop(i)
                            used(split_product(PS[:, 2 * j + g, :], w, range(8), range(8), (XH, XL)))

                def ada_sum_loop(i):
                    pe.wait_ge(sem("ada_added"), 8 * i + 24)
                    pe.wait_ge(sem("mod"), i + 2)
                    for t in range(8):
                        ins = mm(PS[:, 7, t:t + 1], ACC[:, t * P:(t + 1) * P], SQV["ones"][:, 0:1],
                                 start=True, stop=True)
                    ins.then_inc(sem("ada_summed"), 1)

                three(0)
                with pe.Fori(1, 7) as i:
                    three(i)
                three(7, tiles=1)
                released["hid"] += FT
                all_released()
                n0 = FIRST[f"down{f + 1}"]
                pe.wait_ge(sem("hid_lo"), FT * (f + 1))

                def two(i):
                    for j in range(2):
                        if not (isinstance(i, int) and i == 0):
                            pe.wait_ge(sem("x_added"), 2 * i + (XA[f"down{f + 1}"] + j - 1))
                        for g, blocks in enumerate(LAST_DOWN):
                            w = chunk(n0 + 3 * j + g, 6, i)
                            used(split_product(PS[:, j, :], w, range(blocks), range(8 * g, 8 * g + blocks),
                                               (HIDH, HIDL), first=g == 0, last=g == 2))

                two(0)
                with pe.Fori(1, 4) as i:
                    two(i)
                released["x_added"] += DT

            pe.wait_ge(sem("consts_loaded"), 32)
            norm(0)
            pe.wait_ge(sem("split_lo"), SPLIT_TB[1])
            project_in("in1", IN1, [], ROT1, (XH, XL))
            token_major(FIRST["dv1"], 4, 2, 512, (XH, XL))
            ada_sum(1, 7)
            all_released()
            pe.wait_ge(sem("rotated"), len(ROT1))
            attention(0)
            norm(1)
            norm(2)
            pe.wait_ge(sem("split_lo"), SPLIT_TB[3])
            for j in range(3):
                w = chunk(FIRST["uq"] + j, 0, 0)
                for r in range(2):
                    m = 2 * j + r
                    ins = split_product(PS[:, m, :], w, range(3 * r, 3 * r + 3), range(3), (LQH, LQL))
                used(ins)
            w = chunk(FIRST["uk"], 0, 0)
            for m in range(4):
                pe.wait_ge(sem("proj_copied"), m + 1)
                ins = split_product(PS[:, m, :], w, range(2 * m, 2 * m + 2), range(2), (LKH, LKL))
            used(ins)
            for r in range(2):
                pe.wait_ge(sem("proj_copied"), 5 + r)
                rotate(ROT_BASE["uq"] + r, Y[:, r, :], "rot_p", 6 + r)
            released["proj_copied"] += 10
            token_major(FIRST["uv"], 1, 2, 512, (LKH, LKL))
            all_released()
            pe.wait_ge(sem("q_rotated"), 2)
            pe.wait_ge(sem("k_shared"), 8)
            attention(1)
            pe.wait_ge(sem("diff_normed"), 1)
            turn(0)
            pe.wait_ge(sem("onorm"), 2 * NU)
            turn(1)
            pe.wait_ge(sem("turned_lo"), 8)
            merge(0, OTH1, OTL1)
            pe.wait_ge(sem("merged_lo"), 8)
            out_proj(0, MH1, ML1)
            norm(3)
            pe.wait_ge(sem("split_lo"), SPLIT_TB[4])
            ffn(0)
            norm(4)
            pe.wait_ge(sem("normed"), NTB[5])
            norm(5)
            pe.wait_ge(sem("split_lo"), SPLIT_TB[6])
            ffn(1)
            norm(6)
            pe.wait_ge(sem("split_lo"), SPLIT_TB[7])
            project_in("in2", IN2, NRM2, ROT2, (XH, XL))
            token_major(FIRST["fv2"], 4, 2, 512, (XH, XL))
            token_major(FIRST["dvw2"], 1, 8, 72, (XH, XL))
            pe.wait_ge(sem("ik_spread"), 4)
            pe.wait_ge(sem("rotated"), len(ROT1) + len(ROT2) - 1)
            all_released()
            for u in range(24):
                i, h = 1 + u // 8, u % 8
                b = 32 * (h % 4)
                if u >= 2:
                    pe.wait_ge(sem("dots_read"), u - 1)
                mm(PS[:, u % 2, 0:P * (i + 1)], IQ[b:b + 32, h // 4, i * P:(i + 1) * P],
                   IK[b:b + 32, 0:P * (i + 1)], start=True, stop=True).then_inc(sem("dots"), 1)
            pe.wait_ge(sem("dots_read"), 24)
            pe.wait_ge(sem("f_rows"), 32)
            attention(2)
            pe.wait_ge(sem("selected"), 4)
            attention(3)
            pe.wait_ge(sem("onorm"), 4 * NU)
            turn(2)
            turn(3)
            pe.wait_ge(sem("turned_lo"), 16)
            merge(1, OTH2, OTL2)
            pe.wait_ge(sem("merged_lo"), 16)
            out_proj(1, MH2, ML2)
            norm(7)
            pe.wait_ge(sem("split_lo"), SPLIT_TB[8])
            ffn(2)

        @block.scalar
        def _(act):
            A = nc.scalar.activation

            def split_hi(n0, step=0, i=0):
                n0 += 2
                if isinstance(i, int):
                    n0, step, i = n0 + step * i, 0, 0
                    if n0 >= NCH:
                        return
                if step == 0:
                    act.wait_ge(sem(f"raw{n0 % 3}"), 16 * (n0 // 3 + 1))
                    if n0 >= 3:
                        act.wait_ge(sem("chunk_used"), n0 - 2)
                else:
                    act.wait_ge(sem(f"raw{n0 % 3}"), (16 * step // 3) * i + 16 * (n0 // 3 + 1))
                    act.wait_ge(sem("chunk_used"), step * i + (n0 - 2))
                A(HI[n0 % 3][:], RAW[n0 % 3][:], ACT.Copy).then_inc(sem("hi_ready"), 1)

            def norm(k):
                nt, src, width, g, oh, ol = NORMS[k]
                for t in range(nt):
                    if NTB[k] + t >= 2:
                        act.wait_ge(sem("sq_summed"), NTB[k] + t - 1)
                    A(SQ[:, t % 2, :], src[:, t, :], ACT.Square).then_inc(sem("squared"), 1)
                act.wait_ge(sem("sq_summed"), NTB[k + 1])
                A(RB[:, 0, :], PS[:, 7, :], ACT.Sqrt, bias=EPSC, scale=1.0 / width).then_inc(sem("stds"), 1)
                if oh is None:
                    return
                for t in range(nt):
                    act.wait_ge(sem("normed"), NTB[k] + t + 1)
                    A(oh[:, t, :], Y[:, t % 2, :], ACT.Copy).then_inc(sem("split_hi"), 1)

            def table(k, tab):
                act.wait_ge(sem("angle"), k + 1)
                A(tab[:, 1, :], Y[:, 0, :], ACT.Sin).then_inc(sem("sin"), 1)
                A(Y[:, 1, :], Y[:, 0, :], ACT.Abs).then_inc(sem("absolute"), 1)
                act.wait_ge(sem("absolute"), k + 1)
                A(tab[:, 0, :], Y[:, 1, :], ACT.Sin, bias=PIH, scale=-1.0).then_inc(sem("table"), 1)

            def token_copies(n0, nchunks, dest, width):
                for j in range(nchunks):
                    split_hi(n0 + j)
                act.wait_ge(sem("chunk_used"), n0 + nchunks)
                for b in range(NB):
                    A(dest[:, b, :], PS[:, b, 0:width], ACT.Copy).then_inc(sem("v_copied"), 1)

            def project_in(name, tiles, nrms, rots):
                n0 = FIRST[name]
                nn = 0
                for j in range(len(tiles) + 5):
                    if j < len(tiles):
                        split_hi(n0 + j)
                        act.wait_ge(sem("chunk_used"), n0 + j + 1)
                        kind = tiles[j]
                        if j in nrms:
                            q = nrms.index(j)
                            if q >= 2:
                                act.wait_ge(sem("hsum"), q - 1)
                            A(SQ[:, q % 2, :], PS[:, j % 4, :], ACT.Square).then_inc(sem("hsq"), 1)
                            if q >= 3:
                                act.wait_ge(sem("hnormed"), sum(t <= j - 3 for t in nrms))
                            A(R[:, j % 3, :], PS[:, j % 4, :], ACT.Copy).then_inc(sem("in_copied"), 1)
                        else:
                            A(kind[1], PS[:, j % 4, :], ACT.Copy).then_inc(sem("in_copied"), 1)
                    if j - 2 in nrms:
                        act.wait_ge(sem("hsum"), nn + 1)
                        if nn >= 2:
                            act.wait_ge(sem("hnormed"), nn - 1)
                        A(RB[:, nn % 2, :], PS[:, 4 + nn % 2, :], ACT.Sqrt, bias=EPSC, scale=1.0 / 64)\
                            .then_inc(sem("hstd"), 1)
                        nn += 1

            def attention(a):
                at_ = ATT[a]
                for u in range(NU + 1):
                    if u < NU:
                        n = P * (u % NB + 1)
                        act.wait_ge(sem("smax"), NU * a + u + 1)
                        if u >= 2:
                            act.wait_ge(sem("pt"), NU * a + u - 1)
                        if u >= 4:
                            act.wait_ge(sem("onorm"), NU * a + u - 3)
                        A(at_["P"][:, u % 2, 0:n], PS[:, u % 2, 0:n], ACT.Exp, bias=NBI[:, u % 4:u % 4 + 1],
                          scale=at_["scale"], accum_out=RSU[:, u % 4:u % 4 + 1]).then_inc(sem("probs"), 1)
                    if u >= 1:
                        v = u - 1
                        n = P * (v % NB + 1)
                        act.wait_ge(sem("pt"), NU * a + v + 1)
                        if v >= 2:
                            act.wait_ge(sem("pv"), NU * a + v - 1)
                        A(at_["PT"][:, v % 2, 0:n], PS[:, 2 + v % 2, 0:n], ACT.Copy).then_inc(sem("pt_copied"), 1)

            def turn(a):
                src, oh, ol, f0, g = OUT_T[a]
                for f in range(4):
                    k = 4 * g + f
                    act.wait_ge(sem("turned"), k + 1)
                    A(oh[:, f0 + f, :], PS[:, 6 + k % 2, :], ACT.Copy,
                      scale=GM[:, 0:1] if a == 0 else 1.0).then_inc(sem("turned_hi"), 1)

            def merge(b):
                n0 = FIRST[f"merge{b + 1}"]

                def pair(i):
                    for j in range(2):
                        for g in range(2):
                            split_hi(n0 + 3 * j + g, 6, i)
                            act.wait_ge(sem("chunk_used"), 6 * i + (n0 + 3 * j + g + 1))
                            if b == 0:
                                bias = CO[:, bass.ds(COLS["b_gate"][0] + DT * g + j + 2 * i, 1)]
                            else:
                                bias = 0.0
                            if not (isinstance(i, int) and 8 * b + 2 * i + j == 0):
                                act.wait_ge(sem("merged"), 2 * i + (DT * b + j))
                            A(T[:, g, :], PS[:, 4 * j + g, :], ACT.Sigmoid, bias=bias).then_inc(sem("gate"), 1)
                        split_hi(n0 + 3 * j + 2, 6, i)
                        act.wait_ge(sem("merged"), 2 * i + (8 * b + j + 1))
                        A((MH1, MH2)[b][:, bass.ds(2 * i + j, 1), :], Y[:, j:j + 1, :], ACT.Copy)\
                            .then_inc(sem("merged_hi"), 1)

                pair(0)
                with act.Fori(1, 4) as i:
                    pair(i)

            def out_proj(b):
                for m in range(DT):
                    split_hi(FIRST[f"out{b + 1}"] + m)

            def ffn(f):
                n0 = FIRST[f"up{f + 1}"]

                def three(i, tiles=3):
                    for j in range(tiles):
                        split_hi(n0 + 2 * j, 6, i)
                        act.wait_ge(sem("chunk_used"), 6 * i + (n0 + 2 * j + 1))
                        if not (isinstance(i, int) and i == 0 and j == 0):
                            act.wait_ge(sem("hid"), 3 * i + (FT * f + j))
                        A(T[:, 0, :], PS[:, 2 * j, :], ACT.Silu).then_inc(sem("silu"), 1)
                        split_hi(n0 + 2 * j + 1, 6, i)
                        act.wait_ge(sem("hid"), 3 * i + (FT * f + j + 1))
                        A(HIDH[:, bass.ds(3 * i + j, 1), :], Y[:, 0:1, :], ACT.Copy).then_inc(sem("hid_hi"), 1)

                three(0)
                with act.Fori(1, 7) as i:
                    three(i)
                three(7, tiles=1)
                n0 = FIRST[f"down{f + 1}"]

                def six(i):
                    for j in range(6):
                        split_hi(n0 + j, 6, i)

                with act.Fori(0, 3) as i:
                    six(i)
                six(3)

            split_hi(-2)
            split_hi(-1)
            act.wait_ge(sem("x_loaded"), 32)
            act.wait_ge(sem("eps_set"), 1)
            act.wait_ge(sem("consts_loaded"), 32)
            A(CND, col("cond", 0, DT), ACT.Silu).then_inc(sem("cond_ready"), 1)
            act.wait_ge(sem("lams_used"), 1)
            norm(0)
            table(0, TAB_A1)
            table(1, TAB_P1)
            project_in("in1", IN1, [], ROT1)
            token_copies(FIRST["dv1"], 4, DV, 512)
            A(LAM[:, 2:4], LAM[:, 0:2], ACT.Exp).then_inc(sem("lam_exp"), 1)
            attention(0)
            act.wait_ge(sem("onorm"), NU)
            for k in range(16):
                A(T[:, 0, 0:P], OD[:, k // 4, (k % 4) * P:(k % 4 + 1) * P], ACT.Square,
                  accum_out=SSD[:, k:k + 1]).then_inc(sem("diff_ss"), 1)
                act.wait_ge(sem("diff_ss"), k + 1)
            A(RSD, SSD, ACT.Sqrt, bias=EPSC, scale=1.0 / P).then_inc(sem("diff_std"), 1)
            norm(1)
            norm(2)
            for j in range(3):
                split_hi(FIRST["uq"] + j)
                act.wait_ge(sem("chunk_used"), FIRST["uq"] + j + 1)
                for r in range(2):
                    m = 2 * j + r
                    if m < 4:
                        A(QM[0:64, 2 * m, :], PS[0:64, m, :], ACT.Copy).then_inc(sem("half_copied"), 1)
                        A(QM[0:64, 2 * m + 1, :], PS[64:128, m, :], ACT.Copy).then_inc(sem("proj_copied"), 1)
                    else:
                        A(Y[:, m - 4, :], PS[:, m, :], ACT.Copy).then_inc(sem("proj_copied"), 1)
            split_hi(FIRST["uk"])
            act.wait_ge(sem("chunk_used"), FIRST["uk"] + 1)
            for m in range(4):
                for r in range(2):
                    h = 2 * m + r
                    A(KM[h // 4][0:64, h % 4, :], PS[64 * r:64 * r + 64, m, :], ACT.Copy)\
                        .then_inc(sem("proj_copied" if r else "half_copied"), 1)
            token_copies(FIRST["uv"], 1, VM, 512)
            attention(1)
            act.wait_ge(sem("g_sub_scaled"), 1)
            turn(0)
            turn(1)
            merge(0)
            out_proj(0)
            act.wait_ge(sem("x_added"), 8)
            norm(3)
            ffn(0)
            act.wait_ge(sem("x_added"), 16)
            norm(4)
            act.wait_ge(sem("normed"), NTB[5])
            norm(5)
            ffn(1)
            act.wait_ge(sem("x_added"), 24)
            norm(6)
            table(2, TAB_A2)
            table(3, TAB_I2)
            project_in("in2", IN2, NRM2, ROT2)
            token_copies(FIRST["fv2"], 4, VF, 512)
            token_copies(FIRST["dvw2"], 1, DVW, 72)
            act.wait_ge(sem("f_z"), 1)
            A(FW[0:8, 1, :], FW[0:8, 0, :], ACT.Abs).then_inc(sem("f_act"), 1)
            act.wait_ge(sem("f_act"), 1)
            A(FW[0:8, 2, :], FW[0:8, 1, :], ACT.Exp, scale=-1.0).then_inc(sem("f_act"), 1)
            act.wait_ge(sem("f_act"), 2)
            A(FW[0:8, 3, :], FW[0:8, 2, :], ACT.Ln, bias=1.0).then_inc(sem("f_act"), 1)
            for u in range(24):
                n = P * (2 + u // 8)
                act.wait_ge(sem("dots"), u + 1)
                if u >= 2:
                    act.wait_ge(sem("scored"), u - 1)
                A(T[:, u % 2, 0:n], PS[:, u % 2, 0:n], ACT.Relu, scale=32 ** -0.5).then_inc(sem("dots_read"), 1)
            attention(2)
            attention(3)
            turn(2)
            turn(3)
            merge(1)
            out_proj(1)
            act.wait_ge(sem("x_added"), 32)
            norm(7)
            ffn(2)

        @block.vector
        def _(v):
            V = nc.vector

            def split_lo(n0, step=0, i=0):
                n0 += 2
                if isinstance(i, int):
                    n0, step, i = n0 + step * i, 0, 0
                    if n0 >= NCH:
                        return
                v.wait_ge(sem("hi_ready"), n0 + 1 if step == 0 else step * i + (n0 + 1))
                V.tensor_tensor(LO[n0 % 3][:], RAW[n0 % 3][:], HI[n0 % 3][:].bitcast(F32), ALU.subtract)\
                    .then_inc(sem("lo_ready"), 1)

            def norm(k):
                nt, src, width, g, oh, ol = NORMS[k]
                v.wait_ge(sem("stds"), k + 1)
                V.reciprocal(RB[:, 0, :], RB[:, 0, :]).then_inc(sem("rstd"), 1)
                v.wait_ge(sem("rstd"), k + 1)
                for t in range(nt):
                    s = SPLIT_TB[k] + t
                    if oh is None:
                        V.scalar_tensor_tensor(out=src[:, t, :], in0=src[:, t, :], scalar=col(g, t), in1=RB[:, 0, :],
                                               op0=ALU.mult, op1=ALU.mult).then_inc(sem("normed"), 1)
                        continue
                    if t >= 2:
                        v.wait_ge(sem("split_hi"), s - 1)
                        v.wait_ge(sem("split_lo"), s - 1)
                    if isinstance(g, str):
                        V.scalar_tensor_tensor(out=Y[:, t % 2, :], in0=src[:, t, :], scalar=col(g, t),
                                               in1=RB[:, 0, :], op0=ALU.mult, op1=ALU.mult)\
                            .then_inc(sem("normed"), 1)
                    else:
                        V.scalar_tensor_tensor(out=Y[:, t % 2, :], in0=src[:, t, :], scalar=GM[:, t:t + 1],
                                               in1=RB[:, 0, :], op0=ALU.mult, op1=ALU.mult)\
                            .then_inc(sem("mod_mult"), 1)
                        v.wait_ge(sem("mod_mult"), DT * g + t + 1)
                        c = 3 * DT * g + t
                        V.tensor_scalar(Y[:, t % 2, :], Y[:, t % 2, :], MOD[:, c:c + 1], None, ALU.add)\
                            .then_inc(sem("normed"), 1)
                    if t >= 1:
                        lo(k, t - 1)
                if oh is not None:
                    lo(k, nt - 1)
                    v.wait_ge(sem("split_lo"), SPLIT_TB[k + 1])
                else:
                    v.wait_ge(sem("normed"), NTB[k + 1])

            def lo(k, t):
                oh, ol = NORMS[k][4:]
                v.wait_ge(sem("split_hi"), SPLIT_TB[k] + t + 1)
                V.tensor_tensor(ol[:, t, :], Y[:, t % 2, :], oh[:, t, :].bitcast(F32), ALU.subtract)\
                    .then_inc(sem("split_lo"), 1)

            steps = [0]

            def link(ins):
                steps[0] += 1
                ins.then_inc(sem("dve_link"), 1)
                v.wait_ge(sem("dve_link"), steps[0])

            two_pi = 2 * np.pi
            C1 = 6.28125
            C2 = float(np.round((two_pi - C1) * 2 ** 17) / 2 ** 17)
            C3 = float(np.float32(two_pi - C1 - C2))
            MAGIC = float(1.5 * 2 ** 23)

            def angles(k, pos, freq):
                if k % 2:
                    v.wait_ge(sem("table"), k)
                link(V.tensor_scalar(Y[:, 1, :], pos, col(freq), None, ALU.mult))
                link(V.tensor_scalar(RB[:, 1, :], Y[:, 1, :], 1.0 / two_pi, MAGIC, ALU.mult, ALU.add))
                link(V.tensor_scalar(RB[:, 1, :], RB[:, 1, :], -MAGIC, None, ALU.add))
                for c in (C1, C2, C3):
                    link(V.scalar_tensor_tensor(out=Y[:, 1, :], in0=RB[:, 1, :], scalar=-c, in1=Y[:, 1, :],
                                                op0=ALU.mult, op1=ALU.add))
                V.tensor_scalar(Y[:, 0, :], Y[:, 1, :], 3.1415925, -3.1415925, ALU.min, ALU.max)\
                    .then_inc(sem("angle"), 1)

            def ada_piece(a0, step=0, i=0):
                kt = a0 % 8
                j = a0 % 2
                if step:
                    v.wait_ge(sem(f"ada{j}"), (8 * step) * i + 16 * (a0 // 2 + 1))
                    v.wait_ge(sem("ada_added"), step * i + a0)
                    if kt == 0:
                        v.wait_ge(sem("ada_summed"), i + a0 // 8)
                else:
                    v.wait_ge(sem(f"ada{j}"), 16 * (a0 // 2 + 1))
                    if a0:
                        v.wait_ge(sem("ada_added"), a0)
                    if kt == 0 and a0:
                        v.wait_ge(sem("ada_summed"), a0 // 8)
                if kt == 0:
                    V.tensor_scalar(ACC[:], ADA[j][:], CND[:, 0:1], None, ALU.mult).then_inc(sem("ada_added"), 1)
                else:
                    V.scalar_tensor_tensor(out=ACC[:], in0=ADA[j][:], scalar=CND[:, kt:kt + 1], in1=ACC[:],
                                           op0=ALU.mult, op1=ALU.add).then_inc(sem("ada_added"), 1)

            def ada_take(g, loop=False):
                if loop:
                    v.wait_ge(sem("ada_summed"), g + 1)
                    V.tensor_tensor(MOD[:, bass.ds(8 * g, 8)], PS[:, 7, 0:8],
                                    CO[:, bass.ds(8 * g + COLS["ada_b"][0], 8)], ALU.add).then_inc(sem("mod"), 1)
                else:
                    v.wait_ge(sem("ada_summed"), g + 1)
                    V.tensor_tensor(MOD[:, 8 * g:8 * g + 8], PS[:, 7, 0:8], col("ada_b", 8 * g, 8), ALU.add)\
                        .then_inc(sem("mod"), 1)

            def rope(q, bank, dst, tab, rows=slice(0, P), signal="rotated"):
                v.wait_ge(sem("rot_mm"), q + 1)
                ins = V.tensor_tensor(T[rows, 0, :], PS[rows, bank, :], tab[rows, 1, :], ALU.mult)
                ins.then_inc(sem("rot_read"), 1)
                link(V.tensor_tensor(T[rows, 1, :], dst[rows, :], tab[rows, 0, :], ALU.mult))
                return T

            def project_in(name, tiles, nrms, rots):
                n0 = FIRST[name]
                nn = rr = 0
                for j in range(len(tiles) + 5):
                    if j < len(tiles):
                        split_lo(n0 + j)
                    if j - 2 in nrms:
                        k = j - 2
                        t = tiles[k]
                        q = nn
                        v.wait_ge(sem("hstd"), q + 1)
                        link(V.reciprocal(RB[:, q % 2, :], RB[:, q % 2, :]))
                        v.wait_ge(sem("in_copied"), len(IN1) + k + 1)
                        if t[0] in ("foxq", "foxk"):
                            dst = QF if t[0] == "foxq" else KF
                            g = col("fox_g", 0 if t[0] == "foxq" else 1)
                            for r in range(2):
                                rows = slice(64 * r, 64 * r + 64)
                                ins = V.scalar_tensor_tensor(
                                    out=dst[0:64, 2 * t[1] + r, :], in0=R[rows, k % 3, :], scalar=g[rows, :],
                                    in1=RB[rows, q % 2, :], op0=ALU.mult, op1=ALU.mult)
                            ins.then_inc(sem("hnormed"), 1)
                        elif t[0] == "dsaq":
                            V.scalar_tensor_tensor(out=t[1], in0=R[:, k % 3, :], scalar=col("dsa_g", 0),
                                                   in1=RB[:, q % 2, :], op0=ALU.mult, op1=ALU.mult)\
                                .then_inc(sem("hnormed"), 1)
                        else:
                            V.scalar_tensor_tensor(out=R[0:64, k % 3, :], in0=R[0:64, k % 3, :],
                                                   scalar=col("dsa_g", 1)[0:64, :], in1=RB[0:64, q % 2, :],
                                                   op0=ALU.mult, op1=ALU.mult).then_inc(sem("hnormed"), 1)
                        nn += 1
                    for k in rots:
                        if rot_at(tiles, k) == j:
                            q = ROT_BASE[name] + rr
                            bank = 6 + rr % 2 if name == "in2" else 4 + rr % 2
                            if tiles[k][0] == "misc":
                                src = R[:, k % 3, :]
                                v.wait_ge(sem("rot_mm"), q + 1)
                                lo_, hi_ = slice(0, 64), slice(64, 96)
                                link(V.tensor_tensor(T[lo_, 0, :], PS[lo_, bank, :], TAB_A2[lo_, 1, :], ALU.mult))
                                V.tensor_tensor(T[hi_, 0, :], PS[hi_, bank, :], TAB_I2[hi_, 1, :], ALU.mult)\
                                    .then_inc(sem("rot_read"), 1)
                                link(V.tensor_tensor(T[lo_, 1, :], src[lo_, :], TAB_A2[lo_, 0, :], ALU.mult))
                                link(V.tensor_tensor(T[hi_, 1, :], src[hi_, :], TAB_I2[hi_, 0, :], ALU.mult))
                                v.wait_ge(sem("rot_read"), q + 1)
                                for r in range(2):
                                    V.tensor_tensor(DK2[64 * r:64 * r + 64, :], T[lo_, 0, :], T[lo_, 1, :], ALU.add)\
                                        .then_inc(sem("dk_spread"), 1)
                                for r in range(4):
                                    V.tensor_tensor(IK[32 * r:32 * r + 32, :], T[hi_, 0, :], T[hi_, 1, :], ALU.add)\
                                        .then_inc(sem("ik_spread"), 1)
                                V.tensor_scalar(FW[0:8, 0, :], src[96:104, :], col("f_bias")[96:104, :], None, ALU.add)\
                                    .then_inc(sem("f_z"), 1)
                            else:
                                dst = tiles[k][1]
                                rope(q, bank, dst, tiles[k][2])
                                v.wait_ge(sem("rot_read"), q + 1)
                                V.tensor_tensor(dst, T[:, 0, :], T[:, 1, :], ALU.add).then_inc(sem("rotated"), 1)
                                v.wait_ge(sem("rotated"), (rr if name == "in1" else len(ROT1) + rr) + 1)
                            rr += 1
                    if name == "in1":
                        if j < 16:
                            ada_piece(j)
                        if j == 9:
                            ada_take(0)

            def round_of_selection(q):
                i = 1 + q // 16
                link(V.max(M8, BIAS[i][:]))
                link(V.match_replace(BIAS[i][:], M8, BIAS[i][:], TAKEN))
                if q % 16 == 15:
                    V.tensor_scalar(BIAS[i][:], BIAS[i][:], -2.0e38, NEG, ALU.is_gt, ALU.mult)\
                        .then_inc(sem("selected"), 1)

            def attention(a):
                at_ = ATT[a]
                for u in range(NU + 2):
                    if u < NU:
                        h, i = divmod(u, NB)
                        n = P * (i + 1)
                        bank = PS[:, u % 2, 0:n]
                        v.wait_ge(sem("scores"), NU * a + u + 1)
                        if a == 3:
                            link(V.tensor_tensor(bank, bank, BIAS[i][:], ALU.add))
                        else:
                            d = PS[:, u % 2, i * P:(i + 1) * P]
                            link(V.tensor_tensor(d, d, SQV["causal"], ALU.add))
                        c = slice(u % 4, u % 4 + 1)
                        if u >= 4:
                            v.wait_ge(sem("probs"), NU * a + u - 3)
                        link(V.tensor_reduce(NMX[:, c], bank, AX, ALU.max, negate=True))
                        V.tensor_scalar(NBI[:, c], NMX[:, c], at_["scale"], None, ALU.mult)\
                            .then_inc(sem("smax"), 1)
                    if a == 2 and u < NU:
                        for q in range(u * 48 // NU, (u + 1) * 48 // NU):
                            round_of_selection(q)
                    if u >= 2:
                        w = u - 2
                        h, i = divmod(w, NB)
                        r = RIN[:, w % 4:w % 4 + 1]
                        v.wait_ge(sem("probs"), NU * a + w + 1)
                        link(V.reciprocal(r, RSU[:, w % 4:w % 4 + 1]))
                        if a == 0 and h % 2:
                            link(V.tensor_tensor(r, r, LAM[:, 4:5], ALU.mult))
                        v.wait_ge(sem("pv"), NU * a + w + 1)
                        o = PS[:, 4 + w % 2, 0:at_["dv"]]
                        if a == 0:
                            dst = OD[:, i, (h // 2) * P:(h // 2 + 1) * P]
                            if h % 2:
                                ins = V.scalar_tensor_tensor(out=dst, in0=o, scalar=r, in1=dst, op0=ALU.mult,
                                                             op1=ALU.add)
                            else:
                                ins = V.tensor_scalar(dst, o, r, None, ALU.mult)
                        else:
                            dst = (None, OM, OF, OS)[a]
                            ins = V.tensor_scalar(dst[:, i, h * 64:h * 64 + 64], o, r, None, ALU.mult)
                        ins.then_inc(sem("onorm"), 1)

            def turn(a):
                src, oh, ol, f0, g = OUT_T[a]
                for f in range(4):
                    k = 4 * g + f
                    v.wait_ge(sem("turned_hi"), k + 1)
                    if a == 0:
                        ins = V.scalar_tensor_tensor(out=ol[:, f0 + f, :], in0=PS[:, 6 + k % 2, :], scalar=GM[:, 0:1],
                                                     in1=oh[:, f0 + f, :].bitcast(F32), op0=ALU.mult,
                                                     op1=ALU.subtract)
                    else:
                        ins = V.tensor_tensor(ol[:, f0 + f, :], PS[:, 6 + k % 2, :],
                                              oh[:, f0 + f, :].bitcast(F32), ALU.subtract)
                    ins.then_inc(sem("turned_lo"), 1)

            def merge(b):
                n0 = FIRST[f"merge{b + 1}"]
                mh, ml = ((MH1, ML1), (MH2, ML2))[b]

                def pair(i):
                    for j in range(2):
                        for g in range(3):
                            split_lo(n0 + 3 * j + g, 6, i)
                        v.wait_ge(sem("chunk_used"), 6 * i + (n0 + 3 * j + 3))
                        v.wait_ge(sem("gate"), 4 * i + (16 * b + 2 * j + 2))
                        for g in range(2):
                            V.tensor_tensor(T[:, g, :], T[:, g, :], PS[:, 4 * j + 2 + g, :], ALU.mult)\
                                .then_inc(sem("branch_scaled" if g else "first_scaled"), 1)
                        v.wait_ge(sem("branch_scaled"), 2 * i + (DT * b + j + 1))
                        if not (isinstance(i, int) and 2 * i + DT * b == 0):
                            v.wait_ge(sem("merged_lo"), 2 * i + (DT * b + j - 1))
                        V.tensor_tensor(Y[:, j, :], T[:, 0, :], T[:, 1, :], ALU.add).then_inc(sem("merged"), 1)
                        v.wait_ge(sem("merged_hi"), 2 * i + (8 * b + j + 1))
                        V.tensor_tensor(ml[:, bass.ds(2 * i + j, 1), :], Y[:, j:j + 1, :],
                                        mh[:, bass.ds(2 * i + j, 1), :].bitcast(F32), ALU.subtract)\
                            .then_inc(sem("merged_lo"), 1)

                pair(0)
                with v.Fori(1, 4) as i:
                    pair(i)

            def out_proj(b):
                n0 = FIRST[f"out{b + 1}"]
                for m in range(DT):
                    split_lo(n0 + m)
                    v.wait_ge(sem("chunk_used"), n0 + m + 1)
                    if b == 0:
                        V.tensor_tensor(X[:, m, :], X[:, m, :], PS[:, m % 4, :], ALU.add)\
                            .then_inc(sem("x_added"), 1)
                    else:
                        c = 5 * DT + m
                        V.scalar_tensor_tensor(out=X[:, m, :], in0=PS[:, m % 4, :], scalar=MOD[:, c:c + 1],
                                               in1=X[:, m, :], op0=ALU.mult, op1=ALU.add)\
                            .then_inc(sem("x_added"), 1)

            def ffn(f):
                n0 = FIRST[f"up{f + 1}"]

                def three(i, tiles=3):
                    for j in range(tiles):
                        split_lo(n0 + 2 * j, 6, i)
                        if f == 0 and tiles == 3 and j < 2:
                            for r in range(2):
                                ada_piece(16 + 4 * j + r, 8, i)
                        split_lo(n0 + 2 * j + 1, 6, i)
                        v.wait_ge(sem("chunk_used"), 6 * i + (n0 + 2 * j + 2))
                        v.wait_ge(sem("silu"), 3 * i + (FT * f + j + 1))
                        if not (isinstance(i, int) and FT * f + 3 * i + j == 0):
                            v.wait_ge(sem("hid_lo"), 3 * i + (FT * f + j))
                        V.tensor_tensor(Y[:, 0, :], T[:, 0, :], PS[:, 2 * j + 1, :], ALU.mult).then_inc(sem("hid"), 1)
                        v.wait_ge(sem("hid_hi"), 3 * i + (FT * f + j + 1))
                        V.tensor_tensor(HIDL[:, bass.ds(3 * i + j, 1), :], Y[:, 0:1, :],
                                        HIDH[:, bass.ds(3 * i + j, 1), :].bitcast(F32), ALU.subtract)\
                            .then_inc(sem("hid_lo"), 1)
                        if f == 0 and tiles == 3 and j < 2:
                            for r in range(2):
                                ada_piece(18 + 4 * j + r, 8, i)
                        if f == 0 and tiles == 3 and j == 2:
                            ada_take(i + 2, loop=True)

                three(0)
                with v.Fori(1, 7) as i:
                    three(i)
                three(7, tiles=1)
                n0 = FIRST[f"down{f + 1}"]

                def two(i):
                    for j in range(2):
                        for g in range(3):
                            split_lo(n0 + 3 * j + g, 6, i)
                        v.wait_ge(sem("chunk_used"), 6 * i + (n0 + 3 * j + 3))
                        xt = X[:, bass.ds(2 * i + j, 1), :]
                        if f == 0:
                            V.tensor_tensor(xt, xt, PS[:, j:j + 1, :], ALU.add).then_inc(sem("x_added"), 1)
                        else:
                            V.scalar_tensor_tensor(out=xt, in0=PS[:, j:j + 1, :],
                                                   scalar=HG[:, bass.ds(2 * i + j, 1)], in1=xt,
                                                   op0=ALU.mult, op1=ALU.add).then_inc(sem("x_added"), 1)

                with v.Fori(0, 3) as i:
                    two(i)
                two(3)

            def modulation(s):
                link(V.tensor_scalar(GM, MOD[:, (3 * s + 1) * DT:(3 * s + 2) * DT], 1.0, None, ALU.add))
                link(V.tensor_tensor(GM, GM, col("g2", s * DT, DT), ALU.mult))
                link(V.tensor_scalar(HG, MOD[:, (3 * s + 2) * DT:(3 * s + 3) * DT], 0.5, None, ALU.mult))

            link(V.memset(PIH, float(np.pi / 2)))
            V.memset(EPSC, EPS).then_inc(sem("eps_set"), 1)
            v.wait_ge(sem("pos_loaded"), 16)
            v.wait_ge(sem("consts_loaded"), 32)
            v.wait_ge(sem("lams_loaded"), 16)
            for j in range(2):
                link(V.tensor_tensor(SQ[:, 1, 64 * j:64 * j + 64], SQ[:, 0, 128 * j:128 * j + 64],
                                     SQ[:, 0, 128 * j + 64:128 * j + 128], ALU.mult))
                V.tensor_reduce(LAM[:, j:j + 1], SQ[:, 1, 64 * j:64 * j + 64], AX, ALU.add)\
                    .then_inc(sem("lams_used" if j else "lam_half"), 1)
            v.wait_ge(sem("x_loaded"), 32)
            split_lo(-2)
            split_lo(-1)
            link(V.tensor_copy(T[:, 0, :], T[:, 0, :].bitcast(I32)))
            norm(0)
            angles(0, T[:, 0, :], "freq_a")
            angles(1, T[:, 0, :], "freq_p")
            v.wait_ge(sem("table"), 2)
            v.wait_ge(sem("cond_ready"), 1)
            project_in("in1", IN1, [], ROT1)
            for j in range(4):
                split_lo(FIRST["dv1"] + j)
            ada_take(1)
            v.wait_ge(sem("lam_exp"), 1)
            link(V.tensor_tensor(LAM[:, 4:5], LAM[:, 3:4], LAM[:, 2:3], ALU.subtract))
            link(V.tensor_scalar(LAM[:, 4:5], LAM[:, 4:5], -(0.8 - 0.6), None, ALU.add))
            attention(0)
            v.wait_ge(sem("diff_std"), 1)
            link(V.reciprocal(RSD, RSD))
            for k in range(16):
                o = OD[:, k // 4, (k % 4) * P:(k % 4 + 1) * P]
                ins = V.tensor_scalar(o, o, RSD[:, k:k + 1], None, ALU.mult)
            ins.then_inc(sem("diff_normed"), 1)
            V.tensor_scalar(GM[:, 0:1], col("g_sub"), 1.0 - (0.8 - 0.6), None, ALU.mult)\
                .then_inc(sem("g_sub_scaled"), 1)
            norm(1)
            norm(2)
            for j in range(4):
                split_lo(FIRST["uq"] + j)
            for r in range(2):
                q = ROT_BASE["uq"] + r
                rope(q, 6 + r, Y[:, r, :], TAB_P1)
                v.wait_ge(sem("rot_read"), q + 1)
                for h in range(4):
                    rows = slice(32 * h, 32 * h + 32)
                    ins = V.tensor_tensor(QM[64:96, 4 * r + h, :], T[rows, 0, :], T[rows, 1, :], ALU.add)
                ins.then_inc(sem("q_rotated"), 1)
                v.wait_ge(sem("q_rotated"), r + 1)
            split_lo(FIRST["uv"])
            attention(1)
            v.wait_ge(sem("g_sub_scaled"), 1)
            turn(0)
            turn(1)
            merge(0)
            out_proj(0)
            norm(3)
            ffn(0)
            norm(4)
            v.wait_ge(sem("normed"), NTB[5])
            v.wait_ge(sem("mod"), 9)
            modulation(0)
            norm(5)
            ffn(1)
            modulation(1)
            norm(6)
            v.wait_ge(sem("pos_loaded"), 32)
            link(V.tensor_copy(T[:, 1, :], T[:, 1, :].bitcast(I32)))
            angles(2, T[:, 1, :], "freq_a")
            angles(3, T[:, 1, :], "freq_i")
            v.wait_ge(sem("table"), 4)
            project_in("in2", IN2, NRM2, ROT2)
            for j in range(5):
                split_lo(FIRST["fv2"] + j)
            v.wait_ge(sem("f_act"), 3)
            link(V.tensor_scalar(FW[0:8, 0, :], FW[0:8, 0, :], 0.0, None, ALU.min))
            link(V.tensor_tensor(FW[0:8, 0, :], FW[0:8, 0, :], FW[0:8, 3, :], ALU.subtract))
            a, b, d = 0, 1, 1
            while d < S:
                V.tensor_copy(FW[0:8, b, 0:d], FW[0:8, a, 0:d]).then_inc(sem("f_head"), 1)
                link(V.tensor_tensor(FW[0:8, b, d:S], FW[0:8, a, d:S], FW[0:8, a, 0:S - d], ALU.add))
                a, b, d = b, a, 2 * d
            for k, s in ((2, 8.0), (3, -8.0)):
                V.tensor_scalar(FW[0:8, k, :], FW[0:8, a, :], s, None, ALU.mult).then_inc(sem("f_scaled"), 1)
            v.wait_ge(sem("v_copied"), 16)
            link(V.tensor_scalar(IW[:], DVW[:, :, 64:72], 8 ** -0.5, None, ALU.mult))
            V.tensor_copy(BIAS[0][:], SQV["chunked"]).then_inc(sem("selected"), 1)
            for u in range(24):
                i, h = 1 + u // 8, u % 8
                n = P * (i + 1)
                v.wait_ge(sem("dots_read"), u + 1)
                if h == 0:
                    V.tensor_scalar(BIAS[i][:], T[:, u % 2, 0:n], IW[:, i, 0:1], None, ALU.mult)\
                        .then_inc(sem("scored"), 1)
                else:
                    v.wait_ge(sem("scored"), u)
                    V.scalar_tensor_tensor(out=BIAS[i][:], in0=T[:, u % 2, 0:n], scalar=IW[:, i, h:h + 1],
                                           in1=BIAS[i][:], op0=ALU.mult, op1=ALU.add).then_inc(sem("scored"), 1)
            v.wait_ge(sem("scored"), 24)
            for i in range(1, NB):
                d = BIAS[i][:, i * P:(i + 1) * P]
                link(V.tensor_tensor(d, d, SQV["chunked"], ALU.add))
            attention(2)
            attention(3)
            turn(2)
            turn(3)
            merge(1)
            out_proj(1)
            modulation(2)
            norm(7)
            ffn(2)


def rot_at(tiles, k):
    return k + (4 if tiles[k][0] in ("dsaq", "misc") else 2)


def _tile(w):
    k, m = w.shape
    a = w.reshape(k // P, P, m).transpose(1, 0, 2).reshape(P, k // P * m)
    if a.shape[1] < 1024:
        a = np.concatenate([a, np.zeros((P, 1024 - a.shape[1]), w.dtype)], axis=1)
    return a


def _pad(w, n):
    return np.concatenate([w, np.zeros((w.shape[0], n - w.shape[1]), w.dtype)], axis=1)


def _ffn(gate, up, down):
    chunks = []
    for t in range(FT):
        chunks += [_tile(gate[:, t * P:(t + 1) * P]), _tile(up[:, t * P:(t + 1) * P])]
    for m in range(DT):
        w = down[:, m * P:(m + 1) * P]
        chunks += [_tile(w[0:1024]), _tile(w[1024:2048]), _tile(w[2048:FF])]
    return chunks


def _merge(gates, a, b):
    chunks = []
    for m in range(DT):
        c = slice(m * P, (m + 1) * P)
        chunks += [_tile(gates[:, :D][:, c]), _tile(gates[:, D:][:, c]), _tile(np.concatenate([a[:, c], b[:, c]]))]
    return chunks


def _tiles(w):
    return [_tile(w[:, m * P:(m + 1) * P]) for m in range(w.shape[1] // P)]


def _weights(a):
    w1, w2 = a["w_in"][0], a["w_in_2"][0]
    lat = QR + KVR
    o = lat + ROPE
    chunks = _tiles(w1[:, :lat]) + [_tile(_pad(w1[:, lat:o], P))] + _tiles(w1[:, o:o + 1024])
    chunks += [_tile(w1[256 * j:256 * j + 256, o + 1024:o + 1536]) for j in range(4)]
    uq = a["mla_w_uq"][0].reshape(QR, H1, NOPE + ROPE)
    uq = np.concatenate([uq[:, :, :NOPE].reshape(QR, 512), uq[:, :, NOPE:].reshape(QR, 256)], axis=1)
    for j in range(3):
        chunks.append(_pad(np.concatenate([_tile(uq[:, (2 * j + r) * P:(2 * j + r + 1) * P])[:, :384]
                                           for r in range(2)], axis=1), 1024))
    ukv = a["mla_w_ukv"][0].reshape(KVR, H1, NOPE + VDIM)
    uk, uv = ukv[:, :, :NOPE].reshape(KVR, 512), ukv[:, :, NOPE:].reshape(KVR, 512)
    chunks.append(np.concatenate([_tile(uk[:, m * P:(m + 1) * P])[:, :256] for m in range(4)], axis=1))
    chunks.append(_tile(uv))
    chunks += _merge(w1[:, o + 1536:], a["w_branch_mla"][0], a["w_branch_diff"][0])
    chunks += _tiles(a["w_out"][0])
    chunks += _ffn(a["w_ffn_gate"][0], a["w_ffn_up"][0], a["w_ffn_down"][0])
    chunks += _ffn(a["ffn1_w1_2"][0], a["ffn1_w3_2"][0], a["ffn1_w2_2"][0])
    fq, fk, fv, ff, dq, dk, dv, iq, ik, iw, gates = np.split(
        w2, np.cumsum([512, 512, 512, 8, 512, 64, 64, 256, 32, 8]).tolist(), axis=1)
    chunks += _tiles(fq) + _tiles(fk) + _tiles(dq) + _tiles(iq)
    chunks.append(_tile(_pad(np.concatenate([dk, ik, ff], axis=1), P)))
    chunks += [_tile(fv[256 * j:256 * j + 256]) for j in range(4)]
    chunks.append(_tile(_pad(np.concatenate([dv, iw], axis=1), P)))
    chunks += _merge(gates, a["w_br_fox_2"][0], a["w_br_dsa_2"][0])
    chunks += _tiles(a["w_out_2"][0])
    chunks += _ffn(a["ffn2_w1_2"][0], a["ffn2_w3_2"][0], a["ffn2_w2_2"][0])
    return np.stack(chunks)


def _freq(rot, period):
    half = rot // 2
    f = (THETA ** (-np.arange(half) * 2.0 / rot)).astype(np.float32)
    col = np.zeros(P, np.float32)
    for p in range(P):
        if p % period < rot:
            col[p] = f[p % period % half]
    return col


def _columns(a):
    c = np.zeros((P, NCOLS), np.float32)

    def put(name, v, k=0):
        v = np.asarray(v).reshape(-1, P).T
        c[:, COLS[name][0] + k:COLS[name][0] + k + v.shape[1]] = v

    put("g_mix", a["norm_mix_g"])
    put("g_q", a["mla_q_norm_g"])
    put("g_kv", a["mla_kv_norm_g"])
    put("g_sub", a["diff_subln_g"])
    put("g_ffn", a["norm_ffn_g"])
    put("g_final", a["norm_final_g"])
    put("b_gate", a["b_gate"])
    put("g2", a["norm_g_2"])
    put("ada_b", a["ada_b_2"])
    put("cond", a["c_2"])
    for n, src in (("fox_g", a["fox_qk_g_2"][0]), ("dsa_g", a["dsa_qk_g_2"][0])):
        for k in range(2):
            put(n, np.concatenate([src[k], src[k]]), k)
    c[96:104, COLS["f_bias"][0]] = a["fox_f_bias_2"][0]
    put("freq_a", _freq(16, 64))
    put("freq_p", _freq(32, 32))
    put("freq_i", _freq(8, 32))
    return c


def _squares():
    q = np.zeros((P, NSQ, P), np.float32)
    n = {name: k for k, name in enumerate(SQUARES)}
    q[:, n["ident"], :] = np.eye(P)
    q[:, n["ones"], :] = 1.0
    q[:64, n["halves"], :64] = q[64:, n["halves"], 64:] = 1.0
    for name, spans in (("rot_a", [(0, 8), (64, 8)]), ("rot_p", [(32 * b, 16) for b in range(4)]),
                        ("rot_i", [(32 * b, 4) for b in range(4)]), ("rot_m", [(0, 8), (64, 4)])):
        for first, half in spans:
            for r in range(first, first + half):
                q[r + half, n[name], r] = -1.0
                q[r, n[name], r + half] = 1.0
    q[:, n["causal"], :] = np.triu(np.full((P, P), NEG, np.float32), 1)
    q[:CHUNK, n["chunked"], CHUNK:] = NEG
    return q


def kernel(**inputs):
    import concourse.bacc as bacc
    from concourse.bass_utils import run_bass_kernel_spmd

    a = {k: np.asarray(v) for k, v in inputs.items()}
    arrays = {
        "weights": _weights(a),
        "ada": np.ascontiguousarray(a["ada_w_2"][0].reshape(DT, P, 9, D).transpose(2, 0, 1, 3).reshape(72, P, D)),
        "x_in": np.ascontiguousarray(a["x"][0].T.reshape(DT, P, S).transpose(1, 0, 2)),
        "columns": _columns(a),
        "squares": _squares(),
        "positions1": a["positions"].reshape(S),
        "positions2": a["positions_2"].reshape(S),
        "lambdas": np.concatenate([a[f"diff_lambda_{n}"].reshape(-1) for n in ("q1", "k1", "q2", "k2")]),
    }
    nc = bacc.Bacc("TRN2", target_bir_lowering=False, num_devices=1)
    args = [nc.dram_tensor(n, v.shape, mybir.dt.from_np(v.dtype), kind="ExternalInput").ap()
            for n, v in arrays.items()]
    out = nc.dram_tensor("y_out", (P, DT, S), F32, kind="ExternalOutput").ap()
    build(nc, *args, out)
    got = run_bass_kernel_spmd(nc, [arrays], core_ids=[0]).results[0]["y_out"]
    return np.ascontiguousarray(got.transpose(1, 0, 2).reshape(D, S).T)[None]
```

```python
from contextlib import ExitStack

import numpy as np

import concourse.bass as bass
from concourse import mybir

F32 = mybir.dt.float32
F32R = mybir.dt.float32r
I32 = mybir.dt.int32
BF16 = mybir.dt.bfloat16
ALU = mybir.AluOpType
ACT = mybir.ActivationFunctionType
AX = mybir.AxisListType.X

P = 128
S = 512
D = 1024
DT = D // P
FF = 2816
FT = FF // P
NB = S // P
EPS = 1e-6
NEG = -1.0e30
TAKEN = -3.0e38
THETA = 500000.0
H1, NOPE, ROPE, VDIM = 8, 64, 32, 64
QR, KVR = 384, 256
DH, DHD = 4, 64
TOPK = 128
CHUNK = 64

COLS = {}
_at = 0
for _name, _n in (("g_mix", DT), ("g_q", QR // P), ("g_kv", KVR // P), ("g_sub", 1), ("g_ffn", DT),
                  ("g_final", DT), ("b_gate", 2 * DT), ("g2", 3 * DT), ("ada_b", 9 * DT), ("cond", DT),
                  ("fox_g", 2), ("dsa_g", 2), ("f_bias", 1), ("freq_a", 1), ("freq_p", 1),
                  ("freq_i", 1)):
    COLS[_name] = (_at, _n)
    _at += _n
NCOLS = _at
SQUARES = ("ident", "ones", "halves", "rot_a", "rot_p", "rot_i", "rot_m", "causal", "chunked")
NSQ = len(SQUARES)

STREAM = (("in1", 14), ("dv1", 4), ("uq", 3), ("uk", 1), ("uv", 1), ("merge1", 24), ("out1", 8),
          ("up1", 2 * FT), ("down1", 3 * DT),
          ("up2", 2 * FT), ("down2", 3 * DT), ("in2", 16), ("fv2", 4), ("gates2", 2 * DT), ("branch2", 8),
          ("out2", 8), ("up3", 2 * FT), ("down3", 3 * DT))
FIRST = {}
_at = 0
for _name, _n in STREAM:
    FIRST[_name] = _at
    _at += _n
NCH = _at
LAST_DOWN = [8, 8, 6]

KB = 1024


def build(nc, wst, ada, xT, cols_d, squares_d, pos1_d, pos2_d, lams_d, out):
    ctx = ExitStack()
    with ctx:
        used_sems = {}

        def sem(name):
            if name not in used_sems:
                used_sems[name] = ctx.enter_context(nc.semaphore(name))
            return used_sems[name]

        region = ctx.enter_context(nc.sbuf_tensor("region", [P, 207 * KB // 4], F32))
        base = 0
        if nc.sbuf_base - 207 * KB > 0:
            base = nc.sbuf_base - 207 * KB

        def at(name, kb, shape, dt=F32):
            return nc.alloc_sbuf_tensor_at(name, shape, dt, offset=base + int(kb * KB))

        PS = ctx.enter_context(nc.psum_tensor("PS", [P, 8, S], F32))

        WARM = [(4, 1, 2), (1, 1, 1), (1, 1, 1), (1, 1, 2), (1, 1, 2), (1, 1, 2), (1, 1, 2), (1, 1, 2)]
        FV_BANKS = (0, 1, 2, 5)
        FORGET_AT = 9

        X = at("X", 0, [P, DT, S])
        XH, XL = at("XH", 16, [P, DT, S], F32R), at("XL", 32, [P, DT, S], F32R)
        RAW = [at(f"RAW{j}", 48 + 4 * j, [P, 1024]) for j in range(3)]
        HI = [at(f"HI{j}", 60 + 4 * j, [P, 1024], F32R) for j in range(3)]
        LO = [at(f"LO{j}", 72 + 4 * j, [P, 1024], F32R) for j in range(3)]
        ADA = [at(f"ADA{j}", 84 + 4 * j, [P, 1024]) for j in range(2)]
        ACC = at("ACC", 92, [P, 1024])
        RB = at("RB", 96, [P, 2, S])
        SQ = at("SQ", 100, [P, 2, S])
        Y = at("Y", 104, [P, 2, S])
        T = at("T", 108, [P, 2, S])
        SQC = at("SQC", 112, [P, NSQ, P])
        CO = at("CO", 116.5, [P, NCOLS])
        MOD = at("MOD", 117.25, [P, 9 * DT])
        SM = at("SM", 117.625, [P, 96])
        IDENT_B, CAUSAL_B = at("IDENT_B", 206, [P, P], BF16), at("CAUSAL_B", 206.25, [P, P], BF16)
        SM2 = at("SM2", 206.5, [P, 48])
        A0 = 118
        HIDH = at("HIDH", A0, [P, FT, S], F32R)
        HIDL = at("HIDL", A0 + 44, [P, FT, S], F32R)
        LATQ = at("LATQ", A0, [P, 3, S])
        LATK = at("LATK", A0 + 6, [P, 2, S])
        KR = at("KR", A0 + 10, [P, S])
        DQ, DK = at("DQ", A0 + 12, [P, 4, S]), at("DK", A0 + 20, [P, 4, S])
        DV = at("DV", A0 + 28, [P, NB, S])
        TAB_A1 = at("TAB_A1", A0 + 36, [P, 2, S])
        TAB_P1 = at("TAB_P1", A0 + 40, [P, 2, S])
        P1 = [at(f"P1_{j}", A0 + 60 + 2 * j, [P, S]) for j in range(3)]
        PT1 = [at(f"PT1_{j}", A0 + 66 + 2 * j, [P, S]) for j in range(2)]
        OD = at("OD", A0 + 52, [P, NB, S])
        LQH, LQL = at("LQH", A0 + 60, [P, 3, S], F32R), at("LQL", A0 + 66, [P, 3, S], F32R)
        LKH, LKL = at("LKH", A0 + 72, [P, 2, S], F32R), at("LKL", A0 + 76, [P, 2, S], F32R)
        QM = at("QM", A0 + 12, [P, 8, S])
        VM = at("VM", A0 + 28, [P, NB, S])
        KM = [at("KM0", A0 + 80, [P, 4, S]), at("KM1", A0, [P, 4, S])]
        OM = at("OM", A0 + 36, [P, NB, S])
        OTH1, OTL1 = at("OTH1", A0 + 60, [P, 8, S], F32R), at("OTL1", A0 + 12, [P, 8, S], F32R)
        MH1, ML1 = at("MH1", A0 + 28, [P, 8, S], F32R), at("ML1", A0 + 44, [P, 8, S], F32R)
        QF, KF = at("QF", A0, [P, 8, S]), at("KF", A0 + 16, [P, 8, S])
        VF = at("VF", A0 + 32, [P, NB, S])
        DQ2 = at("DQ2", A0 + 40, [P, 4, S])
        IQ, IK, DK2 = at("IQ", A0 + 48, [P, 2, S]), at("IK", A0 + 52, [P, S]), at("DK2", A0 + 54, [P, S])
        DVW = at("DVW", A0 + 56, [P, NB, 72])
        IW = at("IW", A0 + 57.25, [P, NB, 8])
        TAB_A2, TAB_I2 = at("TAB_A2", 84, [P, 2, S]), at("TAB_I2", 88, [P, 2, S])
        P2 = [at(f"P2_{j}", A0 + 66 + 2 * j, [P, S]) for j in range(3)]
        PT2 = [at("PT2_0", A0 + 72, [P, S]), at("PT2_1", A0 + 52, [P, S])]
        MASK = [at(f"MASK{i}", A0 + 48 + 0.25 * (i * (i + 1) // 2), [P, P * (i + 1)], BF16) for i in range(NB)]
        FW = at("FW", A0 + 66, [P, 4, S])
        OF = at("OF", A0 + 74, [P, NB, S])
        R = at("R", A0 + 80, [P, 4, S])
        MISC = at("MISC", A0 + 74, [P, S])
        VW = at("VW", A0 + 76, [P, S])
        OS = at("OS", A0 + 58, [P, NB, S])
        BIAS = [at(f"BIAS{i}", A0 + 58 + 0.5 * (i * (i + 1) // 2), [P, P * (i + 1)]) for i in range(NB)]
        OTH2, OTL2 = at("OTH2", A0 + 32, [P, 8, S], F32R), at("OTL2", A0 + 66, [P, 8, S], F32R)
        GATE_F = [at(f"GATE_F{m}", 84 + 2 * m if m < 6 else A0 + 82 + 2 * (m - 6), [P, S]) for m in range(DT)]
        GATE_D = at("GATE_D", A0, [P, 8, S])
        MH2, ML2 = at("MH2", A0 + 16, [P, 8, S], F32R), at("ML2", A0, [P, 8, S], F32R)
        GATE2 = [[g[:, :] for g in GATE_F], [GATE_D[:, m, :] for m in range(DT)]]

        SQV = {n: SQC[:, k, :] for k, n in enumerate(SQUARES)}

        def col(name, k=0, n=1, rows=slice(0, P)):
            a = COLS[name][0] + k
            return CO[rows, a:a + n]

        NMX, NBI, RSU, RIN = (SM[:, 4 * k:4 * k + 4] for k in range(4))
        LAM = SM[:, 16:24]
        SSD = SM[:, 24:40]
        RSD = SM[:, 40:56]
        M8 = SM[:, 56:64]
        GM = SM[:, 64:72]
        HG = SM[:, 72:80]
        PIH = SM[:, 80:81]
        EPSC = SM[:, 81:82]
        CND = SM[:, 88:96]
        FOXQ_G, DSAQ_G = SM[:, 82:83], SM[:, 83:84]
        NSTD, NR = SM2[:, 0:4], SM2[:, 4:8]
        HSTD = [SM2[:, 8 + 8 * k:16 + 8 * k] for k in range(2)]
        HR = [SM2[:, 24 + 8 * k:32 + 8 * k] for k in range(2)]

        NORMS = [
            (DT, X, D, "g_mix", XH, XL), (3, LATQ, QR, "g_q", LQH, LQL), (2, LATK, KVR, "g_kv", LKH, LKL),
            (DT, X, D, "g_ffn", XH, XL), (DT, X, D, "g_final", None, None),
            (DT, X, D, 0, XH, XL), (DT, X, D, 1, XH, XL), (DT, X, D, 2, XH, XL)]
        NTB = np.cumsum([0] + [n[0] for n in NORMS]).tolist()
        SAB = np.cumsum([0] + [n[0] - 1 for n in NORMS]).tolist()
        SPLIT_TB = np.cumsum([0] + [n[0] if n[4] is not None else 0 for n in NORMS]).tolist()

        def repeat(eng, times, body):
            if times == 1:
                body(0)
                return
            with eng.Fori(0, times) as i:
                body(i)

        IN1 = [("copy", LATQ[:, t, :]) for t in range(3)] + [("copy", LATK[:, t, :]) for t in range(2)] \
            + [("rope", KR[:, :], TAB_P1, "rot_p")] \
            + [("rope", DQ[:, t, :], TAB_A1, "rot_a", DHD ** -0.5) for t in range(4)] \
            + [("rope", DK[:, t, :], TAB_A1, "rot_a") for t in range(4)]
        IN2 = [("rope", IQ[:, t, :], TAB_I2, "rot_i") for t in range(2)] + [("dvw",), ("misc", MISC[:, :])] \
            + [("dsaq", DQ2[:, t, :], TAB_A2, "rot_a") for t in range(4)] \
            + [("foxq", t) for t in range(4)] + [("foxk", t) for t in range(4)]
        DOTS_FROM, NDOTS = 12, 8 * (NB - 1)
        IN2_STEPS = DOTS_FROM + NDOTS // 3

        def rot_tiles(tiles):
            return [k for k, t in enumerate(tiles) if t[0] in ("rope", "dsaq", "misc")]

        ROT1, ROT2 = rot_tiles(IN1), rot_tiles(IN2)
        NRM2 = [k for k, t in enumerate(IN2) if t[0] in ("foxq", "foxk", "dsaq", "misc")]
        ALL_ROTATED = len(ROT1) + len(ROT2) - 1
        ROT_BASE = {"in1": 0, "uq": len(ROT1), "in2": len(ROT1) + 2}
        rot_src = {}

        MLA_SCALE = (NOPE + ROPE) ** -0.5

        def q_diff(c, i):
            return DQ[64 * (c % 2):64 * (c % 2) + 64, c // 2, i * P:(i + 1) * P]

        def k_diff(c, n):
            return DK[64 * (c % 2):64 * (c % 2) + 64, c // 2, 0:n]

        ATT = [
            dict(q=q_diff, k=k_diff, v=lambda kb, c: DV[:, kb, (c // 2) * P:(c // 2 + 1) * P], dv=P, P=P1, PT=PT1),
            dict(q=lambda h, i: QM[0:96, h, i * P:(i + 1) * P], k=lambda h, n: KM[h // 4][0:96, h % 4, 0:n],
                 v=lambda kb, h: VM[:, kb, h * 64:h * 64 + 64], dv=64, P=P1, PT=PT1),
            dict(q=lambda h, i: QF[0:66, h, i * P:(i + 1) * P], k=lambda h, n: KF[0:66, h, 0:n],
                 v=lambda kb, h: VF[:, kb, h * 64:h * 64 + 64], dv=64, P=P2, PT=PT2),
            dict(q=lambda h, i: DQ2[64 * (h % 2):64 * (h % 2) + 64, h // 2, i * P:(i + 1) * P],
                 k=lambda h, n: DK2[64 * (h % 2):64 * (h % 2) + 64, 0:n],
                 v=lambda kb, h: DVW[:, kb, 0:64], dv=64, P=P2, PT=PT2)]
        NU = 8 * NB
        XA = {"out1": 0, "down1": DT, "down2": 2 * DT, "out2": 3 * DT, "down3": 4 * DT}
        OUT_T = [(OD, OTH1, OTL1, 4, 0), (OM, OTH1, OTL1, 0, 1), (OF, OTH2, OTL2, 0, 2), (OS, OTH2, OTL2, 4, 3)]

        block = ctx.enter_context(nc.Block())

        @block.sync
        def _(sp):
            for t in range(4):
                sp.dma_start(X[:, 2 * t:2 * t + 2, :], xT[:, 2 * t:2 * t + 2, :]).then_inc(sem(f"x_loaded{t}"), 16)
            sp.dma_start(CO[:], cols_d).then_inc(sem("consts_loaded"), 16)
            sp.dma_start(SQC[:], squares_d).then_inc(sem("consts_loaded"), 16)
            for j in range(3):
                sp.dma_start(RAW[j][:], wst[j]).then_inc(sem(f"raw{j}"), 16)

            def more(i):
                for j in range(3):
                    sp.wait_ge(sem("lo_ready"), 3 * i + j + 1)
                    sp.dma_start(RAW[j][:], wst[3 * i + (j + 3)]).then_inc(sem(f"raw{j}"), 16)

            repeat(sp, (NCH - 3) // 3, more)
            for n in range(3 + (NCH - 3) // 3 * 3, NCH):
                sp.wait_ge(sem("lo_ready"), n - 2)
                sp.dma_start(RAW[n % 3][:], wst[n]).then_inc(sem(f"raw{n % 3}"), 16)
            for t in range(DT):
                sp.wait_ge(sem("x_added"), XA["down3"] + t + 1)
                sp.dma_start(out[:, t, :], X[:, t, :]).then_inc(sem("stored"), 16)
            sp.wait_ge(sem("stored"), 16 * DT)

        @block.gpsimd
        def _(pool):
            pool.dma_start(T[:, 0, :].bitcast(I32), pos1_d.partition_broadcast(P)).then_inc(sem("pos_loaded"), 16)
            pool.dma_start(SQ[:, 0, 0:256], lams_d.partition_broadcast(P)).then_inc(sem("lams_loaded"), 16)
            for j in range(2):
                pool.dma_start(ADA[j][:], ada[j]).then_inc(sem(f"ada{j}"), 16)

            def ada_more(i):
                for j in range(2):
                    pool.wait_ge(sem("ada_added"), 2 * i + j + 1)
                    pool.dma_start(ADA[j][:], ada[2 * i + (j + 2)]).then_inc(sem(f"ada{j}"), 16)

            repeat(pool, 7, ada_more)
            pool.wait_ge(sem("rotated"), 1)
            pool.wait_ge(sem("split_lo"), SPLIT_TB[3])
            for h in range(8):
                pool.tensor_copy(KM[h // 4][64:96, h % 4, :], KR[0:32, :]).then_inc(sem("k_shared"), 1)
            repeat(pool, 28, lambda i: ada_more(i + 7))
            pool.wait_ge(sem("x_added"), 2 * DT)
            pool.dma_start(T[:, 1, :].bitcast(I32), pos2_d.partition_broadcast(P)).then_inc(sem("pos_loaded"), 16)
            pool.wait_ge(sem("x_added"), 3 * DT)
            pool.memset(QF[64:66, :, :], 1.0).then_inc(sem("f_ones"), 1)
            pool.memset(KF[64:66, :, :], 1.0).then_inc(sem("f_ones"), 1)
            pool.wait_ge(sem("f_ones"), 2)
            pool_steps = [0]

            def link(ins):
                pool_steps[0] += 1
                ins.then_inc(sem("f_link"), 1)
                pool.wait_ge(sem("f_link"), pool_steps[0])

            pool.wait_ge(sem("f_act"), 3)
            link(pool.tensor_scalar(FW[0:8, 0, :], FW[0:8, 0, :], 0.0, None, ALU.min))
            link(pool.tensor_tensor(FW[0:8, 0, :], FW[0:8, 0, :], FW[0:8, 3, :], ALU.subtract))
            a, b, d = 0, 1, 1
            while d < S:
                pool.tensor_copy(FW[0:8, b, 0:d], FW[0:8, a, 0:d]).then_inc(sem("f_head"), 1)
                link(pool.tensor_tensor(FW[0:8, b, d:S], FW[0:8, a, d:S], FW[0:8, a, 0:S - d], ALU.add))
                a, b, d = b, a, 2 * d
            for k, s in ((2, 1.0), (3, -1.0)):
                pool.tensor_scalar(FW[0:8, k, :], FW[0:8, a, :], s, None, ALU.mult).then_inc(sem("f_scaled"), 1)
            pool.wait_ge(sem("f_scaled"), 2)
            pool.dma_start(QF[65:66, :, :], FW[0:8, 2, :]).then_inc(sem("f_rows"), 16)
            pool.dma_start(KF[64:65, :, :], FW[0:8, 3, :]).then_inc(sem("f_rows"), 16)

        @block.tensor
        def _(pe):
            mm = nc.tensor.matmul
            released = dict.fromkeys(("in_copied", "v_copied", "proj_copied", "branch_scaled", "x_added", "hid",
                                      "gate_copied"), 0)

            def all_released():
                for name, count in released.items():
                    if count:
                        pe.wait_ge(sem(name), count)

            def split_product(bank, w, blocks, tiles, moving, first=True, last=True, between={}):
                hi, lo = HI[w][:], LO[w][:]
                for b, t in zip(blocks, tiles):
                    if b in between:
                        between[b]()
                    a, z = hi[:, b * P:(b + 1) * P], lo[:, b * P:(b + 1) * P]
                    start, stop = first and b == blocks[0], last and b == blocks[-1]
                    mm(bank, a, moving[0][:, t, :], start=start, stop=False)
                    mm(bank, a, moving[1][:, t, :], start=False, stop=False)
                    ins = mm(bank, z, moving[0][:, t, :], start=False, stop=stop)
                return ins

            def chunk(n0, step, i):
                pe.wait_ge(sem("lo_ready"), step * i + (n0 + 1))
                return n0 % 3

            def used(ins):
                ins.then_inc(sem("chunk_used"), 1)

            def keep_warm(n):
                for _ in range(n):
                    mm(PS[:, 5, :], SQV["ident"], SQC[:, 0:4, :].rearrange("p n m -> p (n m)"), start=True,
                       stop=True)

            def norm(k):
                nt = NORMS[k][0]
                keep_warm(WARM[k][0])
                pe.wait_ge(sem("sum_added"), SAB[k + 1])
                if k:
                    pe.wait_ge(sem("stds"), k)
                for b in range(NB):
                    mm(PS[:, 7, 8 + b:9 + b], RB[:, 0, b * P:(b + 1) * P], SQV["ones"][:, 0:1],
                       start=b == 0, stop=False)
                pe.wait_ge(sem("squared"), NTB[k + 1])
                for b in range(NB):
                    ins = mm(PS[:, 7, 8 + b:9 + b], SQ[:, (nt - 1) % 2, b * P:(b + 1) * P],
                             SQV["ones"][:, 0:1], start=False, stop=b == NB - 1)
                ins.then_inc(sem("sq_summed"), 1)
                keep_warm(WARM[k][1])
                pe.wait_ge(sem("expanded"), k + 1)
                if k:
                    pe.wait_ge(sem("normed"), NTB[k])
                for b in range(NB):
                    tok = slice(b * P, (b + 1) * P)
                    ins = nc.tensor.transpose(PS[:, 6, tok], RB[:, 1, tok], SQV["ident"])
                ins.then_inc(sem("rstd"), 1)
                keep_warm(WARM[k][2])

            def behind(k, n0, banks):
                ws = [chunk(n0 + g, 0, 0) for g in range(2)]
                for t in range(DT):
                    pe.wait_ge(sem("split_lo"), SPLIT_TB[k] + t + 1)
                    for g in range(2):
                        ins = split_product(PS[:, banks[g], :], ws[g], (t,), (t,), (XH, XL), first=t == 0,
                                            last=t == DT - 1)
                        if t == DT - 1:
                            used(ins)

            def rotate(q, src, perm, bank):
                mm(PS[:, bank, :], SQV[perm], src, start=True, stop=True).then_inc(sem("rot_mm"), 1)

            def token_major(n0, nchunks, tiles_per, width, moving):
                all_released()
                for j in range(nchunks):
                    w = chunk(n0 + j, 0, 0)
                    for b in range(NB):
                        for r in range(tiles_per):
                            t = j * tiles_per + r
                            lw = 1024 // tiles_per
                            wh, wl = HI[w][:, r * lw:r * lw + width], LO[w][:, r * lw:r * lw + width]
                            xh, xl = (m[:, t, b * P:(b + 1) * P] for m in moving)
                            end = j == nchunks - 1 and r == tiles_per - 1
                            mm(PS[:, b, 0:width], xh, wh, start=t == 0, stop=False)
                            mm(PS[:, b, 0:width], xh, wl, start=False, stop=False)
                            ins = mm(PS[:, b, 0:width], xl, wh, start=False, stop=end)
                    used(ins)
                released["v_copied"] += NB

            def index_scores(u):
                i, h = 1 + u // 8, u % 8
                b = 32 * (h % 4)
                if u == 0:
                    pe.wait_ge(sem("ik_spread"), 4)
                    pe.wait_ge(sem("rotated"), len(ROT1) + 2 + 2)
                if u >= 2:
                    pe.wait_ge(sem("dots_read"), u - 1)
                mm(PS[:, 6 + u % 2, 0:P * (i + 1)], IQ[b:b + 32, h // 4, i * P:(i + 1) * P],
                   IK[b:b + 32, 0:P * (i + 1)], start=True, stop=True).then_inc(sem("dots"), 1)

            def project_in2():
                n0 = FIRST["in2"]
                all_released()
                e0 = released["in_copied"]

                def spread(k):
                    q = NRM2.index(k)
                    pe.wait_ge(sem("hexpanded"), q + 1)
                    if q >= 1:
                        pe.wait_ge(sem("hnormed"), q)
                    for b in range(NB):
                        tok = slice(b * P, (b + 1) * P)
                        ins = nc.tensor.transpose(PS[:, 4, tok], RB[:, q % 2, tok], SQV["ident"])
                    ins.then_inc(sem("hspread"), 1)

                def head_sums(k):
                    q = NRM2.index(k)
                    pe.wait_ge(sem("hsq"), q + 1)
                    if q >= 1:
                        pe.wait_ge(sem("hstd"), q)
                    for b in range(NB):
                        c = 8 * (q % 2) + 2 * b
                        ins = mm(PS[:, 3, c:c + 2], SQ[:, q % 2, b * P:(b + 1) * P], SQV["halves"][:, 0:P:64],
                                 start=True, stop=True)
                    ins.then_inc(sem("hsum"), 1)

                def rotation(k):
                    q = ROT_BASE["in2"] + ROT2.index(k)
                    if IN2[k][0] == "rope":
                        pe.wait_ge(sem("in_copied"), e0 + k + 1)
                    else:
                        pe.wait_ge(sem("hnormed"), NRM2.index(k) + 1)
                    if q > ROT_BASE["in2"]:
                        pe.wait_ge(sem("rot_read"), q)
                    if q == ROT_BASE["in2"] + 2:
                        pe.wait_ge(sem("values_copied"), 1)
                    rotate(q, IN2[k][1], "rot_m" if IN2[k][0] == "misc" else IN2[k][3], 5)

                def turn_values():
                    pe.wait_ge(sem("in_copied"), e0 + 3)
                    pe.wait_ge(sem("rot_read"), ROT_BASE["in2"] + 2)
                    for b in range(NB):
                        ins = nc.tensor.transpose(PS[:, 5, b * 72:(b + 1) * 72], VW[0:72, b * P:(b + 1) * P],
                                                  SQV["ident"][0:72, 0:72])
                    ins.then_inc(sem("values_turned"), 1)

                for j in range(IN2_STEPS):
                    amid = {}
                    if j == 5:
                        amid[5] = turn_values
                    if j - 3 in NRM2:
                        amid[1] = lambda: spread(j - 3)
                    if j - 2 in NRM2:
                        amid[2] = lambda: head_sums(j - 2)
                    turning = [k for k in ROT2 if rot_at(IN2, k) == j]
                    if turning:
                        amid[4] = lambda: rotation(turning[0])
                    if j >= DOTS_FROM:
                        for r, b in enumerate((0, 3, 6)):
                            amid[b] = lambda r=r: index_scores(3 * (j - DOTS_FROM) + r)
                    if j == 0:
                        behind(6, n0, (0, 1))
                    if j < 2:
                        continue
                    w = chunk(n0 + j, 0, 0)
                    if j == len(IN2):
                        pe.wait_ge(sem("in_copied"), e0 + len(IN2))
                        pe.wait_ge(sem("rot_read"), ROT_BASE["in2"] + len(ROT2))
                    if j >= len(IN2):
                        used(value_rows(j - len(IN2), w, amid))
                        continue
                    if j >= 3:
                        pe.wait_ge(sem("in_copied"), e0 + j - 2)
                    used(split_product(PS[:, j % 3, :], w, range(8), range(8), (XH, XL), between=amid))
                released["in_copied"] += len(IN2)
                released["v_copied"] += NB

            def value_rows(c, w, amid):
                for b in range(NB):
                    for r in range(2):
                        if 2 * b + r in amid:
                            amid[2 * b + r]()
                        t = 2 * c + r
                        wh, wl = HI[w][:, r * S:(r + 1) * S], LO[w][:, r * S:(r + 1) * S]
                        xh, xl = (m[:, t, b * P:(b + 1) * P] for m in (XH, XL))
                        bank = PS[:, FV_BANKS[b], :]
                        mm(bank, xh, wh, start=t == 0, stop=False)
                        mm(bank, xh, wl, start=False, stop=False)
                        ins = mm(bank, xl, wh, start=False, stop=t == DT - 1)
                return ins

            def branch2():
                all_released()
                for m in range(DT):
                    w = chunk(FIRST["branch2"] + m, 0, 0)
                    if m >= 2:
                        pe.wait_ge(sem("branch_scaled"), DT + m - 1)
                    split_product(PS[:, 2 * (m % 2), :], w, range(4), range(4), (OTH2, OTL2))
                    used(split_product(PS[:, 2 * (m % 2) + 1, :], w, range(4, 8), range(4, 8), (OTH2, OTL2)))
                released["branch_scaled"] += DT

            def ada_sum(g, bank):
                pe.wait_ge(sem("ada_added"), 8 * g + 8)
                if g:
                    pe.wait_ge(sem("mod"), g)
                for t in range(8):
                    ins = mm(PS[:, bank, t:t + 1], ACC[:, t * P:(t + 1) * P], SQV["ones"][:, 0:1],
                             start=True, stop=True)
                ins.then_inc(sem("ada_summed"), 1)

            def project_in1():
                n0 = FIRST["in1"]
                for j in range(len(IN1) + 2):
                    if j - 2 in ROT1:
                        q = ROT1.index(j - 2)
                        pe.wait_ge(sem("in_copied"), j - 1)
                        if q >= 2:
                            pe.wait_ge(sem("rot_read"), q - 1)
                        rotate(q, IN1[j - 2][1], IN1[j - 2][3], 4 + q % 2)
                    if j == 9:
                        ada_sum(0, 7)
                    if j == 0:
                        behind(0, n0, (0, 1))
                    elif 2 <= j < len(IN1):
                        w = chunk(n0 + j, 0, 0)
                        if j >= 4:
                            pe.wait_ge(sem("in_copied"), j - 3)
                        used(split_product(PS[:, j % 4, :], w, range(8), range(8), (XH, XL)))
                released["in_copied"] += len(IN1)

            def attention(a):
                at_ = ATT[a]
                n0 = FIRST["gates2"] + DT * (a - 2)

                def gate_blocks(u, part):
                    if a < 2 or u >= NU:
                        return
                    b = 2 * (u % 4) + part
                    if b == 0:
                        chunk(n0 + u // 4, 0, 0)
                        if u or a == 3:
                            pe.wait_ge(sem("gate_copied"), DT * (a - 2) + u // 4)
                    ins = split_product(PS[:, 7, :], (n0 + u // 4) % 3, (b,), (b,), (XH, XL),
                                        first=b == 0, last=b == 7)
                    if b == 7:
                        used(ins)

                for u in range(NU + 3):
                    if u < NU:
                        h, i = divmod(u, NB)
                        n = P * (i + 1)
                        if u >= 3:
                            pe.wait_ge(sem("probs"), NU * a + u - 2)
                        mm(PS[:, u % 3, 0:n], at_["q"](h, i), at_["k"](h, n), start=True, stop=False)
                        if a == 3:
                            ins = mm(PS[:, u % 3, 0:n], IDENT_B[:], MASK[i][:], start=False, stop=True)
                        else:
                            ins = mm(PS[:, u % 3, n - P:n], IDENT_B[:], CAUSAL_B[:], start=False, stop=True)
                        ins.then_inc(sem("scores"), 1)
                    gate_blocks(u, 0)
                    if 2 <= u < NU + 2:
                        v = u - 2
                        i = v % NB
                        pe.wait_ge(sem("probs"), NU * a + v + 1)
                        if v >= 2:
                            pe.wait_ge(sem("pt_copied"), NU * a + v - 1)
                        for kb in range(i + 1):
                            ins = nc.tensor.transpose(PS[:, 3 + v % 2, kb * P:(kb + 1) * P],
                                                      at_["P"][v % 3][:, kb * P:(kb + 1) * P], SQV["ident"])
                        ins.then_inc(sem("pt"), 1)
                    gate_blocks(u, 1)
                    if u >= 3:
                        v = u - 3
                        h, i = divmod(v, NB)
                        pe.wait_ge(sem("pt_copied"), NU * a + v + 1)
                        if v >= 2:
                            pe.wait_ge(sem("onorm"), NU * a + v - 1)
                        for kb in range(i + 1):
                            ins = mm(PS[:, 5 + v % 2, 0:at_["dv"]], at_["PT"][v % 2][:, kb * P:(kb + 1) * P],
                                     at_["v"](kb, h), start=kb == 0, stop=kb == i)
                        ins.then_inc(sem("pv"), 1)

            def turn(a):
                src, _, _, _, g = OUT_T[a]
                for f in range(4):
                    k = 4 * g + f
                    if k >= 2:
                        pe.wait_ge(sem("turned_lo"), k - 1)
                    for i in range(NB):
                        ins = nc.tensor.transpose(PS[:, 6 + k % 2, i * P:(i + 1) * P],
                                                  src[:, i, f * P:(f + 1) * P], SQV["ident"])
                    ins.then_inc(sem("turned"), 1)

            def merge(b, oh, ol):
                all_released()
                n0 = FIRST[f"merge{b + 1}"]

                def pair(i):
                    for j in range(2):
                        if not isinstance(i, int):
                            pe.wait_ge(sem("branch_scaled"), 2 * i + (DT * b + j - 1))
                        for g in range(2):
                            w = chunk(n0 + 3 * j + g, 6, i)
                            used(split_product(PS[:, 4 * j + g, :], w, range(8), range(8), (XH, XL)))
                        w = chunk(n0 + 3 * j + 2, 6, i)
                        split_product(PS[:, 4 * j + 2, :], w, range(4), range(4), (oh, ol))
                        used(split_product(PS[:, 4 * j + 3, :], w, range(4, 8), range(4, 8), (oh, ol)))

                pair(0)
                with pe.Fori(1, 4) as i:
                    pair(i)
                released["branch_scaled"] += DT

            def out_proj(b, mh, ml):
                all_released()
                n0 = FIRST[f"out{b + 1}"]
                for m in range(DT):
                    w = chunk(n0 + m, 0, 0)
                    if m >= 4:
                        pe.wait_ge(sem("x_added"), XA[f"out{b + 1}"] + m - 3)
                    used(split_product(PS[:, m % 4, :], w, range(8), range(8), (mh, ml)))
                released["x_added"] += DT

            def ffn(f, k):
                all_released()
                n0 = FIRST[f"up{f + 1}"]

                def three(i, tiles=3):
                    for j in range(tiles):
                        if not (isinstance(i, int) and i == 0):
                            pe.wait_ge(sem("hid"), 3 * i + (FT * f + j - 2))
                        if isinstance(i, int) and i == 0 and j == 0:
                            behind(k, n0, (0, 1))
                            continue
                        for g in range(2):
                            w = chunk(n0 + 2 * j + g, 6, i)
                            if f == 0 and j == 2 and g == 1 and tiles == 3:
                                ada_sum_loop(i)
                            used(split_product(PS[:, 2 * j + g, :], w, range(8), range(8), (XH, XL)))

                def ada_sum_loop(i):
                    pe.wait_ge(sem("ada_added"), 8 * i + 24)
                    pe.wait_ge(sem("mod"), i + 2)
                    for t in range(8):
                        ins = mm(PS[:, 7, t:t + 1], ACC[:, t * P:(t + 1) * P], SQV["ones"][:, 0:1],
                                 start=True, stop=True)
                    ins.then_inc(sem("ada_summed"), 1)

                three(0)
                with pe.Fori(1, 7) as i:
                    three(i)
                three(7, tiles=1)
                released["hid"] += FT
                all_released()
                n0 = FIRST[f"down{f + 1}"]
                pe.wait_ge(sem("hid_lo"), FT * (f + 1))

                def two(i):
                    for j in range(2):
                        if not (isinstance(i, int) and i == 0):
                            pe.wait_ge(sem("x_added"), 2 * i + (XA[f"down{f + 1}"] + j - 1))
                        for g, blocks in enumerate(LAST_DOWN):
                            w = chunk(n0 + 3 * j + g, 6, i)
                            used(split_product(PS[:, j, :], w, range(blocks), range(8 * g, 8 * g + blocks),
                                               (HIDH, HIDL), first=g == 0, last=g == 2))

                two(0)
                with pe.Fori(1, 4) as i:
                    two(i)
                released["x_added"] += DT

            pe.wait_ge(sem("consts_loaded"), 32)
            norm(0)
            project_in1()
            token_major(FIRST["dv1"], 4, 2, 512, (XH, XL))
            ada_sum(1, 7)
            all_released()
            pe.wait_ge(sem("rotated"), len(ROT1))
            attention(0)
            pe.wait_ge(sem("onorm"), NU)
            norm(1)
            norm(2)
            pe.wait_ge(sem("split_lo"), SPLIT_TB[3])
            for j in range(3):
                w = chunk(FIRST["uq"] + j, 0, 0)
                for r in range(2):
                    m = 2 * j + r
                    ins = split_product(PS[:, m, :], w, range(3 * r, 3 * r + 3), range(3), (LQH, LQL))
                used(ins)
            w = chunk(FIRST["uk"], 0, 0)
            for m in range(4):
                pe.wait_ge(sem("proj_copied"), m + 1)
                ins = split_product(PS[:, m, :], w, range(2 * m, 2 * m + 2), range(2), (LKH, LKL))
            used(ins)
            for r in range(2):
                pe.wait_ge(sem("proj_copied"), 5 + r)
                rotate(ROT_BASE["uq"] + r, Y[:, r, :], "rot_p", 6 + r)
            released["proj_copied"] += 10
            token_major(FIRST["uv"], 1, 2, 512, (LKH, LKL))
            all_released()
            pe.wait_ge(sem("q_rotated"), 2)
            pe.wait_ge(sem("k_shared"), 8)
            attention(1)
            pe.wait_ge(sem("diff_normed"), 1)
            pe.wait_ge(sem("onorm"), 2 * NU)
            turn(0)
            turn(1)
            pe.wait_ge(sem("turned_lo"), 8)
            merge(0, OTH1, OTL1)
            pe.wait_ge(sem("merged_lo"), 8)
            out_proj(0, MH1, ML1)
            norm(3)
            ffn(0, 3)
            norm(4)
            norm(5)
            ffn(1, 5)
            norm(6)
            project_in2()
            all_released()
            pe.wait_ge(sem("hstd"), len(NRM2))
            pe.wait_ge(sem("hnormed"), len(NRM2))
            pe.wait_ge(sem("dots_read"), NDOTS)
            pe.wait_ge(sem("f_rows"), 32)
            attention(2)
            pe.wait_ge(sem("rotated"), ALL_ROTATED)
            pe.wait_ge(sem("selected"), 4)
            attention(3)
            pe.wait_ge(sem("onorm"), 4 * NU)
            turn(2)
            turn(3)
            pe.wait_ge(sem("turned_lo"), 16)
            branch2()
            pe.wait_ge(sem("merged_lo"), 16)
            out_proj(1, MH2, ML2)
            norm(7)
            ffn(2, 7)

        @block.scalar
        def _(act):
            A = nc.scalar.activation

            def split_hi(n0, step=0, i=0):
                n0 += 2
                if isinstance(i, int):
                    n0, step, i = n0 + step * i, 0, 0
                    if n0 >= NCH:
                        return
                if step == 0:
                    act.wait_ge(sem(f"raw{n0 % 3}"), 16 * (n0 // 3 + 1))
                    if n0 >= 3:
                        act.wait_ge(sem("chunk_used"), n0 - 2)
                else:
                    act.wait_ge(sem(f"raw{n0 % 3}"), (16 * step // 3) * i + 16 * (n0 // 3 + 1))
                    act.wait_ge(sem("chunk_used"), step * i + (n0 - 2))
                A(HI[n0 % 3][:], RAW[n0 % 3][:], ACT.Copy).then_inc(sem("hi_ready"), 1)

            def square(k, t, i=0):
                src = NORMS[k][1]
                if isinstance(i, int):
                    t, i = t + 2 * i, 0
                    if t >= 2:
                        act.wait_ge(sem("sum_added"), SAB[k] + t - 1)
                    elif k:
                        act.wait_ge(sem("sq_summed"), k)
                else:
                    act.wait_ge(sem("sum_added"), 2 * i + (SAB[k] + t - 1))
                A(SQ[:, t % 2:t % 2 + 1, :], src[:, bass.ds(2 * i + t, 1), :], ACT.Square).then_inc(sem("squared"), 1)

            def norm(k, first=0):
                nt, src, width, g, oh, ol = NORMS[k]
                for t in range(first, nt):
                    if k == 0 and t % 2 == 0:
                        act.wait_ge(sem(f"x_loaded{t // 2}"), 16)
                    if k == 5:
                        act.wait_ge(sem("normed"), NTB[5] - DT + t + 1)
                    square(k, t)
                act.wait_ge(sem("sq_summed"), k + 1)
                A(NSTD, PS[:, 7, 8:12], ACT.Sqrt, bias=EPSC, scale=1.0 / width).then_inc(sem("stds"), 1)
                if oh is None:
                    return
                for t in range(nt):
                    act.wait_ge(sem("normed"), NTB[k] + t + 1)
                    if isinstance(g, str):
                        A(oh[:, t, :], Y[:, t % 2, :], ACT.Copy).then_inc(sem("split_hi"), 1)
                    else:
                        shift = 3 * g * DT + t
                        A(oh[:, t, :], Y[:, t % 2, :], ACT.Identity, bias=MOD[:, shift:shift + 1])\
                            .then_inc(sem("split_hi"), 1)

            def table(k, tab):
                act.wait_ge(sem("angle"), k + 1)
                A(tab[:, 1, :], Y[:, 0, :], ACT.Sin).then_inc(sem("sin"), 1)
                A(Y[:, 1, :], Y[:, 0, :], ACT.Abs).then_inc(sem("absolute"), 1)
                act.wait_ge(sem("absolute"), k + 1)
                A(tab[:, 0, :], Y[:, 1, :], ACT.Sin, bias=PIH, scale=-1.0).then_inc(sem("table"), 1)

            def token_copies(n0, nchunks, dest, width):
                for j in range(nchunks):
                    split_hi(n0 + j)
                act.wait_ge(sem("chunk_used"), n0 + nchunks)
                for b in range(NB):
                    A(dest[:, b, :], PS[:, b, 0:width], ACT.Copy).then_inc(sem("v_copied"), 1)

            def project_in1():
                n0 = FIRST["in1"]
                for j, kind in enumerate(IN1):
                    split_hi(n0 + j)
                    act.wait_ge(sem("chunk_used"), n0 + j + 1)
                    A(kind[1], PS[:, j % 4, :], ACT.Copy, scale=kind[4] if len(kind) > 4 else 1.0)\
                        .then_inc(sem("in_copied"), 1)

            def project_in2():
                n0 = FIRST["in2"]
                for j in range(IN2_STEPS):
                    split_hi(n0 + j)
                    if j - 2 in NRM2:
                        q = NRM2.index(j - 2)
                        act.wait_ge(sem("hsum"), q + 1)
                        if q >= 2:
                            act.wait_ge(sem("hexpanded"), q - 1)
                        A(HSTD[q % 2], PS[:, 3, 8 * (q % 2):8 * (q % 2) + 8], ACT.Sqrt, bias=EPSC, scale=1.0 / 64)\
                            .then_inc(sem("hstd"), 1)
                    if j == FORGET_AT:
                        act.wait_ge(sem("f_z"), 1)
                        A(FW[0:8, 1, :], FW[0:8, 0, :], ACT.Abs).then_inc(sem("f_act"), 1)
                        act.wait_ge(sem("f_act"), 1)
                        A(FW[0:8, 2, :], FW[0:8, 1, :], ACT.Exp, scale=-1.0).then_inc(sem("f_act"), 1)
                        act.wait_ge(sem("f_act"), 2)
                        A(FW[0:8, 3, :], FW[0:8, 2, :], ACT.Ln, bias=1.0).then_inc(sem("f_act"), 1)
                    if j >= DOTS_FROM:
                        for u in range(3 * (j - DOTS_FROM), 3 * (j - DOTS_FROM) + 3):
                            n = P * (2 + u // 8)
                            act.wait_ge(sem("dots"), u + 1)
                            if u >= 2:
                                act.wait_ge(sem("scored"), u - 1)
                            A(Y[:, u % 2, 0:n], PS[:, 6 + u % 2, 0:n], ACT.Relu, scale=32 ** -0.5)\
                                .then_inc(sem("dots_read"), 1)
                    act.wait_ge(sem("chunk_used"), n0 + j + 1)
                    if j in NRM2:
                        q = NRM2.index(j)
                        if q >= 2:
                            act.wait_ge(sem("hsum"), q - 1)
                        A(SQ[:, q % 2, :], PS[:, j % 3, :], ACT.Square).then_inc(sem("hsq"), 1)
                        if q >= 5:
                            act.wait_ge(sem("hnormed"), q - 3)
                        dst = MISC[:, :] if IN2[j][0] == "misc" else R[:, j % 4, :]
                        A(dst, PS[:, j % 3, :], ACT.Copy).then_inc(sem("in_copied"), 1)
                    elif j < len(IN2):
                        dst = VW[:, :] if IN2[j][0] == "dvw" else IN2[j][1]
                        A(dst, PS[:, j % 3, :], ACT.Copy).then_inc(sem("in_copied"), 1)
                    if j == 5:
                        act.wait_ge(sem("values_turned"), 1)
                        A(DVW[:].rearrange("p b n -> p (b n)"), PS[:, 5, 0:72 * NB], ACT.Copy)\
                            .then_inc(sem("values_copied"), 1)
                for b in range(NB):
                    A(VF[:, b, :], PS[:, FV_BANKS[b], :], ACT.Copy).then_inc(sem("v_copied"), 1)

            def branch2():
                for m in range(DT):
                    split_hi(FIRST["branch2"] + m)
                    for g in range(2):
                        A(GATE2[g][m], GATE2[g][m], ACT.Sigmoid).then_inc(sem("gated"), 1)
                    if m == 0:
                        continue
                    act.wait_ge(sem("merged"), DT + m)
                    A(MH2[:, m - 1, :], Y[:, (m - 1) % 2, :], ACT.Copy).then_inc(sem("merged_hi"), 1)
                act.wait_ge(sem("merged"), 2 * DT)
                A(MH2[:, DT - 1, :], Y[:, (DT - 1) % 2, :], ACT.Copy).then_inc(sem("merged_hi"), 1)

            def attention(a):
                at_ = ATT[a]
                n0 = FIRST["gates2"] + DT * (a - 2)
                for u in range(NU + 2):
                    if a >= 2 and u % 4 == 0:
                        if u:
                            m = u // 4 - 1
                            act.wait_ge(sem("chunk_used"), n0 + m + 1)
                            A(GATE2[a - 2][m], PS[:, 7, :], ACT.Copy).then_inc(sem("gate_copied"), 1)
                    if a >= 2 and u % 4 == 1 and u < NU:
                        split_hi(n0 + u // 4)
                    if u >= 2:
                        v = u - 2
                        n = P * (v % NB + 1)
                        act.wait_ge(sem("pt"), NU * a + v + 1)
                        if v >= 2:
                            act.wait_ge(sem("pv"), NU * a + v - 1)
                        A(at_["PT"][v % 2][:, 0:n], PS[:, 3 + v % 2, 0:n], ACT.Copy).then_inc(sem("pt_copied"), 1)
                    if u < NU:
                        n = P * (u % NB + 1)
                        act.wait_ge(sem("smax"), NU * a + u + 1)
                        if u >= 4:
                            act.wait_ge(sem("onorm"), NU * a + u - 3)
                        A(at_["P"][u % 3][:, 0:n], PS[:, u % 3, 0:n], ACT.Exp, bias=NMX[:, u % 4:u % 4 + 1],
                          accum_out=RSU[:, u % 4:u % 4 + 1]).then_inc(sem("probs"), 1)

            def turn(a):
                src, oh, ol, f0, g = OUT_T[a]
                for f in range(4):
                    k = 4 * g + f
                    act.wait_ge(sem("turned"), k + 1)
                    A(oh[:, f0 + f, :], PS[:, 6 + k % 2, :], ACT.Copy,
                      scale=GM[:, 0:1] if a == 0 else 1.0).then_inc(sem("turned_hi"), 1)

            def merge(b):
                n0 = FIRST[f"merge{b + 1}"]

                def pair(i):
                    for j in range(2):
                        for g in range(2):
                            split_hi(n0 + 3 * j + g, 6, i)
                            act.wait_ge(sem("chunk_used"), 6 * i + (n0 + 3 * j + g + 1))
                            if b == 0:
                                bias = CO[:, bass.ds(COLS["b_gate"][0] + DT * g + j + 2 * i, 1)]
                            else:
                                bias = 0.0
                            if not (isinstance(i, int) and 8 * b + 2 * i + j == 0):
                                act.wait_ge(sem("merged"), 2 * i + (DT * b + j))
                            A(T[:, g, :], PS[:, 4 * j + g, :], ACT.Sigmoid, bias=bias).then_inc(sem("gate"), 1)
                        split_hi(n0 + 3 * j + 2, 6, i)
                        act.wait_ge(sem("merged"), 2 * i + (8 * b + j + 1))
                        A((MH1, MH2)[b][:, bass.ds(2 * i + j, 1), :], Y[:, j:j + 1, :], ACT.Copy)\
                            .then_inc(sem("merged_hi"), 1)

                pair(0)
                with act.Fori(1, 4) as i:
                    pair(i)

            def out_proj(b):
                k = (3, 7)[b]
                for m in range(DT):
                    split_hi(FIRST[f"out{b + 1}"] + m)
                    if m:
                        act.wait_ge(sem("x_added"), XA[f"out{b + 1}"] + m)
                        square(k, m - 1)
                act.wait_ge(sem("x_added"), XA[f"out{b + 1}"] + DT)
                norm(k, first=DT - 1)

            def ffn(f):
                n0 = FIRST[f"up{f + 1}"]

                def three(i, tiles=3):
                    for j in range(tiles):
                        split_hi(n0 + 2 * j, 6, i)
                        act.wait_ge(sem("chunk_used"), 6 * i + (n0 + 2 * j + 1))
                        if not (isinstance(i, int) and i == 0 and j == 0):
                            act.wait_ge(sem("hid"), 3 * i + (FT * f + j))
                        A(T[:, 0, :], PS[:, 2 * j, :], ACT.Silu).then_inc(sem("silu"), 1)
                        split_hi(n0 + 2 * j + 1, 6, i)
                        act.wait_ge(sem("hid"), 3 * i + (FT * f + j + 1))
                        A(HIDH[:, bass.ds(3 * i + j, 1), :], Y[:, 0:1, :], ACT.Copy).then_inc(sem("hid_hi"), 1)

                three(0)
                with act.Fori(1, 7) as i:
                    three(i)
                three(7, tiles=1)
                n0 = FIRST[f"down{f + 1}"]

                def two(i):
                    for j in range(2):
                        for g in range(3):
                            split_hi(n0 + 3 * j + g, 6, i)
                        if f < 2 and not (isinstance(i, int) and i == 0 and j == 0):
                            act.wait_ge(sem("x_added"), 2 * i + (XA[f"down{f + 1}"] + j))
                            square((4, 6)[f], j - 1, i)

                two(0)
                if f == 1:
                    table(2, TAB_A2)
                    table(3, TAB_I2)
                with act.Fori(1, 3) as i:
                    two(i)
                two(3)
                if f < 2:
                    act.wait_ge(sem("x_added"), XA[f"down{f + 1}"] + DT)
                    norm((4, 6)[f], first=DT - 1)

            split_hi(-2)
            split_hi(-1)
            act.wait_ge(sem("eps_set"), 1)
            act.wait_ge(sem("lams_used"), 1)
            norm(0)
            act.wait_ge(sem("consts_loaded"), 32)
            A(CND, col("cond", 0, DT), ACT.Silu).then_inc(sem("cond_ready"), 1)
            table(0, TAB_A1)
            table(1, TAB_P1)
            project_in1()
            token_copies(FIRST["dv1"], 4, DV, 512)
            A(LAM[:, 2:4], LAM[:, 0:2], ACT.Exp).then_inc(sem("lam_exp"), 1)
            attention(0)
            act.wait_ge(sem("onorm"), NU)
            for k in range(16):
                A(T[:, 0, 0:P], OD[:, k // 4, (k % 4) * P:(k % 4 + 1) * P], ACT.Square,
                  accum_out=SSD[:, k:k + 1]).then_inc(sem("diff_ss"), 1)
                act.wait_ge(sem("diff_ss"), k + 1)
            A(RSD, SSD, ACT.Sqrt, bias=EPSC, scale=1.0 / P).then_inc(sem("diff_std"), 1)
            norm(1)
            norm(2)
            for j in range(3):
                split_hi(FIRST["uq"] + j)
                act.wait_ge(sem("chunk_used"), FIRST["uq"] + j + 1)
                for r in range(2):
                    m = 2 * j + r
                    if m < 4:
                        A(QM[0:64, 2 * m, :], PS[0:64, m, :], ACT.Copy, scale=MLA_SCALE).then_inc(sem("half_copied"), 1)
                        A(QM[0:64, 2 * m + 1, :], PS[64:128, m, :], ACT.Copy, scale=MLA_SCALE).then_inc(sem("proj_copied"), 1)
                    else:
                        A(Y[:, m - 4, :], PS[:, m, :], ACT.Copy, scale=MLA_SCALE).then_inc(sem("proj_copied"), 1)
            split_hi(FIRST["uk"])
            act.wait_ge(sem("chunk_used"), FIRST["uk"] + 1)
            for m in range(4):
                for r in range(2):
                    h = 2 * m + r
                    A(KM[h // 4][0:64, h % 4, :], PS[64 * r:64 * r + 64, m, :], ACT.Copy)\
                        .then_inc(sem("proj_copied" if r else "half_copied"), 1)
            token_copies(FIRST["uv"], 1, VM, 512)
            attention(1)
            act.wait_ge(sem("g_sub_scaled"), 1)
            turn(0)
            turn(1)
            merge(0)
            out_proj(0)
            ffn(0)
            norm(5)
            ffn(1)
            project_in2()
            attention(2)
            attention(3)
            turn(2)
            turn(3)
            branch2()
            out_proj(1)
            ffn(2)

        @block.vector
        def _(v):
            V = nc.vector

            def split_lo(n0, step=0, i=0):
                n0 += 2
                if isinstance(i, int):
                    n0, step, i = n0 + step * i, 0, 0
                    if n0 >= NCH:
                        return
                v.wait_ge(sem("hi_ready"), n0 + 1 if step == 0 else step * i + (n0 + 1))
                V.tensor_tensor(LO[n0 % 3][:], RAW[n0 % 3][:], HI[n0 % 3][:].bitcast(F32), ALU.subtract)\
                    .then_inc(sem("lo_ready"), 1)

            def clear_sum(k):
                if k:
                    v.wait_ge(sem("sq_summed"), k)
                link(V.memset(RB[:, 0, :], 0.0))

            def add_square(k, t, i=0):
                if isinstance(i, int):
                    t, i = t + 2 * i, 0
                    if t:
                        v.wait_ge(sem("sum_added"), SAB[k] + t)
                else:
                    v.wait_ge(sem("sum_added"), 2 * i + (SAB[k] + t))
                v.wait_ge(sem("squared"), 2 * i + (NTB[k] + t + 1))
                V.tensor_tensor(RB[:, 0, :], RB[:, 0, :], SQ[:, t % 2, :], ALU.add).then_inc(sem("sum_added"), 1)

            def norm(k):
                nt, src, width, g, oh, ol = NORMS[k]
                v.wait_ge(sem("stds"), k + 1)
                link(V.reciprocal(NR, NSTD))
                if k:
                    v.wait_ge(sem("rstd"), k)
                V.tensor_copy(RB[:, 1, :].rearrange("p (b n) -> p b n", b=NB),
                              NR.unsqueeze(2).to_broadcast([P, NB, P])).then_inc(sem("expanded"), 1)
                v.wait_ge(sem("rstd"), k + 1)
                roots = PS[:, 6, :]
                if k == 4:
                    clear_sum(5)
                for t in range(nt):
                    s = SPLIT_TB[k] + t
                    if oh is None:
                        V.scalar_tensor_tensor(out=src[:, t, :], in0=src[:, t, :], scalar=col(g, t), in1=roots,
                                               op0=ALU.mult, op1=ALU.mult).then_inc(sem("normed"), 1)
                        if t:
                            add_square(5, t - 1)
                        continue
                    if t >= 2:
                        v.wait_ge(sem("split_hi"), s - 1)
                        v.wait_ge(sem("split_lo"), s - 1)
                    if isinstance(g, str):
                        V.scalar_tensor_tensor(out=Y[:, t % 2, :], in0=src[:, t, :], scalar=col(g, t),
                                               in1=roots, op0=ALU.mult, op1=ALU.mult)\
                            .then_inc(sem("normed"), 1)
                    else:
                        gain = (3 * g + 1) * DT + t
                        V.scalar_tensor_tensor(out=Y[:, t % 2, :], in0=src[:, t, :], scalar=MOD[:, gain:gain + 1],
                                               in1=roots, op0=ALU.mult, op1=ALU.mult)\
                            .then_inc(sem("normed"), 1)
                    if t >= 1:
                        lo(k, t - 1)
                if oh is not None:
                    lo(k, nt - 1)
                    v.wait_ge(sem("split_lo"), SPLIT_TB[k + 1])
                else:
                    v.wait_ge(sem("normed"), NTB[k + 1])

            def lo(k, t):
                g, oh, ol = NORMS[k][3:]
                v.wait_ge(sem("split_hi"), SPLIT_TB[k] + t + 1)
                if not isinstance(g, str):
                    shift = 3 * g * DT + t
                    V.scalar_tensor_tensor(out=ol[:, t, :], in0=Y[:, t % 2, :], scalar=MOD[:, shift:shift + 1],
                                           in1=oh[:, t, :].bitcast(F32), op0=ALU.add, op1=ALU.subtract)\
                        .then_inc(sem("split_lo"), 1)
                    return
                V.tensor_tensor(ol[:, t, :], Y[:, t % 2, :], oh[:, t, :].bitcast(F32), ALU.subtract)\
                    .then_inc(sem("split_lo"), 1)

            steps = [0]

            def link(ins):
                steps[0] += 1
                ins.then_inc(sem("dve_link"), 1)
                v.wait_ge(sem("dve_link"), steps[0])

            two_pi = 2 * np.pi
            C1 = 6.28125
            C2 = float(np.round((two_pi - C1) * 2 ** 17) / 2 ** 17)
            C3 = float(np.float32(two_pi - C1 - C2))
            MAGIC = float(1.5 * 2 ** 23)

            def angles(k, pos, freq):
                if k % 2:
                    v.wait_ge(sem("table"), k)
                link(V.tensor_scalar(Y[:, 1, :], pos, col(freq), None, ALU.mult))
                link(V.tensor_scalar(RB[:, 1, :], Y[:, 1, :], 1.0 / two_pi, MAGIC, ALU.mult, ALU.add))
                link(V.tensor_scalar(RB[:, 1, :], RB[:, 1, :], -MAGIC, None, ALU.add))
                for c in (C1, C2, C3):
                    link(V.scalar_tensor_tensor(out=Y[:, 1, :], in0=RB[:, 1, :], scalar=-c, in1=Y[:, 1, :],
                                                op0=ALU.mult, op1=ALU.add))
                V.tensor_scalar(Y[:, 0, :], Y[:, 1, :], 3.1415925, -3.1415925, ALU.min, ALU.max)\
                    .then_inc(sem("angle"), 1)

            def ada_piece(a0, step=0, i=0):
                kt = a0 % 8
                j = a0 % 2
                if step:
                    v.wait_ge(sem(f"ada{j}"), (8 * step) * i + 16 * (a0 // 2 + 1))
                    v.wait_ge(sem("ada_added"), step * i + a0)
                    if kt == 0:
                        v.wait_ge(sem("ada_summed"), i + a0 // 8)
                else:
                    v.wait_ge(sem(f"ada{j}"), 16 * (a0 // 2 + 1))
                    if a0:
                        v.wait_ge(sem("ada_added"), a0)
                    if kt == 0 and a0:
                        v.wait_ge(sem("ada_summed"), a0 // 8)
                if kt == 0:
                    V.tensor_scalar(ACC[:], ADA[j][:], CND[:, 0:1], None, ALU.mult).then_inc(sem("ada_added"), 1)
                else:
                    V.scalar_tensor_tensor(out=ACC[:], in0=ADA[j][:], scalar=CND[:, kt:kt + 1], in1=ACC[:],
                                           op0=ALU.mult, op1=ALU.add).then_inc(sem("ada_added"), 1)

            def ada_take(g, loop=False):
                if loop:
                    v.wait_ge(sem("ada_summed"), g + 1)
                    V.tensor_tensor(MOD[:, bass.ds(8 * g, 8)], PS[:, 7, 0:8],
                                    CO[:, bass.ds(8 * g + COLS["ada_b"][0], 8)], ALU.add).then_inc(sem("mod"), 1)
                else:
                    v.wait_ge(sem("ada_summed"), g + 1)
                    V.tensor_tensor(MOD[:, 8 * g:8 * g + 8], PS[:, 7, 0:8], col("ada_b", 8 * g, 8), ALU.add)\
                        .then_inc(sem("mod"), 1)

            def rope(q, bank, dst, tab, rows=slice(0, P), signal="rotated"):
                v.wait_ge(sem("rot_mm"), q + 1)
                ins = V.tensor_tensor(T[rows, 0, :], PS[rows, bank, :], tab[rows, 1, :], ALU.mult)
                ins.then_inc(sem("rot_read"), 1)
                link(V.tensor_tensor(T[rows, 1, :], dst[rows, :], tab[rows, 0, :], ALU.mult))
                return T

            def project_in1():
                n0 = FIRST["in1"]
                for j in range(len(IN1) + 2):
                    if j < len(IN1):
                        split_lo(n0 + j)
                    if j - 2 in ROT1:
                        q = ROT1.index(j - 2)
                        dst = IN1[j - 2][1]
                        rope(q, 4 + q % 2, dst, IN1[j - 2][2])
                        v.wait_ge(sem("rot_read"), q + 1)
                        V.tensor_tensor(dst, T[:, 0, :], T[:, 1, :], ALU.add).then_inc(sem("rotated"), 1)
                        v.wait_ge(sem("rotated"), q + 1)
                    ada_piece(j)
                    if j == 9:
                        ada_take(0)

            def head_norm(k):
                t, q = IN2[k], NRM2.index(k)
                roots = PS[:, 4, :]
                v.wait_ge(sem("hspread"), q + 1)
                v.wait_ge(sem("in_copied"), len(IN1) + k + 1)
                if t[0] in ("foxq", "foxk"):
                    dst = QF if t[0] == "foxq" else KF
                    g = FOXQ_G if t[0] == "foxq" else col("fox_g", 1)
                    for r in range(2):
                        rows = slice(64 * r, 64 * r + 64)
                        ins = V.scalar_tensor_tensor(
                            out=dst[0:64, 2 * t[1] + r, :], in0=R[rows, k % 4, :], scalar=g[rows, :],
                            in1=roots[rows, :], op0=ALU.mult, op1=ALU.mult)
                elif t[0] == "dsaq":
                    ins = V.scalar_tensor_tensor(out=t[1], in0=R[:, k % 4, :], scalar=DSAQ_G,
                                                 in1=roots, op0=ALU.mult, op1=ALU.mult)
                else:
                    ins = V.scalar_tensor_tensor(out=MISC[0:64, :], in0=MISC[0:64, :],
                                                 scalar=col("dsa_g", 1)[0:64, :], in1=roots[0:64, :],
                                                 op0=ALU.mult, op1=ALU.mult)
                ins.then_inc(sem("hnormed"), 1)

            def rotate_misc(q, bank):
                v.wait_ge(sem("rot_mm"), q + 1)
                lo_, hi_ = slice(0, 64), slice(64, 96)
                link(V.tensor_tensor(T[lo_, 0, :], PS[lo_, bank, :], TAB_A2[lo_, 1, :], ALU.mult))
                V.tensor_tensor(T[hi_, 0, :], PS[hi_, bank, :], TAB_I2[hi_, 1, :], ALU.mult)\
                    .then_inc(sem("rot_read"), 1)
                link(V.tensor_tensor(T[lo_, 1, :], MISC[lo_, :], TAB_A2[lo_, 0, :], ALU.mult))
                link(V.tensor_tensor(T[hi_, 1, :], MISC[hi_, :], TAB_I2[hi_, 0, :], ALU.mult))
                v.wait_ge(sem("rot_read"), q + 1)
                for r in range(2):
                    V.tensor_tensor(DK2[64 * r:64 * r + 64, :], T[lo_, 0, :], T[lo_, 1, :], ALU.add)\
                        .then_inc(sem("dk_spread"), 1)
                for r in range(4):
                    V.tensor_tensor(IK[32 * r:32 * r + 32, :], T[hi_, 0, :], T[hi_, 1, :], ALU.add)\
                        .then_inc(sem("ik_spread"), 1)
                V.tensor_scalar(FW[0:8, 0, :], MISC[96:104, :], col("f_bias")[96:104, :], None, ALU.add)\
                    .then_inc(sem("f_z"), 1)
                v.wait_ge(sem("dk_spread"), 2)
                v.wait_ge(sem("ik_spread"), 4)

            def index_sum(u):
                i, h = 1 + u // 8, u % 8
                n = P * (i + 1)
                v.wait_ge(sem("dots_read"), u + 1)
                if h == 0:
                    V.tensor_scalar(BIAS[i][:], Y[:, u % 2, 0:n], IW[:, i, 0:1], None, ALU.mult)\
                        .then_inc(sem("scored"), 1)
                else:
                    v.wait_ge(sem("scored"), u)
                    V.scalar_tensor_tensor(out=BIAS[i][:], in0=Y[:, u % 2, 0:n], scalar=IW[:, i, h:h + 1],
                                           in1=BIAS[i][:], op0=ALU.mult, op1=ALU.add).then_inc(sem("scored"), 1)

            def project_in2():
                for j in range(IN2_STEPS):
                    split_lo(FIRST["in2"] + j)
                    if j - 2 in NRM2:
                        q = NRM2.index(j - 2)
                        v.wait_ge(sem("hstd"), q + 1)
                        if q >= 2:
                            v.wait_ge(sem("hspread"), q - 1)
                        link(V.reciprocal(HR[q % 2], HSTD[q % 2]))
                        V.tensor_copy(RB[:, q % 2, :].rearrange("p (b n) -> p b n", b=2 * NB),
                                      HR[q % 2].unsqueeze(2).to_broadcast([P, 2 * NB, 64]))\
                            .then_inc(sem("hexpanded"), 1)
                    if j - 3 in NRM2:
                        head_norm(j - 3)
                    for r, k in enumerate(ROT2):
                        if rot_at(IN2, k) == j:
                            q = ROT_BASE["in2"] + r
                            if IN2[k][0] == "misc":
                                rotate_misc(q, 5)
                                continue
                            dst = IN2[k][1]
                            rope(q, 5, dst, IN2[k][2])
                            v.wait_ge(sem("rot_read"), q + 1)
                            V.tensor_tensor(dst, T[:, 0, :], T[:, 1, :], ALU.add).then_inc(sem("rotated"), 1)
                            v.wait_ge(sem("rotated"), len(ROT1) + r + (0 if r > ROT2.index(3) else 1))
                    if j == 7:
                        v.wait_ge(sem("values_copied"), 1)
                        link(V.tensor_scalar(IW[:], DVW[:, :, 64:72], 8 ** -0.5, None, ALU.mult))
                    if j >= DOTS_FROM:
                        for r in range(3):
                            index_sum(3 * (j - DOTS_FROM) + r)

            def branch2():
                for m in range(DT):
                    split_lo(FIRST["branch2"] + m)
                    v.wait_ge(sem("chunk_used"), FIRST["branch2"] + m + 1)
                    v.wait_ge(sem("gated"), 2 * m + 2)
                    for g in range(2):
                        V.tensor_tensor(T[:, g, :], GATE2[g][m], PS[:, 2 * (m % 2) + g, :], ALU.mult)\
                            .then_inc(sem("branch_scaled" if g else "first_scaled"), 1)
                    v.wait_ge(sem("branch_scaled"), DT + m + 1)
                    v.wait_ge(sem("first_scaled"), DT + m + 1)
                    V.tensor_tensor(Y[:, m % 2, :], T[:, 0, :], T[:, 1, :], ALU.add).then_inc(sem("merged"), 1)
                    v.wait_ge(sem("merged_hi"), DT + m + 1)
                    V.tensor_tensor(ML2[:, m, :], Y[:, m % 2, :], MH2[:, m, :].bitcast(F32), ALU.subtract)\
                        .then_inc(sem("merged_lo"), 1)

            def round_of_selection(q):
                i = 1 + q // 16
                link(V.max(M8, BIAS[i][:]))
                link(V.match_replace(BIAS[i][:], M8, BIAS[i][:], TAKEN))
                if q % 16 == 15:
                    V.tensor_scalar(MASK[i][:], BIAS[i][:], -2.0e38, NEG, ALU.is_gt, ALU.mult)\
                        .then_inc(sem("selected"), 1)

            def attention(a):
                at_ = ATT[a]
                for u in range(NU + 3):
                    if a >= 2 and u % 4 == 1 and u < NU:
                        split_lo(FIRST["gates2"] + DT * (a - 2) + u // 4)
                    if u < NU:
                        n = P * (u % NB + 1)
                        v.wait_ge(sem("scores"), NU * a + u + 1)
                        if u >= 4:
                            v.wait_ge(sem("probs"), NU * a + u - 3)
                        V.tensor_reduce(NMX[:, u % 4:u % 4 + 1], PS[:, u % 3, 0:n], AX, ALU.max, negate=True)\
                            .then_inc(sem("smax"), 1)
                    if a == 2 and u < NU:
                        for q in range(u * 48 // NU, (u + 1) * 48 // NU):
                            round_of_selection(q)
                    if u >= 3:
                        w = u - 3
                        h, i = divmod(w, NB)
                        r = RIN[:, w % 4:w % 4 + 1]
                        v.wait_ge(sem("probs"), NU * a + w + 1)
                        link(V.reciprocal(r, RSU[:, w % 4:w % 4 + 1]))
                        if a == 0 and h % 2:
                            link(V.tensor_tensor(r, r, LAM[:, 4:5], ALU.mult))
                        v.wait_ge(sem("pv"), NU * a + w + 1)
                        o = PS[:, 5 + w % 2, 0:at_["dv"]]
                        if a == 0:
                            dst = OD[:, i, (h // 2) * P:(h // 2 + 1) * P]
                            if h % 2:
                                ins = V.scalar_tensor_tensor(out=dst, in0=o, scalar=r, in1=dst, op0=ALU.mult,
                                                             op1=ALU.add)
                            else:
                                ins = V.tensor_scalar(dst, o, r, None, ALU.mult)
                        else:
                            dst = (None, OM, OF, OS)[a]
                            ins = V.tensor_scalar(dst[:, i, h * 64:h * 64 + 64], o, r, None, ALU.mult)
                        ins.then_inc(sem("onorm"), 1)

            def turn(a):
                src, oh, ol, f0, g = OUT_T[a]
                for f in range(4):
                    k = 4 * g + f
                    v.wait_ge(sem("turned_hi"), k + 1)
                    if a == 0:
                        ins = V.scalar_tensor_tensor(out=ol[:, f0 + f, :], in0=PS[:, 6 + k % 2, :], scalar=GM[:, 0:1],
                                                     in1=oh[:, f0 + f, :].bitcast(F32), op0=ALU.mult,
                                                     op1=ALU.subtract)
                    else:
                        ins = V.tensor_tensor(ol[:, f0 + f, :], PS[:, 6 + k % 2, :],
                                              oh[:, f0 + f, :].bitcast(F32), ALU.subtract)
                    ins.then_inc(sem("turned_lo"), 1)

            def merge(b):
                n0 = FIRST[f"merge{b + 1}"]
                mh, ml = ((MH1, ML1), (MH2, ML2))[b]

                def pair(i):
                    for j in range(2):
                        for g in range(3):
                            split_lo(n0 + 3 * j + g, 6, i)
                        v.wait_ge(sem("chunk_used"), 6 * i + (n0 + 3 * j + 3))
                        v.wait_ge(sem("gate"), 4 * i + (16 * b + 2 * j + 2))
                        for g in range(2):
                            V.tensor_tensor(T[:, g, :], T[:, g, :], PS[:, 4 * j + 2 + g, :], ALU.mult)\
                                .then_inc(sem("branch_scaled" if g else "first_scaled"), 1)
                        v.wait_ge(sem("branch_scaled"), 2 * i + (DT * b + j + 1))
                        if not (isinstance(i, int) and 2 * i + DT * b == 0):
                            v.wait_ge(sem("merged_lo"), 2 * i + (DT * b + j - 1))
                        V.tensor_tensor(Y[:, j, :], T[:, 0, :], T[:, 1, :], ALU.add).then_inc(sem("merged"), 1)
                        v.wait_ge(sem("merged_hi"), 2 * i + (8 * b + j + 1))
                        V.tensor_tensor(ml[:, bass.ds(2 * i + j, 1), :], Y[:, j:j + 1, :],
                                        mh[:, bass.ds(2 * i + j, 1), :].bitcast(F32), ALU.subtract)\
                            .then_inc(sem("merged_lo"), 1)

                pair(0)
                with v.Fori(1, 4) as i:
                    pair(i)

            def out_proj(b):
                n0 = FIRST[f"out{b + 1}"]
                k = (3, 7)[b]
                clear_sum(k)
                for m in range(DT):
                    split_lo(n0 + m)
                    v.wait_ge(sem("chunk_used"), n0 + m + 1)
                    if b == 0:
                        V.tensor_tensor(X[:, m, :], X[:, m, :], PS[:, m % 4, :], ALU.add)\
                            .then_inc(sem("x_added"), 1)
                    else:
                        c = 5 * DT + m
                        V.scalar_tensor_tensor(out=X[:, m, :], in0=PS[:, m % 4, :], scalar=MOD[:, c:c + 1],
                                               in1=X[:, m, :], op0=ALU.mult, op1=ALU.add)\
                            .then_inc(sem("x_added"), 1)
                    if m:
                        add_square(k, m - 1)
                norm(k)

            def ffn(f):
                n0 = FIRST[f"up{f + 1}"]

                def three(i, tiles=3):
                    for j in range(tiles):
                        split_lo(n0 + 2 * j, 6, i)
                        if f == 0 and tiles == 3 and j < 2:
                            for r in range(2):
                                ada_piece(16 + 4 * j + r, 8, i)
                        split_lo(n0 + 2 * j + 1, 6, i)
                        v.wait_ge(sem("chunk_used"), 6 * i + (n0 + 2 * j + 2))
                        v.wait_ge(sem("silu"), 3 * i + (FT * f + j + 1))
                        if not (isinstance(i, int) and FT * f + 3 * i + j == 0):
                            v.wait_ge(sem("hid_lo"), 3 * i + (FT * f + j))
                        V.tensor_tensor(Y[:, 0, :], T[:, 0, :], PS[:, 2 * j + 1, :], ALU.mult).then_inc(sem("hid"), 1)
                        v.wait_ge(sem("hid_hi"), 3 * i + (FT * f + j + 1))
                        V.tensor_tensor(HIDL[:, bass.ds(3 * i + j, 1), :], Y[:, 0:1, :],
                                        HIDH[:, bass.ds(3 * i + j, 1), :].bitcast(F32), ALU.subtract)\
                            .then_inc(sem("hid_lo"), 1)
                        if f == 0 and tiles == 3 and j < 2:
                            for r in range(2):
                                ada_piece(18 + 4 * j + r, 8, i)
                        if f == 0 and tiles == 3 and j == 2:
                            ada_take(i + 2, loop=True)

                three(0)
                with v.Fori(1, 7) as i:
                    three(i)
                three(7, tiles=1)
                n0 = FIRST[f"down{f + 1}"]
                if f == 0:
                    modulation()
                if f == 1:
                    v.wait_ge(sem("pos_loaded"), 32)
                    link(V.tensor_copy(T[:, 1, :], T[:, 1, :].bitcast(I32)))
                    v.wait_ge(sem("hid_lo"), 2 * FT)
                    angles(2, T[:, 1, :], "freq_a")
                if f < 2:
                    clear_sum((4, 6)[f])

                def two(i):
                    for j in range(2):
                        for g in range(3):
                            split_lo(n0 + 3 * j + g, 6, i)
                        v.wait_ge(sem("chunk_used"), 6 * i + (n0 + 3 * j + 3))
                        xt = X[:, bass.ds(2 * i + j, 1), :]
                        gate = (0, 2, 8)[f] * DT
                        if f == 0:
                            V.tensor_tensor(xt, xt, PS[:, j:j + 1, :], ALU.add).then_inc(sem("x_added"), 1)
                        else:
                            V.scalar_tensor_tensor(out=xt, in0=PS[:, j:j + 1, :],
                                                   scalar=MOD[:, bass.ds(2 * i + (gate + j), 1)], in1=xt,
                                                   op0=ALU.mult, op1=ALU.add).then_inc(sem("x_added"), 1)
                        if f < 2 and not (isinstance(i, int) and i == 0 and j == 0):
                            add_square((4, 6)[f], j - 1, i)

                two(0)
                if f == 1:
                    angles(3, T[:, 1, :], "freq_i")
                with v.Fori(1, 3) as i:
                    two(i)
                two(3)
                if f < 2:
                    norm((4, 6)[f])

            def modulation():
                v.wait_ge(sem("mod"), 9)
                for s in range(3):
                    c = MOD[:, (3 * s + 1) * DT:(3 * s + 2) * DT]
                    link(V.tensor_scalar(c, c, 1.0, None, ALU.add))
                    link(V.tensor_tensor(c, c, col("g2", s * DT, DT), ALU.mult))
                for s in (0, 2):
                    c = MOD[:, (3 * s + 2) * DT:(3 * s + 3) * DT]
                    link(V.tensor_scalar(c, c, 0.5, None, ALU.mult))

            link(V.memset(PIH, float(np.pi / 2)))
            V.memset(EPSC, EPS).then_inc(sem("eps_set"), 1)
            v.wait_ge(sem("pos_loaded"), 16)
            v.wait_ge(sem("consts_loaded"), 32)
            v.wait_ge(sem("lams_loaded"), 16)
            for j in range(2):
                link(V.tensor_tensor(SQ[:, 1, 64 * j:64 * j + 64], SQ[:, 0, 128 * j:128 * j + 64],
                                     SQ[:, 0, 128 * j + 64:128 * j + 128], ALU.mult))
                V.tensor_reduce(LAM[:, j:j + 1], SQ[:, 1, 64 * j:64 * j + 64], AX, ALU.add)\
                    .then_inc(sem("lams_used" if j else "lam_half"), 1)
            split_lo(-2)
            split_lo(-1)
            clear_sum(0)
            for t in range(DT - 1):
                add_square(0, t)
            norm(0)
            link(V.tensor_copy(T[:, 0, :], T[:, 0, :].bitcast(I32)))
            link(V.tensor_copy(IDENT_B[:], SQV["ident"]))
            link(V.tensor_copy(CAUSAL_B[:], SQV["causal"]))
            angles(0, T[:, 0, :], "freq_a")
            angles(1, T[:, 0, :], "freq_p")
            v.wait_ge(sem("table"), 2)
            v.wait_ge(sem("cond_ready"), 1)
            project_in1()
            for j in range(4):
                split_lo(FIRST["dv1"] + j)
            ada_take(1)
            v.wait_ge(sem("lam_exp"), 1)
            link(V.tensor_tensor(LAM[:, 4:5], LAM[:, 3:4], LAM[:, 2:3], ALU.subtract))
            link(V.tensor_scalar(LAM[:, 4:5], LAM[:, 4:5], -(0.8 - 0.6), None, ALU.add))
            attention(0)
            v.wait_ge(sem("diff_std"), 1)
            link(V.reciprocal(RSD, RSD))
            for k in range(16):
                o = OD[:, k // 4, (k % 4) * P:(k % 4 + 1) * P]
                ins = V.tensor_scalar(o, o, RSD[:, k:k + 1], None, ALU.mult)
            ins.then_inc(sem("diff_normed"), 1)
            clear_sum(1)
            for t in range(2):
                add_square(1, t)
            V.tensor_scalar(GM[:, 0:1], col("g_sub"), 1.0 - (0.8 - 0.6), None, ALU.mult)\
                .then_inc(sem("g_sub_scaled"), 1)
            norm(1)
            clear_sum(2)
            add_square(2, 0)
            norm(2)
            for j in range(4):
                split_lo(FIRST["uq"] + j)
            for r in range(2):
                q = ROT_BASE["uq"] + r
                rope(q, 6 + r, Y[:, r, :], TAB_P1)
                v.wait_ge(sem("rot_read"), q + 1)
                for h in range(4):
                    rows = slice(32 * h, 32 * h + 32)
                    ins = V.tensor_tensor(QM[64:96, 4 * r + h, :], T[rows, 0, :], T[rows, 1, :], ALU.add)
                ins.then_inc(sem("q_rotated"), 1)
                v.wait_ge(sem("q_rotated"), r + 1)
            split_lo(FIRST["uv"])
            attention(1)
            v.wait_ge(sem("g_sub_scaled"), 1)
            turn(0)
            turn(1)
            merge(0)
            out_proj(0)
            ffn(0)
            norm(5)
            ffn(1)
            link(V.tensor_scalar(FOXQ_G, col("fox_g", 0), 0.125, None, ALU.mult))
            link(V.tensor_scalar(DSAQ_G, col("dsa_g", 0), 0.125, None, ALU.mult))
            project_in2()
            V.tensor_copy(MASK[0][:], SQV["chunked"]).then_inc(sem("selected"), 1)
            v.wait_ge(sem("scored"), NDOTS)
            for i in range(1, NB):
                d = BIAS[i][:, i * P:(i + 1) * P]
                link(V.tensor_tensor(d, d, SQV["chunked"], ALU.add))
            attention(2)
            attention(3)
            turn(2)
            turn(3)
            branch2()
            out_proj(1)
            ffn(2)


def rot_at(tiles, k):
    return k + (5 if tiles[k][0] in ("dsaq", "misc") else 2)


def _tile(w):
    k, m = w.shape
    a = w.reshape(k // P, P, m).transpose(1, 0, 2).reshape(P, k // P * m)
    if a.shape[1] < 1024:
        a = np.concatenate([a, np.zeros((P, 1024 - a.shape[1]), w.dtype)], axis=1)
    return a


def _pad(w, n):
    return np.concatenate([w, np.zeros((w.shape[0], n - w.shape[1]), w.dtype)], axis=1)


def _ffn(gate, up, down):
    chunks = []
    for t in range(FT):
        chunks += [_tile(gate[:, t * P:(t + 1) * P]), _tile(up[:, t * P:(t + 1) * P])]
    for m in range(DT):
        w = down[:, m * P:(m + 1) * P]
        chunks += [_tile(w[0:1024]), _tile(w[1024:2048]), _tile(w[2048:FF])]
    return chunks


def _merge(gates, a, b):
    chunks = []
    for m in range(DT):
        c = slice(m * P, (m + 1) * P)
        chunks += [_tile(gates[:, :D][:, c]), _tile(gates[:, D:][:, c]), _tile(np.concatenate([a[:, c], b[:, c]]))]
    return chunks


def _tiles(w):
    return [_tile(w[:, m * P:(m + 1) * P]) for m in range(w.shape[1] // P)]


def _weights(a):
    w1, w2 = a["w_in"][0], a["w_in_2"][0]
    lat = QR + KVR
    o = lat + ROPE
    chunks = _tiles(w1[:, :lat]) + [_tile(_pad(w1[:, lat:o], P))] + _tiles(w1[:, o:o + 1024])
    chunks += [_tile(w1[256 * j:256 * j + 256, o + 1024:o + 1536]) for j in range(4)]
    uq = a["mla_w_uq"][0].reshape(QR, H1, NOPE + ROPE)
    uq = np.concatenate([uq[:, :, :NOPE].reshape(QR, 512), uq[:, :, NOPE:].reshape(QR, 256)], axis=1)
    for j in range(3):
        chunks.append(_pad(np.concatenate([_tile(uq[:, (2 * j + r) * P:(2 * j + r + 1) * P])[:, :384]
                                           for r in range(2)], axis=1), 1024))
    ukv = a["mla_w_ukv"][0].reshape(KVR, H1, NOPE + VDIM)
    uk, uv = ukv[:, :, :NOPE].reshape(KVR, 512), ukv[:, :, NOPE:].reshape(KVR, 512)
    chunks.append(np.concatenate([_tile(uk[:, m * P:(m + 1) * P])[:, :256] for m in range(4)], axis=1))
    chunks.append(_tile(uv))
    chunks += _merge(w1[:, o + 1536:], a["w_branch_mla"][0], a["w_branch_diff"][0])
    chunks += _tiles(a["w_out"][0])
    chunks += _ffn(a["w_ffn_gate"][0], a["w_ffn_up"][0], a["w_ffn_down"][0])
    chunks += _ffn(a["ffn1_w1_2"][0], a["ffn1_w3_2"][0], a["ffn1_w2_2"][0])
    fq, fk, fv, ff, dq, dk, dv, iq, ik, iw, gates = np.split(
        w2, np.cumsum([512, 512, 512, 8, 512, 64, 64, 256, 32, 8]).tolist(), axis=1)
    chunks += _tiles(iq)
    chunks.append(_tile(_pad(np.concatenate([dv, iw], axis=1), P)))
    chunks.append(_tile(_pad(np.concatenate([dk, ik, ff], axis=1), P)))
    chunks += _tiles(dq) + _tiles(fq) + _tiles(fk)
    chunks += [_tile(fv[256 * j:256 * j + 256]) for j in range(4)]
    merge = _merge(gates, a["w_br_fox_2"][0], a["w_br_dsa_2"][0])
    chunks += merge[0::3] + merge[1::3] + merge[2::3]
    chunks += _tiles(a["w_out_2"][0])
    chunks += _ffn(a["ffn2_w1_2"][0], a["ffn2_w3_2"][0], a["ffn2_w2_2"][0])
    return np.stack(chunks)


def _freq(rot, period):
    half = rot // 2
    f = (THETA ** (-np.arange(half) * 2.0 / rot)).astype(np.float32)
    col = np.zeros(P, np.float32)
    for p in range(P):
        if p % period < rot:
            col[p] = f[p % period % half]
    return col


def _columns(a):
    c = np.zeros((P, NCOLS), np.float32)

    def put(name, v, k=0):
        v = np.asarray(v).reshape(-1, P).T
        c[:, COLS[name][0] + k:COLS[name][0] + k + v.shape[1]] = v

    put("g_mix", a["norm_mix_g"])
    put("g_q", a["mla_q_norm_g"])
    put("g_kv", a["mla_kv_norm_g"])
    put("g_sub", a["diff_subln_g"])
    put("g_ffn", a["norm_ffn_g"])
    put("g_final", a["norm_final_g"])
    put("b_gate", a["b_gate"])
    put("g2", a["norm_g_2"])
    put("ada_b", a["ada_b_2"])
    put("cond", a["c_2"])
    for n, src in (("fox_g", a["fox_qk_g_2"][0]), ("dsa_g", a["dsa_qk_g_2"][0])):
        for k in range(2):
            put(n, np.concatenate([src[k], src[k]]), k)
    c[96:104, COLS["f_bias"][0]] = a["fox_f_bias_2"][0]
    put("freq_a", _freq(16, 64))
    put("freq_p", _freq(32, 32))
    put("freq_i", _freq(8, 32))
    return c


def _squares():
    q = np.zeros((P, NSQ, P), np.float32)
    n = {name: k for k, name in enumerate(SQUARES)}
    q[:, n["ident"], :] = np.eye(P)
    q[:, n["ones"], :] = 1.0
    q[:64, n["halves"], :64] = q[64:, n["halves"], 64:] = 1.0
    for name, spans in (("rot_a", [(0, 8), (64, 8)]), ("rot_p", [(32 * b, 16) for b in range(4)]),
                        ("rot_i", [(32 * b, 4) for b in range(4)]), ("rot_m", [(0, 8), (64, 4)])):
        for first, half in spans:
            for r in range(first, first + half):
                q[r + half, n[name], r] = -1.0
                q[r, n[name], r + half] = 1.0
    q[:, n["causal"], :] = np.triu(np.full((P, P), NEG, np.float32), 1)
    q[:CHUNK, n["chunked"], CHUNK:] = NEG
    return q


def kernel(**inputs):
    import concourse.bacc as bacc
    from concourse.bass_utils import run_bass_kernel_spmd

    a = {k: np.asarray(v) for k, v in inputs.items()}
    arrays = {
        "weights": _weights(a),
        "ada": np.ascontiguousarray(a["ada_w_2"][0].reshape(DT, P, 9, D).transpose(2, 0, 1, 3).reshape(72, P, D)),
        "x_in": np.ascontiguousarray(a["x"][0].T.reshape(DT, P, S).transpose(1, 0, 2)),
        "columns": _columns(a),
        "squares": _squares(),
        "positions1": a["positions"].reshape(S),
        "positions2": a["positions_2"].reshape(S),
        "lambdas": np.concatenate([a[f"diff_lambda_{n}"].reshape(-1) for n in ("q1", "k1", "q2", "k2")]),
    }
    nc = bacc.Bacc("TRN2", target_bir_lowering=False, num_devices=1)
    args = [nc.dram_tensor(n, v.shape, mybir.dt.from_np(v.dtype), kind="ExternalInput").ap()
            for n, v in arrays.items()]
    out = nc.dram_tensor("y_out", (P, DT, S), F32, kind="ExternalOutput").ap()
    build(nc, *args, out)
    got = run_bass_kernel_spmd(nc, [arrays], core_ids=[0]).results[0]["y_out"]
    return np.ascontiguousarray(got.transpose(1, 0, 2).reshape(D, S).T)[None]
```

```python
from contextlib import ExitStack

import numpy as np

import concourse.bass as bass
from concourse import mybir

F32 = mybir.dt.float32
F32R = mybir.dt.float32r
I32 = mybir.dt.int32
BF16 = mybir.dt.bfloat16
ALU = mybir.AluOpType
ACT = mybir.ActivationFunctionType
AX = mybir.AxisListType.X

P = 128
S = 512
D = 1024
DT = D // P
FF = 2816
FT = FF // P
NB = S // P
EPS = 1e-6
NEG = -1.0e30
TAKEN = -3.0e38
THETA = 500000.0
H1, NOPE, ROPE, VDIM = 8, 64, 32, 64
QR, KVR = 384, 256
DH, DHD = 4, 64
TOPK = 128
CHUNK = 64

COLS = {}
_at = 0
for _name, _n in (("g_mix", DT), ("g_q", QR // P), ("g_kv", KVR // P), ("g_sub", 1), ("g_ffn", DT),
                  ("g_final", DT), ("b_gate", 2 * DT), ("g2", 3 * DT), ("ada_b", 9 * DT), ("cond", DT),
                  ("fox_g", 2), ("dsa_g", 2), ("f_bias", 1), ("freq_a", 1), ("freq_p", 1),
                  ("freq_i", 1)):
    COLS[_name] = (_at, _n)
    _at += _n
NCOLS = _at
SQUARES = ("ident", "ones", "halves", "rot_a", "rot_p", "rot_i", "rot_m", "causal", "chunked")
NSQ = len(SQUARES)

STREAM = (("in1", 14), ("dv1", 4), ("uq", 3), ("uk", 1), ("uv", 1), ("merge1", 24), ("out1", 8),
          ("up1", 2 * FT), ("down1", 3 * DT),
          ("up2", 2 * FT), ("down2", 3 * DT), ("in2", 16), ("fv2", 4), ("gates2", 2 * DT), ("branch2", 8),
          ("out2", 8), ("up3", 2 * FT), ("down3", 3 * DT))
FIRST = {}
_at = 0
for _name, _n in STREAM:
    FIRST[_name] = _at
    _at += _n
NCH = _at
LAST_DOWN = [8, 8, 6]

KB = 1024


def build(nc, wst, ada, xT, cols_d, squares_d, pos1_d, pos2_d, lams_d, out):
    ctx = ExitStack()
    with ctx:
        used_sems = {}

        def sem(name):
            if name not in used_sems:
                used_sems[name] = ctx.enter_context(nc.semaphore(name))
            return used_sems[name]

        region = ctx.enter_context(nc.sbuf_tensor("region", [P, 207 * KB // 4], F32))
        base = 0
        if nc.sbuf_base - 207 * KB > 0:
            base = nc.sbuf_base - 207 * KB

        def at(name, kb, shape, dt=F32):
            return nc.alloc_sbuf_tensor_at(name, shape, dt, offset=base + int(kb * KB))

        PS = ctx.enter_context(nc.psum_tensor("PS", [P, 8, S], F32))

        WARM = [(4, 1, 2), None, None, (1, 1, 2), (1, 1, 1), (1, 1, 2), (1, 1, 2)]
        TURN_BANKS = [4, 5, 6, 7] * 2 + [2, 7, 0, 1] * 2
        BRANCH_BANKS = ((3, 4), (5, 6))
        DV_BANKS, UV_BANKS, FV_BANKS = (3, 6, 4, 5), (4, 5, 6, 7), (0, 1, 2, 5)
        FORGET_AT = 9

        X = at("X", 0, [P, DT, S])
        XH, XL = at("XH", 16, [P, DT, S], F32R), at("XL", 32, [P, DT, S], F32R)
        RAW = [at(f"RAW{j}", 48 + 4 * j, [P, 1024]) for j in range(3)]
        HI = [at(f"HI{j}", 60 + 4 * j, [P, 1024], F32R) for j in range(3)]
        LO = [at(f"LO{j}", 72 + 4 * j, [P, 1024], F32R) for j in range(3)]
        ADA = [at(f"ADA{j}", 84 + 4 * j, [P, 1024]) for j in range(2)]
        ACC = at("ACC", 92, [P, 1024])
        RB = at("RB", 96, [P, 2, S])
        SQ = at("SQ", 100, [P, 2, S])
        Y = at("Y", 104, [P, 2, S])
        T = at("T", 108, [P, 2, S])
        SQC = at("SQC", 112, [P, NSQ, P])
        CO = at("CO", 116.5, [P, NCOLS])
        MOD = at("MOD", 117.25, [P, 9 * DT])
        SM = at("SM", 117.625, [P, 96])
        IDENT_B, CAUSAL_B = at("IDENT_B", 206, [P, P], BF16), at("CAUSAL_B", 206.25, [P, P], BF16)
        SM2 = at("SM2", 206.5, [P, 48])
        A0 = 118
        HIDH = at("HIDH", A0, [P, FT, S], F32R)
        HIDL = at("HIDL", A0 + 44, [P, FT, S], F32R)
        LATQ = at("LATQ", A0, [P, 3, S])
        LATK = at("LATK", A0 + 6, [P, 2, S])
        KR = at("KR", A0 + 10, [P, S])
        DQ, DK = at("DQ", A0 + 12, [P, 4, S]), at("DK", A0 + 20, [P, 4, S])
        DV = at("DV", A0 + 28, [P, NB, S])
        TAB_A1 = at("TAB_A1", A0 + 36, [P, 2, S])
        TAB_P1 = at("TAB_P1", A0 + 40, [P, 2, S])
        P1 = [at(f"P1_{j}", A0 + 44 + 2 * j, [P, S]) for j in range(3)]
        PT1 = [at("PT1_0", A0 + 50, [P, S]), at("PT1_1", 100, [P, S])]
        OD = at("OD", A0 + 52, [P, NB, S])
        LQH, LQL = at("LQH", A0 + 60, [P, 3, S], F32R), at("LQL", A0 + 66, [P, 3, S], F32R)
        LKH, LKL = at("LKH", A0 + 72, [P, 2, S], F32R), at("LKL", A0 + 76, [P, 2, S], F32R)
        QM = at("QM", A0 + 12, [P, 8, S])
        VM = at("VM", A0 + 28, [P, NB, S])
        KM = [at("KM0", A0 + 80, [P, 4, S]), at("KM1", A0, [P, 4, S])]
        OM = at("OM", A0 + 36, [P, NB, S])
        OTH1, OTL1 = at("OTH1", A0 + 60, [P, 8, S], F32R), at("OTL1", A0 + 12, [P, 8, S], F32R)
        MH1, ML1 = at("MH1", A0 + 28, [P, 8, S], F32R), at("ML1", A0 + 44, [P, 8, S], F32R)
        LAMS = at("LAMS", A0 + 44, [P, S])
        QF, KF = at("QF", A0, [P, 8, S]), at("KF", A0 + 16, [P, 8, S])
        VF = at("VF", A0 + 32, [P, NB, S])
        DQ2 = at("DQ2", A0 + 40, [P, 4, S])
        IQ, IK, DK2 = at("IQ", A0 + 48, [P, 2, S]), at("IK", A0 + 52, [P, S]), at("DK2", A0 + 54, [P, S])
        DVW = at("DVW", A0 + 56, [P, NB, 72])
        IW = at("IW", A0 + 57.25, [P, NB, 8])
        POS2 = at("POS2", 92, [P, S])
        TAB_A2, TAB_I2 = at("TAB_A2", 84, [P, 2, S]), at("TAB_I2", 88, [P, 2, S])
        P2 = [at(f"P2_{j}", A0 + 66 + 2 * j, [P, S]) for j in range(3)]
        PT2 = [at("PT2_0", A0 + 72, [P, S]), at("PT2_1", A0 + 52, [P, S])]
        P3 = [at("P3_0", 104, [P, S]), at("P3_1", 106, [P, S]), at("P3_2", 100, [P, S])]
        PT3 = [at("PT3_0", 102, [P, S]), at("PT3_1", 98, [P, S])]
        MASK = [at(f"MASK{i}", A0 + 48 + 0.25 * (i * (i + 1) // 2), [P, P * (i + 1)], BF16) for i in range(NB)]
        FW = at("FW", A0 + 66, [P, 4, S])
        OF = at("OF", A0 + 74, [P, NB, S])
        R = at("R", A0 + 80, [P, 4, S])
        MISC = at("MISC", A0 + 74, [P, S])
        VW = at("VW", A0 + 76, [P, S])
        OS = at("OS", A0 + 58, [P, NB, S])
        BIAS = [at(f"BIAS{i}", A0 + 58 + 0.5 * (i * (i + 1) // 2), [P, P * (i + 1)]) for i in range(NB)]
        OTH2, OTL2 = at("OTH2", A0 + 32, [P, 8, S], F32R), at("OTL2", A0 + 66, [P, 8, S], F32R)
        GATE_F = [at(f"GATE_F{m}", 84 + 2 * m if m < 6 else A0 + 82 + 2 * (m - 6), [P, S]) for m in range(DT)]
        GATE_D = at("GATE_D", A0, [P, 8, S])
        MH2, ML2 = at("MH2", A0 + 16, [P, 8, S], F32R), at("ML2", A0, [P, 8, S], F32R)
        GATE2 = [[g[:, :] for g in GATE_F], [GATE_D[:, m, :] for m in range(DT)]]

        SILU = [T[:, 0, :], T[:, 1, :], Y[:, 1, :]]
        SQV = {n: SQC[:, k, :] for k, n in enumerate(SQUARES)}

        def col(name, k=0, n=1, rows=slice(0, P)):
            a = COLS[name][0] + k
            return CO[rows, a:a + n]

        NMX, NBI, RSU, RIN = (SM[:, 4 * k:4 * k + 4] for k in range(4))
        LAM = SM[:, 16:24]
        SSD = SM[:, 24:40]
        RSD = SM[:, 40:56]
        M8 = SM[:, 56:64]
        GM = SM[:, 64:72]
        HG = SM[:, 72:80]
        PIH = SM[:, 80:81]
        EPSC = SM[:, 81:82]
        CND = SM[:, 88:96]
        FOXQ_G, DSAQ_G = SM[:, 82:83], SM[:, 83:84]
        NSTD, NR = SM2[:, 0:4], SM2[:, 4:8]
        HSTD = [SM2[:, 8 + 8 * k:16 + 8 * k] for k in range(2)]
        HR = [SM2[:, 24 + 8 * k:32 + 8 * k] for k in range(2)]

        SM3 = at("SM3", 206.6875, [P, 24])
        FSTD, FR, FV = SM3[:, 0:8], SM3[:, 8:16], SM3[:, 16:24]
        G_BOTH = SM2[:, 40:48]
        EPS2C = SM[:, 84:85]
        S_X, S_XG = PS[:, 7, 8:12], PS[:, 7, 12:16]
        SUM_G = T[:, 0, :]

        NORMS = [
            (DT, X, D, "g_mix", XH, XL), (3, LATQ, QR, "g_q", LQH, LQL), (2, LATK, KVR, "g_kv", LKH, LKL),
            (DT, X, D, "g_ffn", XH, XL),
            (DT, X, D, 0, XH, XL), (DT, X, D, 1, XH, XL), (DT, X, D, 2, XH, XL)]
        NTB = np.cumsum([0] + [n[0] for n in NORMS]).tolist()
        SAB = np.cumsum([0] + [n[0] - 1 for n in NORMS]).tolist()
        SPLIT_TB = np.cumsum([0] + [n[0] if n[4] is not None else 0 for n in NORMS]).tolist()

        def repeat(eng, times, body):
            if times == 1:
                body(0)
                return
            with eng.Fori(0, times) as i:
                body(i)

        IN1 = [("copy", LATQ[:, t, :]) for t in range(3)] + [("copy", LATK[:, t, :]) for t in range(2)] \
            + [("rope", KR[:, :], TAB_P1, "rot_p")] \
            + [("rope", DQ[:, t, :], TAB_A1, "rot_a", DHD ** -0.5) for t in range(4)] \
            + [("rope", DK[:, t, :], TAB_A1, "rot_a") for t in range(4)]
        IN2 = [("rope", IQ[:, t, :], TAB_I2, "rot_i") for t in range(2)] + [("dvw",), ("misc", MISC[:, :])] \
            + [("dsaq", DQ2[:, t, :], TAB_A2, "rot_a") for t in range(4)] \
            + [("foxq", t) for t in range(4)] + [("foxk", t) for t in range(4)]
        DOTS_FROM, NDOTS = 14, 8 * (NB - 1)
        IN2_STEPS = DOTS_FROM + NDOTS // 4

        def rot_tiles(tiles):
            return [k for k, t in enumerate(tiles) if t[0] in ("rope", "dsaq", "misc")]

        ROT1, ROT2 = rot_tiles(IN1), rot_tiles(IN2)
        NRM2 = [k for k, t in enumerate(IN2) if t[0] in ("foxq", "foxk", "dsaq", "misc")]
        ALL_ROTATED = len(ROT1) + len(ROT2) - 1
        ROT_BASE = {"in1": 0, "uq": len(ROT1), "in2": len(ROT1) + 2}
        rot_src = {}

        MLA_SCALE = (NOPE + ROPE) ** -0.5

        def q_diff(c, i):
            return DQ[64 * (c % 2):64 * (c % 2) + 64, c // 2, i * P:(i + 1) * P]

        def k_diff(c, n):
            return DK[64 * (c % 2):64 * (c % 2) + 64, c // 2, 0:n]

        ATT = [
            None,
            dict(q=lambda h, i: QM[0:96, h, i * P:(i + 1) * P], k=lambda h, n: KM[h // 4][0:96, h % 4, 0:n],
                 v=lambda kb, h: VM[:, kb, h * 64:h * 64 + 64], dv=64, P=P1, PT=PT1),
            dict(q=lambda h, i: QF[0:66, h, i * P:(i + 1) * P], k=lambda h, n: KF[0:66, h, 0:n],
                 v=lambda kb, h: VF[:, kb, h * 64:h * 64 + 64], dv=64, P=P2, PT=PT2),
            dict(q=lambda h, i: DQ2[64 * (h % 2):64 * (h % 2) + 64, h // 2, i * P:(i + 1) * P],
                 k=lambda h, n: DK2[64 * (h % 2):64 * (h % 2) + 64, 0:n],
                 v=lambda kb, h: DVW[:, kb, 0:64], dv=64, P=P3, PT=PT3)]
        NU = 8 * NB
        NPAIR = NU // 2
        AFTER = [0] + [NPAIR + NU * k for k in range(3)]
        P1B = [Y[:, 0, :], Y[:, 1, :], T[:, 0, :]]
        PAIR_INV = [SM3[:, 2 * k:2 * k + 2] for k in range(8)]
        FACTOR = [SM3[:, 16 + k:17 + k] for k in range(2)]
        SCORE_BANKS = ((0, 1), (2, 7))
        XA = {"out1": 0, "down1": DT, "down2": 2 * DT, "out2": 3 * DT, "down3": 4 * DT}
        OUT_T = [(OD, OTH1, OTL1, 4, 1), (OM, OTH1, OTL1, 0, 0), (OF, OTH2, OTL2, 0, 2), (OS, OTH2, OTL2, 4, 3)]

        block = ctx.enter_context(nc.Block())

        @block.sync
        def _(sp):
            sp.dma_start(CO[:], cols_d).then_inc(sem("columns_loaded"), 16)
            for t in range(4):
                sp.dma_start(X[:, 2 * t:2 * t + 2, :], xT[:, 2 * t:2 * t + 2, :]).then_inc(sem(f"x_loaded{t}"), 16)
            sp.dma_start(SQC[:], squares_d).then_inc(sem("squares_loaded"), 16)
            for j in range(3):
                sp.dma_start(RAW[j][:], wst[j]).then_inc(sem(f"raw{j}"), 16)

            def more(i):
                for j in range(3):
                    sp.wait_ge(sem("lo_ready"), 3 * i + j + 1)
                    sp.dma_start(RAW[j][:], wst[3 * i + (j + 3)]).then_inc(sem(f"raw{j}"), 16)

            repeat(sp, (NCH - 3) // 3, more)
            for n in range(3 + (NCH - 3) // 3 * 3, NCH):
                sp.wait_ge(sem("lo_ready"), n - 2)
                sp.dma_start(RAW[n % 3][:], wst[n]).then_inc(sem(f"raw{n % 3}"), 16)
            for t in range(DT):
                sp.wait_ge(sem("x_added"), XA["down3"] + t + 1)
                sp.dma_start(out[:, t, :], X[:, t, :]).then_inc(sem("stored"), 16)
            sp.wait_ge(sem("stored"), 16 * DT)

        @block.gpsimd
        def _(pool):
            pool.dma_start(T[:, 0, :].bitcast(I32), pos1_d.partition_broadcast(P)).then_inc(sem("pos_loaded"), 16)
            pool.dma_start(LAMS[:, 0:256], lams_d.partition_broadcast(P)).then_inc(sem("lams_loaded"), 16)
            for j in range(2):
                pool.dma_start(ADA[j][:], ada[j]).then_inc(sem(f"ada{j}"), 16)

            def ada_more(i):
                for j in range(2):
                    pool.wait_ge(sem("ada_added"), 2 * i + j + 1)
                    pool.dma_start(ADA[j][:], ada[2 * i + (j + 2)]).then_inc(sem(f"ada{j}"), 16)

            pool.wait_ge(sem("rotated"), 1)
            pool.wait_ge(sem("split_lo"), SPLIT_TB[3])
            for h in range(8):
                pool.tensor_copy(KM[h // 4][64:96, h % 4, :], KR[0:32, :]).then_inc(sem("k_shared"), 1)
            repeat(pool, 35, ada_more)
            pool.wait_ge(sem("x_added"), 2 * DT)
            pool.wait_ge(sem("mod"), 9)
            pool.dma_start(POS2[:].bitcast(I32), pos2_d.partition_broadcast(P)).then_inc(sem("pos_loaded"), 16)
            pool.wait_ge(sem("x_added"), 3 * DT)
            pool.memset(QF[64:66, :, :], 1.0).then_inc(sem("f_ones"), 1)
            pool.memset(KF[64:66, :, :], 1.0).then_inc(sem("f_ones"), 1)
            pool.wait_ge(sem("f_ones"), 2)
            pool_steps = [0]

            def link(ins):
                pool_steps[0] += 1
                ins.then_inc(sem("f_link"), 1)
                pool.wait_ge(sem("f_link"), pool_steps[0])

            pool.wait_ge(sem("f_act"), 3)
            link(pool.tensor_scalar(FW[0:8, 0, :], FW[0:8, 0, :], 0.0, None, ALU.min))
            link(pool.tensor_tensor(FW[0:8, 0, :], FW[0:8, 0, :], FW[0:8, 3, :], ALU.subtract))
            a, b, d = 0, 1, 1
            while d < S:
                pool.tensor_copy(FW[0:8, b, 0:d], FW[0:8, a, 0:d]).then_inc(sem("f_head"), 1)
                link(pool.tensor_tensor(FW[0:8, b, d:S], FW[0:8, a, d:S], FW[0:8, a, 0:S - d], ALU.add))
                a, b, d = b, a, 2 * d
            for k, s in ((2, 1.0), (3, -1.0)):
                pool.tensor_scalar(FW[0:8, k, :], FW[0:8, a, :], s, None, ALU.mult).then_inc(sem("f_scaled"), 1)
            pool.wait_ge(sem("f_scaled"), 2)
            pool.dma_start(QF[65:66, :, :], FW[0:8, 2, :]).then_inc(sem("f_rows"), 16)
            pool.dma_start(KF[64:65, :, :], FW[0:8, 3, :]).then_inc(sem("f_rows"), 16)

        @block.tensor
        def _(pe):
            mm = nc.tensor.matmul
            released = dict.fromkeys(("in_copied", "v_copied", "proj_copied", "branch_scaled", "x_added", "hid",
                                      "gate_copied"), 0)

            def all_released(but=()):
                for name, count in released.items():
                    if count and name not in but:
                        pe.wait_ge(sem(name), count)

            def split_product(bank, w, blocks, tiles, moving, first=True, last=True, between={}):
                hi, lo = HI[w][:], LO[w][:]
                for b, t in zip(blocks, tiles):
                    if b in between:
                        between[b]()
                    a, z = hi[:, b * P:(b + 1) * P], lo[:, b * P:(b + 1) * P]
                    start, stop = first and b == blocks[0], last and b == blocks[-1]
                    mm(bank, a, moving[0][:, t, :], start=start, stop=False)
                    mm(bank, a, moving[1][:, t, :], start=False, stop=False)
                    ins = mm(bank, z, moving[0][:, t, :], start=False, stop=stop)
                return ins

            def chunk(n0, step, i):
                pe.wait_ge(sem("lo_ready"), step * i + (n0 + 1))
                return n0 % 3

            def used(ins):
                ins.then_inc(sem("chunk_used"), 1)

            def keep_warm(n):
                for _ in range(n):
                    mm(PS[:, 5, :], SQV["ident"], SQC[:, 0:4, :].rearrange("p n m -> p (n m)"), start=True,
                       stop=True)

            def norm(k):
                keep_warm(WARM[k][0])
                norm_sums(k)
                keep_warm(WARM[k][1])
                norm_spread(k)
                if k == 4:
                    pe.wait_ge(sem("final_expanded"), 1)
                    for b in range(NB):
                        tok = slice(b * P, (b + 1) * P)
                        ins = nc.tensor.transpose(PS[:, 7, tok], RB[:, 0, tok], SQV["ident"])
                    ins.then_inc(sem("final_spread"), 1)
                keep_warm(WARM[k][2])

            def norm_sums(k):
                nt = NORMS[k][0]
                pe.wait_ge(sem("sum_added"), SAB[k + 1])
                if k:
                    pe.wait_ge(sem("stds"), k)
                if k == 5:
                    pe.wait_ge(sem("finished"), DT)
                for b in range(NB):
                    mm(PS[:, 7, 8 + b:9 + b], RB[:, 0, b * P:(b + 1) * P], SQV["ones"][:, 0:1],
                       start=b == 0, stop=False)
                pe.wait_ge(sem("squared"), NTB[k + 1])
                for b in range(NB):
                    ins = mm(PS[:, 7, 8 + b:9 + b], SQ[:, (nt - 1) % 2, b * P:(b + 1) * P],
                             SQV["ones"][:, 0:1], start=False, stop=b == NB - 1 and k != 4)
                if k == 4:
                    pe.wait_ge(sem("g_squared"), DT)
                    pe.wait_ge(sem("g_sum_added"), DT)
                    for b in range(NB):
                        for n, src in enumerate((SUM_G, Y[:, 1, :])):
                            ins = mm(PS[:, 7, 12 + b:13 + b], src[:, b * P:(b + 1) * P], SQV["ones"][:, 0:1],
                                     start=False, stop=n == 1 and b == NB - 1)
                ins.then_inc(sem("sq_summed"), 1)

            def norm_spread(k):
                pe.wait_ge(sem("expanded"), k + 1)
                if k:
                    pe.wait_ge(sem("normed"), NTB[k])
                for b in range(NB):
                    tok = slice(b * P, (b + 1) * P)
                    ins = nc.tensor.transpose(PS[:, 6, tok], RB[:, 1, tok], SQV["ident"])
                ins.then_inc(sem("rstd"), 1)

            def behind(k, n0, banks):
                ws = [chunk(n0 + g, 0, 0) for g in range(2)]
                for t in range(DT):
                    pe.wait_ge(sem("split_lo"), SPLIT_TB[k] + t + 1)
                    for g in range(2):
                        ins = split_product(PS[:, banks[g], :], ws[g], (t,), (t,), (XH, XL), first=t == 0,
                                            last=t == DT - 1)
                        if t == DT - 1:
                            used(ins)

            def rotate(q, src, perm, bank):
                mm(PS[:, bank, :], SQV[perm], src, start=True, stop=True).then_inc(sem("rot_mm"), 1)

            def token_major(n0, nchunks, tiles_per, width, moving, banks, rotations):
                for j in range(nchunks):
                    w = chunk(n0 + j, 0, 0)
                    for b in range(NB):
                        if j == 0 and b == 2:
                            pe.wait_ge(sem("rot_read"), rotations)
                        for r in range(tiles_per):
                            t = j * tiles_per + r
                            lw = 1024 // tiles_per
                            wh, wl = HI[w][:, r * lw:r * lw + width], LO[w][:, r * lw:r * lw + width]
                            xh, xl = (m[:, t, b * P:(b + 1) * P] for m in moving)
                            end = j == nchunks - 1 and r == tiles_per - 1
                            bank = PS[:, banks[b], 0:width]
                            mm(bank, xh, wh, start=t == 0, stop=False)
                            mm(bank, xh, wl, start=False, stop=False)
                            ins = mm(bank, xl, wh, start=False, stop=end)
                    used(ins)
                released["v_copied"] += NB

            def index_scores(first):
                if first == 0:
                    pe.wait_ge(sem("ik_spread"), 4)
                    pe.wait_ge(sem("rotated"), len(ROT1) + 2 + 2)
                else:
                    pe.wait_ge(sem("dots_read"), first)
                for u in (first, first + 1):
                    i, h = 1 + u // 8, u % 8
                    b = 32 * (h % 4)
                    mm(PS[:, 6 + u % 2, 0:P * (i + 1)], IQ[b:b + 32, h // 4, i * P:(i + 1) * P],
                       IK[b:b + 32, 0:P * (i + 1)], start=True, stop=True).then_inc(sem("dots"), 1)

            def project_in2():
                n0 = FIRST["in2"]
                all_released()
                e0 = released["in_copied"]

                def spread(k):
                    q = NRM2.index(k)
                    pe.wait_ge(sem("hexpanded"), q + 1)
                    if q >= 1:
                        pe.wait_ge(sem("hnormed"), q)
                    for b in range(NB):
                        tok = slice(b * P, (b + 1) * P)
                        ins = nc.tensor.transpose(PS[:, 4, tok], RB[:, q % 2, tok], SQV["ident"])
                    ins.then_inc(sem("hspread"), 1)

                def head_sums(k):
                    q = NRM2.index(k)
                    pe.wait_ge(sem("hsq"), q + 1)
                    if q >= 1:
                        pe.wait_ge(sem("hstd"), q)
                    for b in range(NB):
                        c = 8 * (q % 2) + 2 * b
                        ins = mm(PS[:, 3, c:c + 2], SQ[:, q % 2, b * P:(b + 1) * P], SQV["halves"][:, 0:P:64],
                                 start=True, stop=True)
                    ins.then_inc(sem("hsum"), 1)

                def rotation(k):
                    q = ROT_BASE["in2"] + ROT2.index(k)
                    if IN2[k][0] == "rope":
                        pe.wait_ge(sem("in_copied"), e0 + k + 1)
                    else:
                        pe.wait_ge(sem("hnormed"), NRM2.index(k) + 1)
                    if q > ROT_BASE["in2"]:
                        pe.wait_ge(sem("rot_read"), q)
                    if q == ROT_BASE["in2"] + 2:
                        pe.wait_ge(sem("values_copied"), 1)
                    rotate(q, IN2[k][1], "rot_m" if IN2[k][0] == "misc" else IN2[k][3], 5)

                def turn_values():
                    pe.wait_ge(sem("in_copied"), e0 + 3)
                    pe.wait_ge(sem("rot_read"), ROT_BASE["in2"] + 2)
                    for b in range(NB):
                        ins = nc.tensor.transpose(PS[:, 5, b * 72:(b + 1) * 72], VW[0:72, b * P:(b + 1) * P],
                                                  SQV["ident"][0:72, 0:72])
                    ins.then_inc(sem("values_turned"), 1)

                for j in range(IN2_STEPS):
                    amid = {}
                    if j == 5:
                        amid[5] = turn_values
                    if j - 3 in NRM2:
                        amid[1] = lambda: spread(j - 3)
                    if j - 2 in NRM2:
                        amid[2] = lambda: head_sums(j - 2)
                    turning = [k for k in ROT2 if rot_at(IN2, k) == j]
                    if turning:
                        amid[4] = lambda: rotation(turning[0])
                    if j >= DOTS_FROM:
                        for r, b in enumerate((3, 7)):
                            amid[b] = lambda r=r: index_scores(4 * (j - DOTS_FROM) + 2 * r)
                    if j == 0:
                        behind(5, n0, (0, 1))
                    if j < 2:
                        continue
                    w = chunk(n0 + j, 0, 0)
                    if j == len(IN2):
                        pe.wait_ge(sem("in_copied"), e0 + len(IN2))
                        pe.wait_ge(sem("rot_read"), ROT_BASE["in2"] + len(ROT2))
                    if j >= len(IN2):
                        used(value_rows(j - len(IN2), w, amid))
                        continue
                    if j >= 3:
                        pe.wait_ge(sem("in_copied"), e0 + j - 2)
                    used(split_product(PS[:, j % 3, :], w, range(8), range(8), (XH, XL), between=amid))
                released["in_copied"] += len(IN2)
                released["v_copied"] += NB

            def value_rows(c, w, amid):
                for b in range(NB):
                    for r in range(2):
                        if 2 * b + r in amid:
                            amid[2 * b + r]()
                        t = 2 * c + r
                        wh, wl = HI[w][:, r * S:(r + 1) * S], LO[w][:, r * S:(r + 1) * S]
                        xh, xl = (m[:, t, b * P:(b + 1) * P] for m in (XH, XL))
                        bank = PS[:, FV_BANKS[b], :]
                        mm(bank, xh, wh, start=t == 0, stop=False)
                        mm(bank, xh, wl, start=False, stop=False)
                        ins = mm(bank, xl, wh, start=False, stop=t == DT - 1)
                return ins

            def branch2():
                for m in range(DT):
                    w = chunk(FIRST["branch2"] + m, 0, 0)
                    if m == 0:
                        pe.wait_ge(sem("turned_lo"), 12)
                    if m >= 2:
                        pe.wait_ge(sem("branch_scaled"), DT + m - 1)
                    split_product(PS[:, BRANCH_BANKS[m % 2][0], :], w, range(4), range(4), (OTH2, OTL2))
                    if m == 0:
                        pe.wait_ge(sem("turned_lo"), 16)
                    used(split_product(PS[:, BRANCH_BANKS[m % 2][1], :], w, range(4, 8), range(4, 8),
                                       (OTH2, OTL2)))
                released["branch_scaled"] += DT

            def ada_sum(g, bank):
                pe.wait_ge(sem("ada_added"), 8 * g + 8)
                if g:
                    pe.wait_ge(sem("mod"), g)
                for t in range(8):
                    ins = mm(PS[:, bank, t:t + 1], ACC[:, t * P:(t + 1) * P], SQV["ones"][:, 0:1],
                             start=True, stop=True)
                ins.then_inc(sem("ada_summed"), 1)

            def project_in1():
                n0 = FIRST["in1"]
                for j in range(len(IN1) + 2):
                    if j - 2 in ROT1:
                        q = ROT1.index(j - 2)
                        pe.wait_ge(sem("in_copied"), j - 1)
                        if q >= 2:
                            pe.wait_ge(sem("rot_read"), q - 1)
                        rotate(q, IN1[j - 2][1], IN1[j - 2][3], 4 + q % 2)
                    if j == 5:
                        norm_sums(1)
                    if j == 7:
                        norm_spread(1)
                    if j == 8:
                        norm_sums(2)
                    if j == 11:
                        norm_spread(2)
                    if j == 0:
                        behind(0, n0, (0, 1))
                    elif 2 <= j < len(IN1):
                        w = chunk(n0 + j, 0, 0)
                        if j >= 4:
                            pe.wait_ge(sem("in_copied"), j - 3)
                        used(split_product(PS[:, j % 4, :], w, range(8), range(8), (XH, XL)))
                released["in_copied"] += len(IN1)

            def diff_attention():
                for s in range(NPAIR + 3):
                    if s < NPAIR:
                        p, i = divmod(s, NB)
                        n = P * (i + 1)
                        if s >= 2:
                            pe.wait_ge(sem("probs"), 2 * s - 2)
                        for r in range(2):
                            bank = PS[:, SCORE_BANKS[s % 2][r], :]
                            mm(bank[:, 0:n], q_diff(2 * p + r, i), k_diff(2 * p + r, n), start=True, stop=False)
                            mm(bank[:, n - P:n], IDENT_B[:], CAUSAL_B[:], start=False, stop=True)\
                                .then_inc(sem("scores"), 1)
                    if 2 <= s < NPAIR + 2:
                        w = s - 2
                        if w == 0:
                            pe.wait_ge(sem("v_copied"), NB)
                        pe.wait_ge(sem("combined"), w + 1)
                        if w >= 2:
                            pe.wait_ge(sem("pt_copied"), w - 1)
                        for kb in range(w % NB + 1):
                            ins = nc.tensor.transpose(PS[:, 3 + w % 2, kb * P:(kb + 1) * P],
                                                      P1[w % 3][:, kb * P:(kb + 1) * P], SQV["ident"])
                        ins.then_inc(sem("pt"), 1)
                    if s >= 3:
                        w = s - 3
                        p, i = divmod(w, NB)
                        pe.wait_ge(sem("pt_copied"), w + 1)
                        if w >= 2:
                            pe.wait_ge(sem("onorm"), w - 1)
                        for kb in range(i + 1):
                            ins = mm(PS[:, 5 + w % 2, 0:P], PT1[w % 2][:, kb * P:(kb + 1) * P],
                                     DV[:, kb, p * P:(p + 1) * P], start=kb == 0, stop=kb == i)
                        ins.then_inc(sem("pv"), 1)

            def attention(a):
                at_ = ATT[a]
                n0 = FIRST["gates2"] + DT * (a - 2)

                def gate_blocks(u, part):
                    if a < 2 or u >= NU:
                        return
                    if u % 4 == 0:
                        blocks = ((), (0, 1))[part]
                    else:
                        blocks = (2 * (u % 4) + part,)
                    if not blocks:
                        return
                    if blocks[0] == 0:
                        chunk(n0 + u // 4, 0, 0)
                        if u or a == 3:
                            pe.wait_ge(sem("gate_copied"), DT * (a - 2) + u // 4)
                    ins = split_product(PS[:, 7, :], (n0 + u // 4) % 3, blocks, blocks, (XH, XL),
                                        first=blocks[0] == 0, last=blocks[0] == 7)
                    if blocks[0] == 7:
                        used(ins)

                for u in range(NU + 3):
                    if u < NU:
                        h, i = divmod(u, NB)
                        n = P * (i + 1)
                        if u >= 3:
                            pe.wait_ge(sem("probs"), NU * a + u - 2)
                        if a == 2 and u < NB:
                            pe.wait_ge(sem("v_copied"), 2 * NB + u + 1)
                        mm(PS[:, u % 3, 0:n], at_["q"](h, i), at_["k"](h, n), start=True, stop=False)
                        if a == 3:
                            ins = mm(PS[:, u % 3, 0:n], IDENT_B[:], MASK[i][:], start=False, stop=True)
                        else:
                            ins = mm(PS[:, u % 3, n - P:n], IDENT_B[:], CAUSAL_B[:], start=False, stop=True)
                        ins.then_inc(sem("scores"), 1)
                    gate_blocks(u, 0)
                    if 2 <= u < NU + 2:
                        v = u - 2
                        i = v % NB
                        if a == 1 and u == 2:
                            pe.wait_ge(sem("v_copied"), 2 * NB)
                        pe.wait_ge(sem("probs"), NU * a + v + 1)
                        if v >= 2:
                            pe.wait_ge(sem("pt_copied"), AFTER[a] + v - 1)
                        for kb in range(i + 1):
                            ins = nc.tensor.transpose(PS[:, 3 + v % 2, kb * P:(kb + 1) * P],
                                                      at_["P"][v % 3][:, kb * P:(kb + 1) * P], SQV["ident"])
                        ins.then_inc(sem("pt"), 1)
                    if a == 3 and u >= NU:
                        pe.wait_ge(sem("gate_copied"), 2 * DT)
                        turn(2, (u - NU,))
                    gate_blocks(u, 1)
                    if u >= 3:
                        v = u - 3
                        h, i = divmod(v, NB)
                        pe.wait_ge(sem("pt_copied"), AFTER[a] + v + 1)
                        if v >= 2:
                            pe.wait_ge(sem("onorm"), AFTER[a] + v - 1)
                        for kb in range(i + 1):
                            ins = mm(PS[:, 5 + v % 2, 0:at_["dv"]], at_["PT"][v % 2][:, kb * P:(kb + 1) * P],
                                     at_["v"](kb, h), start=kb == 0, stop=kb == i)
                        ins.then_inc(sem("pv"), 1)

            def turn(a, tiles=range(4)):
                src, _, _, _, g = OUT_T[a]
                for f in tiles:
                    k = 4 * g + f
                    if k % 8 >= 4:
                        pe.wait_ge(sem("turned_lo"), k - 3)
                    if a == 0:
                        pe.wait_ge(sem("diff_normed"), f + 1)
                    for i in range(NB):
                        ins = nc.tensor.transpose(PS[:, TURN_BANKS[k], i * P:(i + 1) * P],
                                                  src[:, i, f * P:(f + 1) * P], SQV["ident"])
                    ins.then_inc(sem("turned"), 1)

            def merge(b, oh, ol):
                all_released()
                n0 = FIRST[f"merge{b + 1}"]

                def pair(i):
                    for j in range(2):
                        if not isinstance(i, int):
                            pe.wait_ge(sem("branch_scaled"), 2 * i + (DT * b + j - 1))
                        for g in range(2):
                            w = chunk(n0 + 3 * j + g, 6, i)
                            used(split_product(PS[:, 4 * j + g, :], w, range(8), range(8), (XH, XL)))
                        if isinstance(i, int) and j == 0:
                            pe.wait_ge(sem("onorm"), AFTER[2])
                            turn(1)
                            turn(0)
                            pe.wait_ge(sem("turned_lo"), 4)
                        w = chunk(n0 + 3 * j + 2, 6, i)
                        split_product(PS[:, 4 * j + 2, :], w, range(4), range(4), (oh, ol))
                        if isinstance(i, int) and j == 0:
                            pe.wait_ge(sem("turned_lo"), 8)
                        used(split_product(PS[:, 4 * j + 3, :], w, range(4, 8), range(4, 8), (oh, ol)))

                pair(0)
                with pe.Fori(1, 4) as i:
                    pair(i)
                released["branch_scaled"] += DT

            def out_proj(b, mh, ml):
                pe.wait_ge(sem("branch_scaled"), DT * b + DT - 1)
                n0 = FIRST[f"out{b + 1}"]
                ws = [chunk(n0 + g, 0, 0) for g in range(2)]
                for tiles in (range(DT - 1), (DT - 1,)):
                    pe.wait_ge(sem("merged_lo"), DT * b + tiles[-1] + 1)
                    for g in range(2):
                        ins = split_product(PS[:, g, :], ws[g], tiles, tiles, (mh, ml), first=tiles[0] == 0,
                                            last=tiles[-1] == DT - 1)
                        if tiles[-1] == DT - 1:
                            used(ins)
                all_released()
                if b == 0:
                    ada_sum(0, 5)
                for m in range(2, DT):
                    w = chunk(n0 + m, 0, 0)
                    if m >= 4:
                        pe.wait_ge(sem("x_added"), XA[f"out{b + 1}"] + m - 3)
                    used(split_product(PS[:, m % 4, :], w, range(8), range(8), (mh, ml)))
                released["x_added"] += DT

            def ffn(f, k):
                all_released()
                n0 = FIRST[f"up{f + 1}"]

                def three(i, tiles=3):
                    for j in range(tiles):
                        if not (isinstance(i, int) and i == 0):
                            pe.wait_ge(sem("hid"), 3 * i + (FT * f + j - 2))
                        if isinstance(i, int) and i == 0 and j == 0:
                            behind(k, n0, (0, 1))
                            continue
                        for g in range(2):
                            w = chunk(n0 + 2 * j + g, 6, i)
                            used(split_product(PS[:, 2 * j + g, :], w, range(8), range(8), (XH, XL)))
                    if f == 0 and tiles == 3:
                        ada_sum_loop(i)

                def ada_sum_loop(i):
                    pe.wait_ge(sem("ada_added"), 8 * i + 24)
                    pe.wait_ge(sem("mod"), i + 2)
                    for t in range(8):
                        ins = mm(PS[:, 7, t:t + 1], ACC[:, t * P:(t + 1) * P], SQV["ones"][:, 0:1],
                                 start=True, stop=True)
                    ins.then_inc(sem("ada_summed"), 1)

                three(0)
                with pe.Fori(1, 7) as i:
                    three(i)
                three(7, tiles=1)
                pe.wait_ge(sem("hid"), FT * f + FT - 2)
                released["hid"] += FT
                n0 = FIRST[f"down{f + 1}"]

                def two(i):
                    for j in range(2):
                        if not (isinstance(i, int) and i == 0):
                            pe.wait_ge(sem("x_added"), 2 * i + (XA[f"down{f + 1}"] + j - 1))
                        for g, blocks in enumerate(LAST_DOWN):
                            w = chunk(n0 + 3 * j + g, 6, i)
                            if isinstance(i, int) and i == 0 and j == 0:
                                pe.wait_ge(sem("hid_lo"), FT * f + 8 * g + blocks)
                            used(split_product(PS[:, 2 + j, :], w, range(blocks), range(8 * g, 8 * g + blocks),
                                               (HIDH, HIDL), first=g == 0, last=g == 2))

                two(0)
                with pe.Fori(1, 4) as i:
                    two(i)
                released["x_added"] += DT

            pe.wait_ge(sem("squares_loaded"), 16)
            norm(0)
            project_in1()
            all_released()
            pe.wait_ge(sem("normed"), NTB[3])
            token_major(FIRST["dv1"], 4, 2, 512, (XH, XL), DV_BANKS, len(ROT1))
            pe.wait_ge(sem("rotated"), len(ROT1))
            diff_attention()
            pe.wait_ge(sem("split_lo"), SPLIT_TB[3])
            for j in range(3):
                w = chunk(FIRST["uq"] + j, 0, 0)
                for r in range(2):
                    m = 2 * j + r
                    if m == 5:
                        pe.wait_ge(sem("onorm"), AFTER[1])
                    ins = split_product(PS[:, m, :], w, range(3 * r, 3 * r + 3), range(3), (LQH, LQL))
                used(ins)
            w = chunk(FIRST["uk"], 0, 0)
            for m in range(4):
                pe.wait_ge(sem("proj_copied"), m + 1)
                ins = split_product(PS[:, m, :], w, range(2 * m, 2 * m + 2), range(2), (LKH, LKL))
                if m in (1, 2):
                    r = m - 1
                    pe.wait_ge(sem("proj_copied"), 5 + r)
                    rotate(ROT_BASE["uq"] + r, Y[:, r, :], "rot_p", 6 + r)
            used(ins)
            token_major(FIRST["uv"], 1, 2, 512, (LKH, LKL), UV_BANKS, ROT_BASE["uq"] + 2)
            released["proj_copied"] += 10
            all_released(but=("v_copied",))
            pe.wait_ge(sem("q_rotated"), 2)
            pe.wait_ge(sem("k_shared"), 8)
            attention(1)
            merge(0, OTH1, OTL1)
            out_proj(0, MH1, ML1)
            norm(3)
            ada_sum(1, 7)
            ffn(0, 3)
            norm(4)
            ffn(1, 4)
            norm(5)
            project_in2()
            all_released(but=("v_copied",))
            pe.wait_ge(sem("hstd"), len(NRM2))
            pe.wait_ge(sem("hnormed"), len(NRM2))
            pe.wait_ge(sem("dots_read"), NDOTS)
            pe.wait_ge(sem("f_rows"), 32)
            attention(2)
            pe.wait_ge(sem("rotated"), ALL_ROTATED)
            pe.wait_ge(sem("selected"), 4)
            attention(3)
            turn(2, (3,))
            for f in range(4):
                pe.wait_ge(sem("onorm"), AFTER[3] + 2 * NB * (f + 1))
                turn(3, (f,))
            branch2()
            out_proj(1, MH2, ML2)
            norm(6)
            ffn(2, 6)

        @block.scalar
        def _(act):
            A = nc.scalar.activation

            def split_hi(n0, step=0, i=0):
                n0 += 2
                if isinstance(i, int):
                    n0, step, i = n0 + step * i, 0, 0
                    if n0 >= NCH:
                        return
                if step == 0:
                    act.wait_ge(sem(f"raw{n0 % 3}"), 16 * (n0 // 3 + 1))
                    if n0 >= 3:
                        act.wait_ge(sem("chunk_used"), n0 - 2)
                else:
                    act.wait_ge(sem(f"raw{n0 % 3}"), (16 * step // 3) * i + 16 * (n0 // 3 + 1))
                    act.wait_ge(sem("chunk_used"), step * i + (n0 - 2))
                A(HI[n0 % 3][:], RAW[n0 % 3][:], ACT.Copy).then_inc(sem("hi_ready"), 1)

            def square(k, t, i=0):
                src = NORMS[k][1]
                if isinstance(i, int):
                    t, i = t + 2 * i, 0
                    if t >= 2:
                        act.wait_ge(sem("sum_added"), SAB[k] + t - 1)
                    elif k:
                        act.wait_ge(sem("sq_summed"), k)
                else:
                    act.wait_ge(sem("sum_added"), 2 * i + (SAB[k] + t - 1))
                A(SQ[:, t % 2:t % 2 + 1, :], src[:, bass.ds(2 * i + t, 1), :], ACT.Square).then_inc(sem("squared"), 1)

            def square_g(t, i=0):
                if isinstance(i, int):
                    t, i = t + 2 * i, 0
                if not isinstance(i, int) or t >= 2:
                    act.wait_ge(sem("g_sum_added"), 2 * i + t)
                A(Y[:, t % 2:t % 2 + 1, :], X[:, bass.ds(2 * i + t, 1), :], ACT.Square,
                  scale=CO[:, bass.ds(2 * i + (COLS["g_final"][0] + t), 1)]).then_inc(sem("g_squared"), 1)

            def stds(k):
                if k == 4:
                    act.wait_ge(sem("fused_sums"), 2)
                    A(FSTD[:, 0:4], FV[:, 0:4], ACT.Sqrt, bias=EPS2C, scale=1.0 / D).then_inc(sem("fused_std"), 1)
                    A(FSTD[:, 4:8], FV[:, 4:8], ACT.Sqrt, bias=EPSC, scale=1.0 / D).then_inc(sem("stds"), 1)
                    return
                act.wait_ge(sem("sq_summed"), k + 1)
                A(NSTD, PS[:, 7, 8:12], ACT.Sqrt, bias=EPSC, scale=1.0 / NORMS[k][2]).then_inc(sem("stds"), 1)

            def high(k, t):
                g, oh = NORMS[k][3:5]
                act.wait_ge(sem("normed"), NTB[k] + t + 1)
                if isinstance(g, str):
                    A(oh[:, t, :], Y[:, t % 2, :], ACT.Copy).then_inc(sem("split_hi"), 1)
                else:
                    shift = 3 * g * DT + t
                    A(oh[:, t, :], Y[:, t % 2, :], ACT.Identity, bias=MOD[:, shift:shift + 1])\
                        .then_inc(sem("split_hi"), 1)

            def norm(k, first=0):
                nt, src, width, g, oh, ol = NORMS[k]
                for t in range(first, nt):
                    square(k, t)
                    if k == 4:
                        square_g(t)
                stds(k)
                for t in range(nt):
                    high(k, t)

            def table(k, tab):
                act.wait_ge(sem("angle"), k + 1)
                A(tab[:, 1, :], Y[:, 0, :], ACT.Sin).then_inc(sem("sin"), 1)
                A(Y[:, 1, :], Y[:, 0, :], ACT.Abs).then_inc(sem("absolute"), 1)
                act.wait_ge(sem("absolute"), k + 1)
                A(tab[:, 0, :], Y[:, 1, :], ACT.Sin, bias=PIH, scale=-1.0).then_inc(sem("table"), 1)

            def token_copies(n0, nchunks, dest, width, banks):
                for j in range(nchunks):
                    split_hi(n0 + j)
                if dest is DV:
                    act.wait_ge(sem("lams_used"), 2)
                    A(LAM[:, 2:4], LAM[:, 0:2], ACT.Exp).then_inc(sem("lam_exp"), 1)
                act.wait_ge(sem("chunk_used"), n0 + nchunks)
                for b in range(NB):
                    A(dest[:, b, :], PS[:, banks[b], 0:width], ACT.Copy).then_inc(sem("v_copied"), 1)

            def latents(j):
                if j == 3:
                    table(0, TAB_A1)
                if j == 6:
                    table(1, TAB_P1)
                if j == 6:
                    stds(1)
                for k, t, step in ((1, 0, 3), (1, 1, 3), (1, 2, 4), (2, 0, 6), (2, 1, 6)):
                    if step == j:
                        act.wait_ge(sem("in_copied"), 3 * (k - 1) + t + 1)
                        square(k, t)
                if j == 9:
                    stds(2)
                if 8 <= j < 11:
                    high(1, j - 8)
                if 12 <= j < 14:
                    high(2, j - 12)

            def project_in1():
                n0 = FIRST["in1"]
                for j, kind in enumerate(IN1):
                    split_hi(n0 + j)
                    latents(j)
                    act.wait_ge(sem("chunk_used"), n0 + j + 1)
                    A(kind[1], PS[:, j % 4, :], ACT.Copy, scale=kind[4] if len(kind) > 4 else 1.0)\
                        .then_inc(sem("in_copied"), 1)

            def project_in2():
                n0 = FIRST["in2"]
                for j in range(IN2_STEPS):
                    split_hi(n0 + j)
                    if j - 2 in NRM2:
                        q = NRM2.index(j - 2)
                        act.wait_ge(sem("hsum"), q + 1)
                        if q >= 2:
                            act.wait_ge(sem("hexpanded"), q - 1)
                        A(HSTD[q % 2], PS[:, 3, 8 * (q % 2):8 * (q % 2) + 8], ACT.Sqrt, bias=EPSC, scale=1.0 / 64)\
                            .then_inc(sem("hstd"), 1)
                    if j == FORGET_AT:
                        act.wait_ge(sem("f_z"), 1)
                        A(FW[0:8, 1, :], FW[0:8, 0, :], ACT.Abs).then_inc(sem("f_act"), 1)
                        act.wait_ge(sem("f_act"), 1)
                        A(FW[0:8, 2, :], FW[0:8, 1, :], ACT.Exp, scale=-1.0).then_inc(sem("f_act"), 1)
                        act.wait_ge(sem("f_act"), 2)
                        A(FW[0:8, 3, :], FW[0:8, 2, :], ACT.Ln, bias=1.0).then_inc(sem("f_act"), 1)
                    if j >= DOTS_FROM:
                        for u in range(4 * (j - DOTS_FROM), 4 * (j - DOTS_FROM) + 4):
                            n = P * (2 + u // 8)
                            act.wait_ge(sem("dots"), u + 1)
                            if u >= 2:
                                act.wait_ge(sem("scored"), u - 1)
                            A(Y[:, u % 2, 0:n], PS[:, 6 + u % 2, 0:n], ACT.Relu, scale=32 ** -0.5)\
                                .then_inc(sem("dots_read"), 1)
                    if j == IN2_STEPS - 1:
                        A(SM[:, 85:86], EPSC, ACT.Exp).then_inc(sem("table_loaded"), 1)
                    act.wait_ge(sem("chunk_used"), n0 + j + 1)
                    if j in NRM2:
                        q = NRM2.index(j)
                        if q >= 2:
                            act.wait_ge(sem("hsum"), q - 1)
                        A(SQ[:, q % 2, :], PS[:, j % 3, :], ACT.Square).then_inc(sem("hsq"), 1)
                        if q >= 5:
                            act.wait_ge(sem("hnormed"), q - 3)
                        dst = MISC[:, :] if IN2[j][0] == "misc" else R[:, j % 4, :]
                        A(dst, PS[:, j % 3, :], ACT.Copy).then_inc(sem("in_copied"), 1)
                    elif j < len(IN2):
                        dst = VW[:, :] if IN2[j][0] == "dvw" else IN2[j][1]
                        A(dst, PS[:, j % 3, :], ACT.Copy).then_inc(sem("in_copied"), 1)
                    if j == 5:
                        act.wait_ge(sem("values_turned"), 1)
                        A(DVW[:].rearrange("p b n -> p (b n)"), PS[:, 5, 0:72 * NB], ACT.Copy)\
                            .then_inc(sem("values_copied"), 1)
                for b in range(NB):
                    A(VF[:, b, :], PS[:, FV_BANKS[b], :], ACT.Copy).then_inc(sem("v_copied"), 1)

            def branch2():
                for m in range(DT):
                    split_hi(FIRST["branch2"] + m)
                    for g in range(2):
                        A(GATE2[g][m], GATE2[g][m], ACT.Sigmoid).then_inc(sem("gated"), 1)
                    if m == 0:
                        continue
                    act.wait_ge(sem("merged"), DT + m)
                    A(MH2[:, m - 1, :], Y[:, (m - 1) % 2, :], ACT.Copy).then_inc(sem("merged_hi"), 1)
                act.wait_ge(sem("merged"), 2 * DT)
                A(MH2[:, DT - 1, :], Y[:, (DT - 1) % 2, :], ACT.Copy).then_inc(sem("merged_hi"), 1)

            def diff_attention():
                for s in range(NPAIR + 2):
                    if s >= 2:
                        w = s - 2
                        n = P * (w % NB + 1)
                        act.wait_ge(sem("pt"), w + 1)
                        if w >= 2:
                            act.wait_ge(sem("pv"), w - 1)
                        A(PT1[w % 2][:, 0:n], PS[:, 3 + w % 2, 0:n], ACT.Copy).then_inc(sem("pt_copied"), 1)
                    if s < NPAIR:
                        n = P * (s % NB + 1)
                        if s >= 2:
                            act.wait_ge(sem("combined"), s - 1)
                        for r in range(2):
                            c = 2 * (s % 2) + r
                            act.wait_ge(sem("smax"), 2 * s + r + 1)
                            A((P1B if r else P1)[s % 3][:, 0:n], PS[:, SCORE_BANKS[s % 2][r], 0:n], ACT.Exp,
                              bias=NMX[:, c:c + 1], accum_out=RSU[:, c:c + 1]).then_inc(sem("probs"), 1)

            def attention(a):
                at_ = ATT[a]
                n0 = FIRST["gates2"] + DT * (a - 2)
                for u in range(NU + 4):
                    if a >= 2 and u % 4 == 0 and u <= NU:
                        if u:
                            m = u // 4 - 1
                            act.wait_ge(sem("chunk_used"), n0 + m + 1)
                            A(GATE2[a - 2][m], PS[:, 7, :], ACT.Copy).then_inc(sem("gate_copied"), 1)
                    if a == 2 and u >= 4:
                        h, i = divmod(u - 4, NB)
                        act.wait_ge(sem("sum_inverse"), u - 3)
                        act.wait_ge(sem("pv"), AFTER[a] + u - 3)
                        A(OF[:, i, h * 64:h * 64 + 64], PS[:, 5 + u % 2, 0:64], ACT.Copy,
                          scale=RIN[:, u % 4:u % 4 + 1]).then_inc(sem("onorm"), 1)
                    if a >= 2 and u % 4 == 1 and u < NU:
                        split_hi(n0 + u // 4)
                    if 2 <= u < NU + 2:
                        v = u - 2
                        n = P * (v % NB + 1)
                        act.wait_ge(sem("pt"), AFTER[a] + v + 1)
                        if v >= 2:
                            act.wait_ge(sem("pv"), AFTER[a] + v - 1)
                        A(at_["PT"][v % 2][:, 0:n], PS[:, 3 + v % 2, 0:n], ACT.Copy).then_inc(sem("pt_copied"), 1)
                    if a == 3 and NU <= u < NU + 3:
                        turn(2, (u - NU,))
                    if u < NU:
                        n = P * (u % NB + 1)
                        act.wait_ge(sem("smax"), NU * a + u + 1)
                        if u >= 4:
                            act.wait_ge(sem("onorm"), AFTER[a] + u - 3)
                        A(at_["P"][u % 3][:, 0:n], PS[:, u % 3, 0:n], ACT.Exp, bias=NMX[:, u % 4:u % 4 + 1],
                          accum_out=RSU[:, u % 4:u % 4 + 1]).then_inc(sem("probs"), 1)
                    if a == 1 and 4 <= u < 20:
                        k = u - 4
                        if k:
                            act.wait_ge(sem("diff_ss"), k)
                        A(T[:, 0, 0:P], OD[:, k // 4, (k % 4) * P:(k % 4 + 1) * P], ACT.Square,
                          accum_out=SSD[:, k:k + 1]).then_inc(sem("diff_ss"), 1)

            def turn(a, tiles=range(4)):
                src, oh, ol, f0, g = OUT_T[a]
                for f in tiles:
                    k = 4 * g + f
                    act.wait_ge(sem("turned"), k + 1)
                    A(oh[:, f0 + f, :], PS[:, TURN_BANKS[k], :], ACT.Copy,
                      scale=GM[:, 0:1] if a == 0 else 1.0).then_inc(sem("turned_hi"), 1)

            def merge(b):
                n0 = FIRST[f"merge{b + 1}"]

                def pair(i):
                    for j in range(2):
                        for g in range(2):
                            split_hi(n0 + 3 * j + g, 6, i)
                            act.wait_ge(sem("chunk_used"), 6 * i + (n0 + 3 * j + g + 1))
                            if b == 0:
                                bias = CO[:, bass.ds(COLS["b_gate"][0] + DT * g + j + 2 * i, 1)]
                            else:
                                bias = 0.0
                            if not (isinstance(i, int) and 8 * b + 2 * i + j == 0):
                                act.wait_ge(sem("merged"), 2 * i + (DT * b + j))
                            A(T[:, g, :], PS[:, 4 * j + g, :], ACT.Sigmoid, bias=bias).then_inc(sem("gate"), 1)
                        if isinstance(i, int) and j == 0:
                            turn(1)
                        split_hi(n0 + 3 * j + 2, 6, i)
                        if isinstance(i, int) and j == 0:
                            turn(0)
                        act.wait_ge(sem("merged"), 2 * i + (8 * b + j + 1))
                        A((MH1, MH2)[b][:, bass.ds(2 * i + j, 1), :], Y[:, j:j + 1, :], ACT.Copy)\
                            .then_inc(sem("merged_hi"), 1)

                pair(0)
                with act.Fori(1, 4) as i:
                    pair(i)

            def out_proj(b):
                k = (3, 6)[b]
                for m in range(DT):
                    split_hi(FIRST[f"out{b + 1}"] + m)
                    if m:
                        act.wait_ge(sem("x_added"), XA[f"out{b + 1}"] + m)
                        square(k, m - 1)
                act.wait_ge(sem("x_added"), XA[f"out{b + 1}"] + DT)
                norm(k, first=DT - 1)

            def ffn(f):
                n0 = FIRST[f"up{f + 1}"]

                def three(i, tiles=3):
                    for j in range(tiles):
                        split_hi(n0 + 2 * j, 6, i)
                        if not (isinstance(i, int) and i == 0 and j == 0):
                            hidden(3 * i + (j - 1))
                        act.wait_ge(sem("chunk_used"), 6 * i + (n0 + 2 * j + 1))
                        A(SILU[j], PS[:, 2 * j, :], ACT.Silu).then_inc(sem("silu"), 1)
                        split_hi(n0 + 2 * j + 1, 6, i)

                def hidden(t):
                    act.wait_ge(sem("hid"), t + (FT * f + 1))
                    A(HIDH[:, bass.ds(t, 1), :], Y[:, 0:1, :], ACT.Copy).then_inc(sem("hid_hi"), 1)

                three(0)
                with act.Fori(1, 7) as i:
                    three(i)
                three(7, tiles=1)
                hidden(FT - 1)
                n0 = FIRST[f"down{f + 1}"]

                def two(i):
                    for j in range(2):
                        for g in range(3):
                            split_hi(n0 + 3 * j + g, 6, i)
                        if f < 2 and not (isinstance(i, int) and i == 0 and j == 0):
                            act.wait_ge(sem("x_added"), 2 * i + (XA[f"down{f + 1}"] + j))
                            square(4 + f, j - 1, i)
                            if f == 0:
                                square_g(j - 1, i)

                if f == 0:
                    act.wait_ge(sem("hid_lo"), FT)
                two(0)
                if f == 1:
                    table(2, TAB_A2)
                    table(3, TAB_I2)
                with act.Fori(1, 3) as i:
                    two(i)
                two(3)
                if f < 2:
                    act.wait_ge(sem("x_added"), XA[f"down{f + 1}"] + DT)
                    norm(4 + f, first=DT - 1)

            act.wait_ge(sem("eps_set"), 1)
            act.wait_ge(sem("columns_loaded"), 16)
            A(CND, col("cond", 0, DT), ACT.Silu).then_inc(sem("cond_ready"), 1)
            for t in range(DT):
                if t % 2 == 0:
                    act.wait_ge(sem(f"x_loaded{t // 2}"), 16)
                square(0, t)
            split_hi(-2)
            split_hi(-1)
            norm(0, first=DT)
            project_in1()
            token_copies(FIRST["dv1"], 4, DV, 512, DV_BANKS)
            diff_attention()
            for j in range(3):
                split_hi(FIRST["uq"] + j)
                act.wait_ge(sem("chunk_used"), FIRST["uq"] + j + 1)
                for r in range(2):
                    m = 2 * j + r
                    if m < 4:
                        A(QM[0:64, 2 * m, :], PS[0:64, m, :], ACT.Copy, scale=MLA_SCALE).then_inc(sem("half_copied"), 1)
                        A(QM[0:64, 2 * m + 1, :], PS[64:128, m, :], ACT.Copy, scale=MLA_SCALE).then_inc(sem("proj_copied"), 1)
                    else:
                        A(Y[:, m - 4, :], PS[:, m, :], ACT.Copy, scale=MLA_SCALE).then_inc(sem("proj_copied"), 1)
            split_hi(FIRST["uk"])
            act.wait_ge(sem("chunk_used"), FIRST["uk"] + 1)
            for m in range(4):
                for r in range(2):
                    h = 2 * m + r
                    A(KM[h // 4][0:64, h % 4, :], PS[64 * r:64 * r + 64, m, :], ACT.Copy)\
                        .then_inc(sem("proj_copied" if r else "half_copied"), 1)
            token_copies(FIRST["uv"], 1, VM, 512, UV_BANKS)
            attention(1)
            act.wait_ge(sem("diff_ss"), 16)
            A(RSD, SSD, ACT.Sqrt, bias=EPSC, scale=1.0 / P).then_inc(sem("diff_std"), 1)
            act.wait_ge(sem("g_sub_scaled"), 1)
            merge(0)
            out_proj(0)
            ffn(0)
            ffn(1)
            project_in2()
            attention(2)
            attention(3)
            turn(2, (3,))
            turn(3)
            branch2()
            out_proj(1)
            ffn(2)

        @block.vector
        def _(v):
            V = nc.vector

            def split_lo(n0, step=0, i=0):
                n0 += 2
                if isinstance(i, int):
                    n0, step, i = n0 + step * i, 0, 0
                    if n0 >= NCH:
                        return
                v.wait_ge(sem("hi_ready"), n0 + 1 if step == 0 else step * i + (n0 + 1))
                V.tensor_tensor(LO[n0 % 3][:], RAW[n0 % 3][:], HI[n0 % 3][:].bitcast(F32), ALU.subtract)\
                    .then_inc(sem("lo_ready"), 1)

            def add_square_g(t, i=0):
                if isinstance(i, int):
                    t, i = t + 2 * i, 0
                v.wait_ge(sem("g_sum_added"), 2 * i + t + 1)
                v.wait_ge(sem("g_squared"), 2 * i + (t + 1))
                V.tensor_tensor(SUM_G, SUM_G, Y[:, t % 2, :], ALU.add).then_inc(sem("g_sum_added"), 1)

            def finish(t):
                v.wait_ge(sem("final_spread"), 1)
                V.scalar_tensor_tensor(out=X[:, t, :], in0=X[:, t, :], scalar=col("g_final", t),
                                       in1=PS[:, 7, :], op0=ALU.mult, op1=ALU.mult).then_inc(sem("finished"), 1)

            def clear_sum(k):
                if k == 5:
                    v.wait_ge(sem("final_spread"), 1)
                if k:
                    v.wait_ge(sem("sq_summed"), k)
                link(V.memset(RB[:, 0, :], 0.0))

            def add_square(k, t, i=0):
                if isinstance(i, int):
                    t, i = t + 2 * i, 0
                    if t:
                        v.wait_ge(sem("sum_added"), SAB[k] + t)
                else:
                    v.wait_ge(sem("sum_added"), 2 * i + (SAB[k] + t))
                v.wait_ge(sem("squared"), 2 * i + (NTB[k] + t + 1))
                V.tensor_tensor(RB[:, 0, :], RB[:, 0, :], SQ[:, t % 2, :], ALU.add).then_inc(sem("sum_added"), 1)

            def roots_of(k):
                if k == 4:
                    v.wait_ge(sem("sq_summed"), 5)
                    V.tensor_copy(FV[:, 4:8], S_X).then_inc(sem("fused_sums"), 1)
                    v.wait_ge(sem("fused_sums"), 1)
                    V.scalar_tensor_tensor(out=FV[:, 0:4], in0=FV[:, 4:8], scalar=EPS, in1=S_XG, op0=ALU.mult,
                                           op1=ALU.add).then_inc(sem("fused_sums"), 1)
                    v.wait_ge(sem("stds"), 5)
                    link(V.reciprocal(FR, FSTD))
                    v.wait_ge(sem("rstd"), 4)
                    for n, name in ((0, "expanded"), (4, "final_expanded")):
                        V.tensor_copy(RB[:, 0 if n else 1, :].rearrange("p (b n) -> p b n", b=NB),
                                      FR[:, n:n + 4].unsqueeze(2).to_broadcast([P, NB, P])).then_inc(sem(name), 1)
                    return
                v.wait_ge(sem("stds"), k + 1)
                link(V.reciprocal(NR, NSTD))
                if k:
                    v.wait_ge(sem("rstd"), k)
                V.tensor_copy(RB[:, 1, :].rearrange("p (b n) -> p b n", b=NB),
                              NR.unsqueeze(2).to_broadcast([P, NB, P])).then_inc(sem("expanded"), 1)

            def norm(k):
                nt, src, width, g, oh, ol = NORMS[k]
                roots_of(k)
                v.wait_ge(sem("rstd"), k + 1)
                for t in range(nt):
                    scaled(k, t)
                    if t >= 1:
                        lo(k, t - 1)
                lo(k, nt - 1)
                v.wait_ge(sem("split_lo"), SPLIT_TB[k + 1])

            def scaled(k, t):
                nt, src, width, g, oh, ol = NORMS[k]
                s = SPLIT_TB[k] + t - 1
                if s > 0:
                    v.wait_ge(sem("split_hi"), s)
                    v.wait_ge(sem("split_lo"), s)
                if isinstance(g, str):
                    scale = col(g, t)
                elif k == 4:
                    scale = G_BOTH[:, t:t + 1]
                else:
                    gain = (3 * g + 1) * DT + t
                    scale = MOD[:, gain:gain + 1]
                V.scalar_tensor_tensor(out=Y[:, t % 2, :], in0=src[:, t, :], scalar=scale, in1=PS[:, 6, :],
                                       op0=ALU.mult, op1=ALU.mult).then_inc(sem("normed"), 1)

            def lo(k, t):
                g, oh, ol = NORMS[k][3:]
                v.wait_ge(sem("split_hi"), SPLIT_TB[k] + t + 1)
                if not isinstance(g, str):
                    shift = 3 * g * DT + t
                    V.scalar_tensor_tensor(out=ol[:, t, :], in0=Y[:, t % 2, :], scalar=MOD[:, shift:shift + 1],
                                           in1=oh[:, t, :].bitcast(F32), op0=ALU.add, op1=ALU.subtract)\
                        .then_inc(sem("split_lo"), 1)
                    return
                V.tensor_tensor(ol[:, t, :], Y[:, t % 2, :], oh[:, t, :].bitcast(F32), ALU.subtract)\
                    .then_inc(sem("split_lo"), 1)

            steps = [0]

            def link(ins):
                steps[0] += 1
                ins.then_inc(sem("dve_link"), 1)
                v.wait_ge(sem("dve_link"), steps[0])

            two_pi = 2 * np.pi
            C1 = 6.28125
            C2 = float(np.round((two_pi - C1) * 2 ** 17) / 2 ** 17)
            C3 = float(np.float32(two_pi - C1 - C2))
            MAGIC = float(1.5 * 2 ** 23)

            def angles(k, pos, freq):
                if k % 2:
                    v.wait_ge(sem("table"), k)
                link(V.tensor_scalar(Y[:, 1, :], pos, col(freq), None, ALU.mult))
                link(V.tensor_scalar(RB[:, 1, :], Y[:, 1, :], 1.0 / two_pi, MAGIC, ALU.mult, ALU.add))
                link(V.tensor_scalar(RB[:, 1, :], RB[:, 1, :], -MAGIC, None, ALU.add))
                for c in (C1, C2, C3):
                    link(V.scalar_tensor_tensor(out=Y[:, 1, :], in0=RB[:, 1, :], scalar=-c, in1=Y[:, 1, :],
                                                op0=ALU.mult, op1=ALU.add))
                V.tensor_scalar(Y[:, 0, :], Y[:, 1, :], 3.1415925, -3.1415925, ALU.min, ALU.max)\
                    .then_inc(sem("angle"), 1)

            def ada_piece(a0, step=0, i=0):
                kt = a0 % 8
                j = a0 % 2
                if step:
                    v.wait_ge(sem(f"ada{j}"), (8 * step) * i + 16 * (a0 // 2 + 1))
                    v.wait_ge(sem("ada_added"), step * i + a0)
                    if kt == 0:
                        v.wait_ge(sem("ada_summed"), i + a0 // 8)
                else:
                    v.wait_ge(sem(f"ada{j}"), 16 * (a0 // 2 + 1))
                    if a0:
                        v.wait_ge(sem("ada_added"), a0)
                    if kt == 0 and a0:
                        v.wait_ge(sem("ada_summed"), a0 // 8)
                if kt == 0:
                    V.tensor_scalar(ACC[:], ADA[j][:], CND[:, 0:1], None, ALU.mult).then_inc(sem("ada_added"), 1)
                else:
                    V.scalar_tensor_tensor(out=ACC[:], in0=ADA[j][:], scalar=CND[:, kt:kt + 1], in1=ACC[:],
                                           op0=ALU.mult, op1=ALU.add).then_inc(sem("ada_added"), 1)

            def ada_take(g, loop=False, bank=7):
                if loop:
                    v.wait_ge(sem("ada_summed"), g + 1)
                    V.tensor_tensor(MOD[:, bass.ds(8 * g, 8)], PS[:, 7, 0:8],
                                    CO[:, bass.ds(8 * g + COLS["ada_b"][0], 8)], ALU.add).then_inc(sem("mod"), 1)
                else:
                    v.wait_ge(sem("ada_summed"), g + 1)
                    V.tensor_tensor(MOD[:, 8 * g:8 * g + 8], PS[:, bank, 0:8], col("ada_b", 8 * g, 8), ALU.add)\
                        .then_inc(sem("mod"), 1)

            def rope(q, bank, dst, tab, rows=slice(0, P), signal="rotated"):
                v.wait_ge(sem("rot_mm"), q + 1)
                ins = V.tensor_tensor(T[rows, 0, :], PS[rows, bank, :], tab[rows, 1, :], ALU.mult)
                ins.then_inc(sem("rot_read"), 1)
                link(V.tensor_tensor(T[rows, 1, :], dst[rows, :], tab[rows, 0, :], ALU.mult))
                return T

            def project_in1():
                n0 = FIRST["in1"]
                for j in range(len(IN1) + 2):
                    if j < len(IN1):
                        split_lo(n0 + j)
                    if j == 7:
                        v.wait_ge(sem("table"), 2)
                    if j - 2 in ROT1:
                        q = ROT1.index(j - 2)
                        dst = IN1[j - 2][1]
                        rope(q, 4 + q % 2, dst, IN1[j - 2][2])
                        v.wait_ge(sem("rot_read"), q + 1)
                        V.tensor_tensor(dst, T[:, 0, :], T[:, 1, :], ALU.add).then_inc(sem("rotated"), 1)
                        v.wait_ge(sem("rotated"), q + 1)
                    latents(j)

            def latents(j):
                if j == 1:
                    v.wait_ge(sem("pos_loaded"), 16)
                    link(V.tensor_copy(T[:, 0, :], T[:, 0, :].bitcast(I32)))
                    angles(0, T[:, 0, :], "freq_a")
                if j == 5:
                    angles(1, T[:, 0, :], "freq_p")
                if j == 4:
                    clear_sum(1)
                    add_square(1, 0)
                    add_square(1, 1)
                if j == 6:
                    roots_of(1)
                if j == 7:
                    clear_sum(2)
                    add_square(2, 0)
                if j == 10:
                    roots_of(2)
                for k, first, tiles in ((1, 8, 3), (2, 12, 2)):
                    if first <= j < first + tiles:
                        v.wait_ge(sem("rstd"), k + 1)
                        scaled(k, j - first)
                        lo(k, j - first)

            def head_norm(k):
                t, q = IN2[k], NRM2.index(k)
                roots = PS[:, 4, :]
                v.wait_ge(sem("hspread"), q + 1)
                v.wait_ge(sem("in_copied"), len(IN1) + k + 1)
                if t[0] in ("foxq", "foxk"):
                    dst = QF if t[0] == "foxq" else KF
                    g = FOXQ_G if t[0] == "foxq" else col("fox_g", 1)
                    for r in range(2):
                        rows = slice(64 * r, 64 * r + 64)
                        ins = V.scalar_tensor_tensor(
                            out=dst[0:64, 2 * t[1] + r, :], in0=R[rows, k % 4, :], scalar=g[rows, :],
                            in1=roots[rows, :], op0=ALU.mult, op1=ALU.mult)
                elif t[0] == "dsaq":
                    ins = V.scalar_tensor_tensor(out=t[1], in0=R[:, k % 4, :], scalar=DSAQ_G,
                                                 in1=roots, op0=ALU.mult, op1=ALU.mult)
                else:
                    ins = V.scalar_tensor_tensor(out=MISC[0:64, :], in0=MISC[0:64, :],
                                                 scalar=col("dsa_g", 1)[0:64, :], in1=roots[0:64, :],
                                                 op0=ALU.mult, op1=ALU.mult)
                ins.then_inc(sem("hnormed"), 1)

            def rotate_misc(q, bank):
                v.wait_ge(sem("rot_mm"), q + 1)
                lo_, hi_ = slice(0, 64), slice(64, 96)
                link(V.tensor_tensor(T[lo_, 0, :], PS[lo_, bank, :], TAB_A2[lo_, 1, :], ALU.mult))
                V.tensor_tensor(T[hi_, 0, :], PS[hi_, bank, :], TAB_I2[hi_, 1, :], ALU.mult)\
                    .then_inc(sem("rot_read"), 1)
                link(V.tensor_tensor(T[lo_, 1, :], MISC[lo_, :], TAB_A2[lo_, 0, :], ALU.mult))
                link(V.tensor_tensor(T[hi_, 1, :], MISC[hi_, :], TAB_I2[hi_, 0, :], ALU.mult))
                v.wait_ge(sem("rot_read"), q + 1)
                for r in range(2):
                    V.tensor_tensor(DK2[64 * r:64 * r + 64, :], T[lo_, 0, :], T[lo_, 1, :], ALU.add)\
                        .then_inc(sem("dk_spread"), 1)
                for r in range(4):
                    V.tensor_tensor(IK[32 * r:32 * r + 32, :], T[hi_, 0, :], T[hi_, 1, :], ALU.add)\
                        .then_inc(sem("ik_spread"), 1)
                V.tensor_scalar(FW[0:8, 0, :], MISC[96:104, :], col("f_bias")[96:104, :], None, ALU.add)\
                    .then_inc(sem("f_z"), 1)
                v.wait_ge(sem("dk_spread"), 2)
                v.wait_ge(sem("ik_spread"), 4)

            def index_sum(u):
                i, h = 1 + u // 8, u % 8
                n = P * (i + 1)
                v.wait_ge(sem("dots_read"), u + 1)
                if h == 0:
                    V.tensor_scalar(BIAS[i][:], Y[:, u % 2, 0:n], IW[:, i, 0:1], None, ALU.mult)\
                        .then_inc(sem("scored"), 1)
                else:
                    v.wait_ge(sem("scored"), u)
                    V.scalar_tensor_tensor(out=BIAS[i][:], in0=Y[:, u % 2, 0:n], scalar=IW[:, i, h:h + 1],
                                           in1=BIAS[i][:], op0=ALU.mult, op1=ALU.add).then_inc(sem("scored"), 1)

            def project_in2():
                for j in range(IN2_STEPS):
                    split_lo(FIRST["in2"] + j)
                    if j - 2 in NRM2:
                        q = NRM2.index(j - 2)
                        v.wait_ge(sem("hstd"), q + 1)
                        if q >= 2:
                            v.wait_ge(sem("hspread"), q - 1)
                        link(V.reciprocal(HR[q % 2], HSTD[q % 2]))
                        V.tensor_copy(RB[:, q % 2, :].rearrange("p (b n) -> p b n", b=2 * NB),
                                      HR[q % 2].unsqueeze(2).to_broadcast([P, 2 * NB, 64]))\
                            .then_inc(sem("hexpanded"), 1)
                    if j - 3 in NRM2:
                        head_norm(j - 3)
                    for r, k in enumerate(ROT2):
                        if rot_at(IN2, k) == j:
                            q = ROT_BASE["in2"] + r
                            if IN2[k][0] == "misc":
                                rotate_misc(q, 5)
                                continue
                            dst = IN2[k][1]
                            rope(q, 5, dst, IN2[k][2])
                            v.wait_ge(sem("rot_read"), q + 1)
                            V.tensor_tensor(dst, T[:, 0, :], T[:, 1, :], ALU.add).then_inc(sem("rotated"), 1)
                            v.wait_ge(sem("rotated"), len(ROT1) + r + (0 if r > ROT2.index(3) else 1))
                    if j == 7:
                        v.wait_ge(sem("values_copied"), 1)
                        link(V.tensor_scalar(IW[:], DVW[:, :, 64:72], 8 ** -0.5, None, ALU.mult))
                    if j >= DOTS_FROM:
                        for r in range(4):
                            index_sum(4 * (j - DOTS_FROM) + r)

            def branch2():
                for m in range(DT):
                    split_lo(FIRST["branch2"] + m)
                    v.wait_ge(sem("chunk_used"), FIRST["branch2"] + m + 1)
                    v.wait_ge(sem("gated"), 2 * m + 2)
                    for g in range(2):
                        V.tensor_tensor(T[:, g, :], GATE2[g][m], PS[:, BRANCH_BANKS[m % 2][g], :], ALU.mult)\
                            .then_inc(sem("branch_scaled" if g else "first_scaled"), 1)
                    v.wait_ge(sem("branch_scaled"), DT + m + 1)
                    v.wait_ge(sem("first_scaled"), DT + m + 1)
                    V.tensor_tensor(Y[:, m % 2, :], T[:, 0, :], T[:, 1, :], ALU.add).then_inc(sem("merged"), 1)
                    v.wait_ge(sem("merged_hi"), DT + m + 1)
                    V.tensor_tensor(ML2[:, m, :], Y[:, m % 2, :], MH2[:, m, :].bitcast(F32), ALU.subtract)\
                        .then_inc(sem("merged_lo"), 1)

            def round_of_selection(q):
                i = 1 + q // 16
                link(V.max(M8, BIAS[i][:]))
                link(V.match_replace(BIAS[i][:], M8, BIAS[i][:], TAKEN))
                if q % 16 == 15:
                    V.tensor_scalar(MASK[i][:], BIAS[i][:], -2.0e38, NEG, ALU.is_gt, ALU.mult)\
                        .then_inc(sem("selected"), 1)

            def diff_attention():
                for s in range(NPAIR + 4):
                    if s >= 4:
                        w = s - 4
                        p, i = divmod(w, NB)
                        v.wait_ge(sem("pv"), w + 1)
                        V.tensor_scalar(OD[:, i, p * P:(p + 1) * P], PS[:, 5 + w % 2, 0:P],
                                        PAIR_INV[w % 8][:, 0:1], None, ALU.mult).then_inc(sem("onorm"), 1)
                    if s < NPAIR:
                        n = P * (s % NB + 1)
                        if s >= 2:
                            v.wait_ge(sem("probs"), 2 * s - 2)
                        for r in range(2):
                            c = 2 * (s % 2) + r
                            v.wait_ge(sem("scores"), 2 * s + r + 1)
                            V.tensor_reduce(NMX[:, c:c + 1], PS[:, SCORE_BANKS[s % 2][r], 0:n], AX, ALU.max,
                                            negate=True).then_inc(sem("smax"), 1)
                    if 1 <= s < NPAIR + 1:
                        w = s - 1
                        n = P * (w % NB + 1)
                        c = 2 * (w % 2)
                        v.wait_ge(sem("probs"), 2 * w + 2)
                        if w >= 8:
                            v.wait_ge(sem("onorm"), w - 7)
                        link(V.reciprocal(PAIR_INV[w % 8], RSU[:, c:c + 2]))
                        link(V.scalar_tensor_tensor(out=FACTOR[w % 2], in0=PAIR_INV[w % 8][:, 1:2],
                                                    scalar=LAM[:, 4:5], in1=RSU[:, c:c + 1], op0=ALU.mult,
                                                    op1=ALU.mult))
                        V.scalar_tensor_tensor(out=P1[w % 3][:, 0:n], in0=P1B[w % 3][:, 0:n], scalar=FACTOR[w % 2],
                                               in1=P1[w % 3][:, 0:n], op0=ALU.mult, op1=ALU.add)\
                            .then_inc(sem("combined"), 1)

            def attention(a):
                at_ = ATT[a]
                for u in range(NU + 3):
                    if a >= 2 and u % 4 == 1 and u < NU:
                        split_lo(FIRST["gates2"] + DT * (a - 2) + u // 4)
                    if u < NU:
                        n = P * (u % NB + 1)
                        v.wait_ge(sem("scores"), NU * a + u + 1)
                        if u >= 4:
                            v.wait_ge(sem("probs"), NU * a + u - 3)
                        V.tensor_reduce(NMX[:, u % 4:u % 4 + 1], PS[:, u % 3, 0:n], AX, ALU.max, negate=True)\
                            .then_inc(sem("smax"), 1)
                    if a == 2 and 2 <= u < NU + 2:
                        w = u - 2
                        v.wait_ge(sem("probs"), NU * a + w + 1)
                        if w >= 4:
                            v.wait_ge(sem("onorm"), AFTER[a] + w - 3)
                        V.reciprocal(RIN[:, w % 4:w % 4 + 1], RSU[:, w % 4:w % 4 + 1]).then_inc(sem("sum_inverse"), 1)
                    if a == 3 and u >= NU:
                        turn(2, (u - NU,))
                    if a == 2 and u < NU:
                        for q in range(u * 48 // NU, (u + 1) * 48 // NU):
                            round_of_selection(q)
                    if u >= 3 and a != 2:
                        w = u - 3
                        h, i = divmod(w, NB)
                        r = RIN[:, w % 4:w % 4 + 1]
                        v.wait_ge(sem("probs"), NU * a + w + 1)
                        link(V.reciprocal(r, RSU[:, w % 4:w % 4 + 1]))
                        v.wait_ge(sem("pv"), AFTER[a] + w + 1)
                        o = PS[:, 5 + w % 2, 0:at_["dv"]]
                        dst = (None, OM, OF, OS)[a]
                        V.tensor_scalar(dst[:, i, h * 64:h * 64 + 64], o, r, None, ALU.mult)\
                            .then_inc(sem("onorm"), 1)

            def turn(a, tiles=range(4)):
                src, oh, ol, f0, g = OUT_T[a]
                for f in tiles:
                    k = 4 * g + f
                    v.wait_ge(sem("turned_hi"), k + 1)
                    if a == 0:
                        ins = V.scalar_tensor_tensor(out=ol[:, f0 + f, :], in0=PS[:, TURN_BANKS[k], :], scalar=GM[:, 0:1],
                                                     in1=oh[:, f0 + f, :].bitcast(F32), op0=ALU.mult,
                                                     op1=ALU.subtract)
                    else:
                        ins = V.tensor_tensor(ol[:, f0 + f, :], PS[:, TURN_BANKS[k], :],
                                              oh[:, f0 + f, :].bitcast(F32), ALU.subtract)
                    ins.then_inc(sem("turned_lo"), 1)

            def merge(b):
                n0 = FIRST[f"merge{b + 1}"]
                mh, ml = ((MH1, ML1), (MH2, ML2))[b]

                def pair(i):
                    for j in range(2):
                        for g in range(2):
                            split_lo(n0 + 3 * j + g, 6, i)
                        if isinstance(i, int) and j == 0:
                            diff_norm()
                            turn(1)
                        split_lo(n0 + 3 * j + 2, 6, i)
                        if isinstance(i, int) and j == 0:
                            turn(0)
                        merge_piece(i, j)
                        v.wait_ge(sem("chunk_used"), 6 * i + (n0 + 3 * j + 3))
                        v.wait_ge(sem("gate"), 4 * i + (16 * b + 2 * j + 2))
                        for g in range(2):
                            V.tensor_tensor(T[:, g, :], T[:, g, :], PS[:, 4 * j + 2 + g, :], ALU.mult)\
                                .then_inc(sem("branch_scaled" if g else "first_scaled"), 1)
                        v.wait_ge(sem("branch_scaled"), 2 * i + (DT * b + j + 1))
                        if not (isinstance(i, int) and 2 * i + DT * b == 0):
                            v.wait_ge(sem("merged_lo"), 2 * i + (DT * b + j - 1))
                        V.tensor_tensor(Y[:, j, :], T[:, 0, :], T[:, 1, :], ALU.add).then_inc(sem("merged"), 1)
                        v.wait_ge(sem("merged_hi"), 2 * i + (8 * b + j + 1))
                        V.tensor_tensor(ml[:, bass.ds(2 * i + j, 1), :], Y[:, j:j + 1, :],
                                        mh[:, bass.ds(2 * i + j, 1), :].bitcast(F32), ALU.subtract)\
                            .then_inc(sem("merged_lo"), 1)

                pair(0)
                with v.Fori(1, 4) as i:
                    pair(i)

            def diff_norm():
                v.wait_ge(sem("diff_std"), 1)
                link(V.reciprocal(RSD, RSD))
                for f in range(4):
                    for i in range(NB):
                        o = OD[:, i, f * P:(f + 1) * P]
                        ins = V.tensor_scalar(o, o, RSD[:, 4 * i + f:4 * i + f + 1], None, ALU.mult)
                    ins.then_inc(sem("diff_normed"), 1)

            def merge_piece(i, j):
                kt = 2 * i + j
                if isinstance(i, int):
                    ada_piece(kt)
                    return
                v.wait_ge(sem(f"ada{j}"), 16 * i + 16)
                v.wait_ge(sem("ada_added"), kt)
                V.scalar_tensor_tensor(out=ACC[:], in0=ADA[j][:], scalar=CND[:, bass.ds(kt, 1)], in1=ACC[:],
                                       op0=ALU.mult, op1=ALU.add).then_inc(sem("ada_added"), 1)

            def out_proj(b):
                n0 = FIRST[f"out{b + 1}"]
                k = (3, 6)[b]
                clear_sum(k)
                for m in range(DT):
                    split_lo(n0 + m)
                    if b == 0:
                        if m == 2:
                            ada_take(0, bank=5)
                        for r in ((), (), (0,), (1, 2), (3, 4), (5, 6), (7,), ())[m]:
                            ada_piece(8 + r)
                    v.wait_ge(sem("chunk_used"), n0 + m + 1)
                    if b == 0:
                        V.tensor_tensor(X[:, m, :], X[:, m, :], PS[:, m % 4, :], ALU.add)\
                            .then_inc(sem("x_added"), 1)
                    else:
                        c = 5 * DT + m
                        V.scalar_tensor_tensor(out=X[:, m, :], in0=PS[:, m % 4, :], scalar=MOD[:, c:c + 1],
                                               in1=X[:, m, :], op0=ALU.mult, op1=ALU.add)\
                            .then_inc(sem("x_added"), 1)
                    if m:
                        add_square(k, m - 1)
                norm(k)
                if b == 0:
                    ada_take(1)

            def ffn(f):
                n0 = FIRST[f"up{f + 1}"]

                def three(i, tiles=3):
                    for j in range(tiles):
                        earlier = not (isinstance(i, int) and i == 0 and j == 0)
                        if earlier:
                            multiply(i, j - 1)
                        if f == 0 and j == 0 and not (isinstance(i, int) and i == 0):
                            ada_take(i + 1, loop=True)
                        split_lo(n0 + 2 * j, 6, i)
                        if f == 0 and tiles == 3:
                            ada_piece(16 + 3 * j, 8, i)
                        if earlier:
                            low(3 * i + (j - 1))
                        if f == 0 and tiles == 3:
                            ada_piece(17 + 3 * j, 8, i)
                        split_lo(n0 + 2 * j + 1, 6, i)
                        if f == 1 and isinstance(i, int) and i == 0:
                            for t in range(3 * j, min(3 * j + 3, DT)):
                                finish(t)
                        if f == 0 and tiles == 3 and j < 2:
                            ada_piece(18 + 3 * j, 8, i)

                def multiply(i, j):
                    v.wait_ge(sem("chunk_used"), 6 * i + (n0 + 2 * j + 2))
                    v.wait_ge(sem("silu"), 3 * i + (FT * f + j + 1))
                    if not (isinstance(i, int) and FT * f + 3 * i + j == 0):
                        v.wait_ge(sem("hid_lo"), 3 * i + (FT * f + j))
                    V.tensor_tensor(Y[:, 0, :], SILU[j % 3], PS[:, 2 * (j % 3) + 1, :], ALU.mult)\
                        .then_inc(sem("hid"), 1)

                def low(t):
                    v.wait_ge(sem("hid_hi"), t + (FT * f + 1))
                    V.tensor_tensor(HIDL[:, bass.ds(t, 1), :], Y[:, 0:1, :], HIDH[:, bass.ds(t, 1), :].bitcast(F32),
                                    ALU.subtract).then_inc(sem("hid_lo"), 1)

                three(0)
                with v.Fori(1, 7) as i:
                    three(i)
                three(7, tiles=1)
                multiply(7, 0)
                low(FT - 1)
                n0 = FIRST[f"down{f + 1}"]
                if f == 0:
                    modulation()
                if f == 1:
                    v.wait_ge(sem("pos_loaded"), 32)
                    link(V.tensor_copy(POS2[:], POS2[:].bitcast(I32)))
                    v.wait_ge(sem("hid_lo"), 2 * FT)
                    angles(2, POS2[:], "freq_a")
                if f < 2:
                    clear_sum(4 + f)
                if f == 0:
                    v.wait_ge(sem("hid_lo"), FT)
                    V.memset(SUM_G, 0.0).then_inc(sem("g_sum_added"), 1)

                def two(i):
                    for j in range(2):
                        for g in range(3):
                            split_lo(n0 + 3 * j + g, 6, i)
                        v.wait_ge(sem("chunk_used"), 6 * i + (n0 + 3 * j + 3))
                        bank = PS[:, 2 + j:3 + j, :]
                        xt = X[:, bass.ds(2 * i + j, 1), :]
                        gate = (0, 2, 8)[f] * DT
                        if f == 0:
                            V.tensor_tensor(xt, xt, bank, ALU.add).then_inc(sem("x_added"), 1)
                        else:
                            V.scalar_tensor_tensor(out=xt, in0=bank,
                                                   scalar=MOD[:, bass.ds(2 * i + (gate + j), 1)], in1=xt,
                                                   op0=ALU.mult, op1=ALU.add).then_inc(sem("x_added"), 1)
                        if f < 2 and not (isinstance(i, int) and i == 0 and j == 0):
                            add_square(4 + f, j - 1, i)
                            if f == 0:
                                add_square_g(j - 1, i)

                two(0)
                if f == 1:
                    angles(3, POS2[:], "freq_i")
                with v.Fori(1, 3) as i:
                    two(i)
                two(3)
                if f < 2:
                    norm(4 + f)

            def modulation():
                v.wait_ge(sem("mod"), 9)
                for s in range(3):
                    c = MOD[:, (3 * s + 1) * DT:(3 * s + 2) * DT]
                    link(V.tensor_scalar(c, c, 1.0, None, ALU.add))
                    link(V.tensor_tensor(c, c, col("g2", s * DT, DT), ALU.mult))
                link(V.tensor_tensor(G_BOTH, MOD[:, DT:2 * DT], col("g_final", 0, DT), ALU.mult))
                for s in (0, 2):
                    c = MOD[:, (3 * s + 2) * DT:(3 * s + 3) * DT]
                    link(V.tensor_scalar(c, c, 0.5, None, ALU.mult))

            link(V.memset(PIH, float(np.pi / 2)))
            link(V.memset(EPS2C, EPS * EPS))
            V.memset(EPSC, EPS).then_inc(sem("eps_set"), 1)
            clear_sum(0)
            for t in range(DT - 1):
                add_square(0, t)
            split_lo(-2)
            split_lo(-1)
            norm(0)
            v.wait_ge(sem("lams_loaded"), 16)
            for j in range(2):
                link(V.tensor_tensor(LAMS[:, 256 + 64 * j:320 + 64 * j], LAMS[:, 128 * j:128 * j + 64],
                                     LAMS[:, 128 * j + 64:128 * j + 128], ALU.mult))
                V.tensor_reduce(LAM[:, j:j + 1], LAMS[:, 256 + 64 * j:320 + 64 * j], AX, ALU.add)\
                    .then_inc(sem("lams_used"), 1)
            v.wait_ge(sem("squares_loaded"), 16)
            link(V.tensor_copy(IDENT_B[:], SQV["ident"]))
            link(V.tensor_copy(CAUSAL_B[:], SQV["causal"]))
            v.wait_ge(sem("cond_ready"), 1)
            project_in1()
            for j in range(4):
                split_lo(FIRST["dv1"] + j)
            v.wait_ge(sem("lam_exp"), 1)
            link(V.tensor_tensor(LAM[:, 4:5], LAM[:, 3:4], LAM[:, 2:3], ALU.subtract))
            link(V.tensor_scalar(LAM[:, 4:5], LAM[:, 4:5], -(0.8 - 0.6), None, ALU.add))
            diff_attention()
            V.tensor_scalar(GM[:, 0:1], col("g_sub"), 1.0 - (0.8 - 0.6), None, ALU.mult)\
                .then_inc(sem("g_sub_scaled"), 1)
            for j in range(4):
                split_lo(FIRST["uq"] + j)
            for r in range(2):
                q = ROT_BASE["uq"] + r
                rope(q, 6 + r, Y[:, r, :], TAB_P1)
                v.wait_ge(sem("rot_read"), q + 1)
                for h in range(4):
                    rows = slice(32 * h, 32 * h + 32)
                    ins = V.tensor_tensor(QM[64:96, 4 * r + h, :], T[rows, 0, :], T[rows, 1, :], ALU.add)
                ins.then_inc(sem("q_rotated"), 1)
                v.wait_ge(sem("q_rotated"), r + 1)
            split_lo(FIRST["uv"])
            attention(1)
            v.wait_ge(sem("g_sub_scaled"), 1)
            merge(0)
            out_proj(0)
            ffn(0)
            ffn(1)
            link(V.tensor_scalar(FOXQ_G, col("fox_g", 0), 0.125, None, ALU.mult))
            link(V.tensor_scalar(DSAQ_G, col("dsa_g", 0), 0.125, None, ALU.mult))
            project_in2()
            V.tensor_copy(MASK[0][:], SQV["chunked"]).then_inc(sem("selected"), 1)
            v.wait_ge(sem("scored"), NDOTS)
            for i in range(1, NB):
                d = BIAS[i][:, i * P:(i + 1) * P]
                link(V.tensor_tensor(d, d, SQV["chunked"], ALU.add))
            attention(2)
            attention(3)
            turn(2, (3,))
            turn(3)
            branch2()
            out_proj(1)
            ffn(2)


def rot_at(tiles, k):
    return k + (5 if tiles[k][0] in ("dsaq", "misc") else 2)


def _tile(w):
    k, m = w.shape
    a = w.reshape(k // P, P, m).transpose(1, 0, 2).reshape(P, k // P * m)
    if a.shape[1] < 1024:
        a = np.concatenate([a, np.zeros((P, 1024 - a.shape[1]), w.dtype)], axis=1)
    return a


def _pad(w, n):
    return np.concatenate([w, np.zeros((w.shape[0], n - w.shape[1]), w.dtype)], axis=1)


def _ffn(gate, up, down):
    chunks = []
    for t in range(FT):
        chunks += [_tile(gate[:, t * P:(t + 1) * P]), _tile(up[:, t * P:(t + 1) * P])]
    for m in range(DT):
        w = down[:, m * P:(m + 1) * P]
        chunks += [_tile(w[0:1024]), _tile(w[1024:2048]), _tile(w[2048:FF])]
    return chunks


def _merge(gates, a, b):
    chunks = []
    for m in range(DT):
        c = slice(m * P, (m + 1) * P)
        chunks += [_tile(gates[:, :D][:, c]), _tile(gates[:, D:][:, c]), _tile(np.concatenate([a[:, c], b[:, c]]))]
    return chunks


def _tiles(w):
    return [_tile(w[:, m * P:(m + 1) * P]) for m in range(w.shape[1] // P)]


def _weights(a):
    w1, w2 = a["w_in"][0], a["w_in_2"][0]
    lat = QR + KVR
    o = lat + ROPE
    chunks = _tiles(w1[:, :lat]) + [_tile(_pad(w1[:, lat:o], P))] + _tiles(w1[:, o:o + 1024])
    chunks += [_tile(w1[256 * j:256 * j + 256, o + 1024:o + 1536]) for j in range(4)]
    uq = a["mla_w_uq"][0].reshape(QR, H1, NOPE + ROPE)
    uq = np.concatenate([uq[:, :, :NOPE].reshape(QR, 512), uq[:, :, NOPE:].reshape(QR, 256)], axis=1)
    for j in range(3):
        chunks.append(_pad(np.concatenate([_tile(uq[:, (2 * j + r) * P:(2 * j + r + 1) * P])[:, :384]
                                           for r in range(2)], axis=1), 1024))
    ukv = a["mla_w_ukv"][0].reshape(KVR, H1, NOPE + VDIM)
    uk, uv = ukv[:, :, :NOPE].reshape(KVR, 512), ukv[:, :, NOPE:].reshape(KVR, 512)
    chunks.append(np.concatenate([_tile(uk[:, m * P:(m + 1) * P])[:, :256] for m in range(4)], axis=1))
    chunks.append(_tile(uv))
    chunks += _merge(w1[:, o + 1536:], a["w_branch_mla"][0], a["w_branch_diff"][0])
    chunks += _tiles(a["w_out"][0])
    chunks += _ffn(a["w_ffn_gate"][0], a["w_ffn_up"][0], a["w_ffn_down"][0])
    chunks += _ffn(a["ffn1_w1_2"][0], a["ffn1_w3_2"][0], a["ffn1_w2_2"][0])
    fq, fk, fv, ff, dq, dk, dv, iq, ik, iw, gates = np.split(
        w2, np.cumsum([512, 512, 512, 8, 512, 64, 64, 256, 32, 8]).tolist(), axis=1)
    chunks += _tiles(iq)
    chunks.append(_tile(_pad(np.concatenate([dv, iw], axis=1), P)))
    chunks.append(_tile(_pad(np.concatenate([dk, ik, ff], axis=1), P)))
    chunks += _tiles(dq) + _tiles(fq) + _tiles(fk)
    chunks += [_tile(fv[256 * j:256 * j + 256]) for j in range(4)]
    merge = _merge(gates, a["w_br_fox_2"][0], a["w_br_dsa_2"][0])
    chunks += merge[0::3] + merge[1::3] + merge[2::3]
    chunks += _tiles(a["w_out_2"][0])
    chunks += _ffn(a["ffn2_w1_2"][0], a["ffn2_w3_2"][0], a["ffn2_w2_2"][0])
    return np.stack(chunks)


def _freq(rot, period):
    half = rot // 2
    f = (THETA ** (-np.arange(half) * 2.0 / rot)).astype(np.float32)
    col = np.zeros(P, np.float32)
    for p in range(P):
        if p % period < rot:
            col[p] = f[p % period % half]
    return col


def _columns(a):
    c = np.zeros((P, NCOLS), np.float32)

    def put(name, v, k=0):
        v = np.asarray(v).reshape(-1, P).T
        c[:, COLS[name][0] + k:COLS[name][0] + k + v.shape[1]] = v

    put("g_mix", a["norm_mix_g"])
    put("g_q", a["mla_q_norm_g"])
    put("g_kv", a["mla_kv_norm_g"])
    put("g_sub", a["diff_subln_g"])
    put("g_ffn", a["norm_ffn_g"])
    put("g_final", a["norm_final_g"])
    put("b_gate", a["b_gate"])
    put("g2", a["norm_g_2"])
    put("ada_b", a["ada_b_2"])
    put("cond", a["c_2"])
    for n, src in (("fox_g", a["fox_qk_g_2"][0]), ("dsa_g", a["dsa_qk_g_2"][0])):
        for k in range(2):
            put(n, np.concatenate([src[k], src[k]]), k)
    c[96:104, COLS["f_bias"][0]] = a["fox_f_bias_2"][0]
    put("freq_a", _freq(16, 64))
    put("freq_p", _freq(32, 32))
    put("freq_i", _freq(8, 32))
    return c


def _squares():
    q = np.zeros((P, NSQ, P), np.float32)
    n = {name: k for k, name in enumerate(SQUARES)}
    q[:, n["ident"], :] = np.eye(P)
    q[:, n["ones"], :] = 1.0
    q[:64, n["halves"], :64] = q[64:, n["halves"], 64:] = 1.0
    for name, spans in (("rot_a", [(0, 8), (64, 8)]), ("rot_p", [(32 * b, 16) for b in range(4)]),
                        ("rot_i", [(32 * b, 4) for b in range(4)]), ("rot_m", [(0, 8), (64, 4)])):
        for first, half in spans:
            for r in range(first, first + half):
                q[r + half, n[name], r] = -1.0
                q[r, n[name], r + half] = 1.0
    q[:, n["causal"], :] = np.triu(np.full((P, P), NEG, np.float32), 1)
    q[:CHUNK, n["chunked"], CHUNK:] = NEG
    return q


def kernel(**inputs):
    import concourse.bacc as bacc
    from concourse.bass_utils import run_bass_kernel_spmd

    a = {k: np.asarray(v) for k, v in inputs.items()}
    arrays = {
        "weights": _weights(a),
        "ada": np.ascontiguousarray(a["ada_w_2"][0].reshape(DT, P, 9, D).transpose(2, 0, 1, 3).reshape(72, P, D)),
        "x_in": np.ascontiguousarray(a["x"][0].T.reshape(DT, P, S).transpose(1, 0, 2)),
        "columns": _columns(a),
        "squares": _squares(),
        "positions1": a["positions"].reshape(S),
        "positions2": a["positions_2"].reshape(S),
        "lambdas": np.concatenate([a[f"diff_lambda_{n}"].reshape(-1) for n in ("q1", "k1", "q2", "k2")]),
    }
    nc = bacc.Bacc("TRN2", target_bir_lowering=False, num_devices=1)
    args = [nc.dram_tensor(n, v.shape, mybir.dt.from_np(v.dtype), kind="ExternalInput").ap()
            for n, v in arrays.items()]
    out = nc.dram_tensor("y_out", (P, DT, S), F32, kind="ExternalOutput").ap()
    build(nc, *args, out)
    got = run_bass_kernel_spmd(nc, [arrays], core_ids=[0]).results[0]["y_out"]
    return np.ascontiguousarray(got.transpose(1, 0, 2).reshape(D, S).T)[None]
```
